# Optimizing a Trainium2 kernel written in Bass

```python
import jax, jax.numpy as jnp
from jax import lax
import numpy as np

D_MODEL = 2048
BATCH = 1
SEQ = 256
DEPTH = 1

MLA_HEADS = 8
MLA_Q_RANK = 512
MLA_KV_RANK = 512
MLA_NOPE_DIM = 128
MLA_ROPE_DIM = 64
MLA_V_DIM = 128
FOX_HEADS = 8
FOX_HEAD_DIM = 128
D_FF = 5632
CONV_WIDTH = 3
Q_BLOCK = 128
ROPE_THETA = 10000.0
NORM_EPS = 1e-6

IN_SPLITS = (
    MLA_Q_RANK,
    MLA_KV_RANK,
    MLA_ROPE_DIM,
    FOX_HEADS * FOX_HEAD_DIM,
    FOX_HEADS * FOX_HEAD_DIM,
    FOX_HEADS * FOX_HEAD_DIM,
    FOX_HEADS,
    D_MODEL,
    D_MODEL,
)
D_IN = int(sum(IN_SPLITS))
SPLIT_IDX = [int(v) for v in np.cumsum(IN_SPLITS)[:-1]]

kernel_name = "hybrid_mla_fox_convffn_gated_merge"

def _rmsnorm(x, g):
    xf = x.astype(jnp.float32)
    y = xf * lax.rsqrt(jnp.mean(xf * xf, axis=-1, keepdims=True) + NORM_EPS)
    return (y * g.astype(jnp.float32)).astype(x.dtype)

def _rope_tables(positions):
    inv_freq = ROPE_THETA ** (-jnp.arange(0, MLA_ROPE_DIM, 2, dtype=jnp.float32) / MLA_ROPE_DIM)
    ang = positions.astype(jnp.float32)[..., None] * inv_freq
    return jnp.cos(ang), jnp.sin(ang)

def _rope(x, cos, sin):
    xf = x.astype(jnp.float32)
    x1, x2 = jnp.split(xf, 2, axis=-1)
    out = jnp.concatenate([x1 * cos - x2 * sin, x2 * cos + x1 * sin], axis=-1)
    return out.astype(x.dtype)

def _sweep_query_blocks(logits_fn, v):
    B, H, S, Dv = v.shape
    n_blocks = S // Q_BLOCK
    key_pos = jnp.arange(S)

    def one_block(i):
        start = i * Q_BLOCK
        logits = logits_fn(start)
        q_pos = start + jnp.arange(Q_BLOCK)
        causal = key_pos[None, :] <= q_pos[:, None]
        logits = jnp.where(causal, logits, -jnp.inf)
        p = jax.nn.softmax(logits, axis=-1)
        return jnp.einsum('bhqk,bhkd->bhqd', p.astype(v.dtype), v)

    out = lax.map(one_block, jnp.arange(n_blocks))
    return out.transpose(1, 2, 0, 3, 4).reshape(B, H, S, Dv)

def _hybrid_mixer(xn, positions, w_in, b_forget, norm_q_a, w_uq, norm_kv_a, w_ukv,
                  w_proj_mla, w_proj_fox, w_out):
    B, S, _ = xn.shape
    proj = xn @ w_in
    c_q, c_kv, k_rope, fq, fk, fv, f_logit, g_mla, g_fox = jnp.split(proj, SPLIT_IDX, axis=-1)

    q = (_rmsnorm(c_q, norm_q_a) @ w_uq).reshape(B, S, MLA_HEADS, MLA_NOPE_DIM + MLA_ROPE_DIM)
    q = q.transpose(0, 2, 1, 3)
    q_nope, q_rope = q[..., :MLA_NOPE_DIM], q[..., MLA_NOPE_DIM:]
    kv = (_rmsnorm(c_kv, norm_kv_a) @ w_ukv).reshape(B, S, MLA_HEADS, MLA_NOPE_DIM + MLA_V_DIM)
    kv = kv.transpose(0, 2, 1, 3)
    k_nope, v_mla = kv[..., :MLA_NOPE_DIM], kv[..., MLA_NOPE_DIM:]
    cos, sin = _rope_tables(positions)
    q_rope = _rope(q_rope, cos[:, None], sin[:, None])
    k_rope = _rope(k_rope, cos, sin)
    mla_scale = (MLA_NOPE_DIM + MLA_ROPE_DIM) ** -0.5

    def mla_logits(start):
        qn = lax.dynamic_slice_in_dim(q_nope, start, Q_BLOCK, axis=2)
        qr = lax.dynamic_slice_in_dim(q_rope, start, Q_BLOCK, axis=2)
        s = (jnp.einsum('bhqd,bhkd->bhqk', qn, k_nope)
             + jnp.einsum('bhqr,bkr->bhqk', qr, k_rope))
        return s.astype(jnp.float32) * mla_scale

    o_mla = _sweep_query_blocks(mla_logits, v_mla)
    o_mla = o_mla.transpose(0, 2, 1, 3).reshape(B, S, MLA_HEADS * MLA_V_DIM)

    def heads(t):
        return t.reshape(B, S, FOX_HEADS, FOX_HEAD_DIM).transpose(0, 2, 1, 3)
    fq, fk, fv = heads(fq), heads(fk), heads(fv)
    log_f = jax.nn.log_sigmoid((f_logit + b_forget).astype(jnp.float32))
    cum = jnp.cumsum(log_f, axis=1).transpose(0, 2, 1)
    fox_scale = FOX_HEAD_DIM ** -0.5

    def fox_logits(start):
        qb = lax.dynamic_slice_in_dim(fq, start, Q_BLOCK, axis=2)
        cq = lax.dynamic_slice_in_dim(cum, start, Q_BLOCK, axis=2)
        s = jnp.einsum('bhqd,bhkd->bhqk', qb, fk).astype(jnp.float32) * fox_scale
        return s + cq[..., :, None] - cum[..., None, :]

    o_fox = _sweep_query_blocks(fox_logits, fv)
    o_fox = o_fox.transpose(0, 2, 1, 3).reshape(B, S, FOX_HEADS * FOX_HEAD_DIM)

    merged = (jax.nn.sigmoid(g_mla) * (o_mla @ w_proj_mla)
              + jax.nn.sigmoid(g_fox) * (o_fox @ w_proj_fox))
    return merged @ w_out

def _causal_dwconv(h, w_conv, b_conv):
    C = h.shape[-1]
    out = lax.conv_general_dilated(
        h, w_conv[:, None, :], window_strides=(1,), padding=((CONV_WIDTH - 1, 0),),
        dimension_numbers=('NWC', 'WIO', 'NWC'), feature_group_count=C)
    return out + b_conv

def _conv_ffn(xn, w_ffn_in, w_conv, b_conv, w_ffn_out):
    h = xn @ w_ffn_in
    h = _causal_dwconv(h, w_conv, b_conv)
    gate, up = jnp.split(h, 2, axis=-1)
    return (jax.nn.silu(gate) * up) @ w_ffn_out

def setup_inputs(seed: int = 0) -> dict:
    key = jax.random.key(seed)
    ks = jax.random.split(key, 20)

    def dense(k, shape, fan_in):
        return jax.random.normal(k, shape, jnp.float32) * fan_in ** -0.5

    def gain(k, n):
        return 1.0 + 0.02 * jax.random.normal(k, (DEPTH, n), jnp.float32)

    x = jax.random.normal(ks[0], (BATCH, SEQ, D_MODEL), jnp.float32)
    offset = jax.random.randint(ks[1], (BATCH, 1), 0, 4096)
    positions = (offset + jnp.arange(SEQ)[None, :]).astype(jnp.int32)
    return {
        "x": x,
        "positions": positions,
        "norm_mix": gain(ks[2], D_MODEL),
        "w_in": dense(ks[3], (DEPTH, D_MODEL, D_IN), D_MODEL),
        "b_forget": 3.0 + 0.5 * jax.random.normal(ks[4], (DEPTH, FOX_HEADS), jnp.float32),
        "norm_q_a": gain(ks[5], MLA_Q_RANK),
        "w_uq": dense(ks[6], (DEPTH, MLA_Q_RANK, MLA_HEADS * (MLA_NOPE_DIM + MLA_ROPE_DIM)), MLA_Q_RANK),
        "norm_kv_a": gain(ks[7], MLA_KV_RANK),
        "w_ukv": dense(ks[8], (DEPTH, MLA_KV_RANK, MLA_HEADS * (MLA_NOPE_DIM + MLA_V_DIM)), MLA_KV_RANK),
        "w_proj_mla": dense(ks[9], (DEPTH, MLA_HEADS * MLA_V_DIM, D_MODEL), MLA_HEADS * MLA_V_DIM),
        "w_proj_fox": dense(ks[10], (DEPTH, FOX_HEADS * FOX_HEAD_DIM, D_MODEL), FOX_HEADS * FOX_HEAD_DIM),
        "w_out": dense(ks[11], (DEPTH, D_MODEL, D_MODEL), D_MODEL),
        "norm_ffn": gain(ks[12], D_MODEL),
        "w_ffn_in": dense(ks[13], (DEPTH, D_MODEL, 2 * D_FF), D_MODEL),
        "w_conv": dense(ks[14], (DEPTH, CONV_WIDTH, 2 * D_FF), CONV_WIDTH),
        "b_conv": 0.02 * jax.random.normal(ks[15], (DEPTH, 2 * D_FF), jnp.float32),
        "w_ffn_out": dense(ks[16], (DEPTH, D_FF, D_MODEL), D_FF),
        "norm_final": 1.0 + 0.02 * jax.random.normal(ks[17], (D_MODEL,), jnp.float32),
    }

def reference(x, positions, norm_mix, w_in, b_forget, norm_q_a, w_uq, norm_kv_a, w_ukv,
              w_proj_mla, w_proj_fox, w_out, norm_ffn, w_ffn_in, w_conv, b_conv, w_ffn_out,
              norm_final):
    h = x
    for l in range(DEPTH):
        xn = _rmsnorm(h, norm_mix[l])
        h = h + _hybrid_mixer(xn, positions, w_in[l], b_forget[l], norm_q_a[l], w_uq[l],
                              norm_kv_a[l], w_ukv[l], w_proj_mla[l], w_proj_fox[l], w_out[l])
        xn = _rmsnorm(h, norm_ffn[l])
        h = h + _conv_ffn(xn, w_ffn_in[l], w_conv[l], b_conv[l], w_ffn_out[l])
    return _rmsnorm(h, norm_final)


_drawn_inputs = setup_inputs


def setup_inputs(seed=0):
    import zlib

    import numpy as np

    out = dict(_drawn_inputs(seed))
    spreads = {}
    factors = {'norm_mix': 7.502,
     'norm_q_a': 8.0,
     'norm_kv_a': 8.0,
     'norm_ffn': 3.93,
     'b_conv': 3.925,
     'norm_final': 2.826}
    for name, (base, spread) in spreads.items():
        noise = np.random.default_rng([zlib.crc32(name.encode()), seed]).standard_normal(out[name].shape)
        drawn = base * np.exp(spread * noise) if base else spread * noise
        out[name] = __import__('jax').numpy.asarray(drawn.astype(out[name].dtype))
    for name, factor in factors.items():
        out[name] = (out[name] * factor).astype(out[name].dtype)
    return out
```

```python
import math
from contextlib import ExitStack

import numpy as np
import concourse.bass as bass
from concourse import mybir
from concourse.alu_op_type import AluOpType as ALU

P = 128
S = 256
D = 2048
NB = S // P
KD = D // P
RANK = 512
KR = RANK // P
H = 8
HD = 128
ROPE = 64
HALF = ROPE // 2
FF = 5632
KF = FF // P
EPS = 1e-6
THETA = 10000.0
MASKED = -3.0e38
MLA_SCALE = float((HD + ROPE) ** -0.5)
FOX_SCALE = float(HD ** -0.5)

COL_CQ, COL_CKV, COL_KROPE = 0, RANK, 2 * RANK
COL_FQ = COL_KROPE + ROPE
COL_FV = COL_FQ + 2 * H * HD
COL_F = COL_FQ + 3 * H * HD
COL_GATE = COL_F + H

RAW_SLOTS = 4
SPLIT_SLOTS = 4
CHUNK = 2048
PIECE = CHUNK // 2
SCORES = 3 * P
KIB = 1024


class Phase:

    def __init__(self, before, trips, widths, dmas=None):
        self.trips, self.widths, self.chunks = trips, widths, len(widths)
        dmas = dmas or [1] * self.chunks
        self.chunk0 = before.chunk0 + before.trips * before.chunks if before else 0
        self.offset = (before.offset + before.chunks) % RAW_SLOTS if before else 0
        base = before.landed_after if before else [0] * RAW_SLOTS
        self.per_body = [0] * RAW_SLOTS
        self.local = []
        for c in range(self.chunks):
            self.per_body[self.slot(c)] += 16 * dmas[c]
            self.local.append(base[self.slot(c)] + self.per_body[self.slot(c)])
        self.landed_after = [b + trips * n for b, n in zip(base, self.per_body)]

    def slot(self, c):
        return (self.offset + c) % RAW_SLOTS

    def landed(self, i, c):
        return i * self.per_body[self.slot(c)] + self.local[c]

    def piece(self, i, p):
        return i * (2 * self.chunks) + (2 * self.chunk0 + p + 1)

    def split_slot(self, p):
        return (2 * self.chunk0 + p) % SPLIT_SLOTS

    def freed(self, i, c):
        seam = self.chunks % RAW_SLOTS
        distance = seam if self.trips > 1 and seam and c < seam else RAW_SLOTS
        if isinstance(i, int) and 2 * (self.chunk0 + i * self.chunks + c - distance + 1) <= 0:
            return None
        return i * (2 * self.chunks) + 2 * (self.chunk0 + c - distance + 1)


FOX_W, UKV_W, UQ_W, MISC_W = 2 * 3 * HD, 2 * 2 * HD, 2 * (HD + ROPE), KD // 2 * (ROPE + H)
LATENT = Phase(None, 1, [PIECE] * 4 + [MISC_W] + [PIECE] * 4, [1] * 4 + [2] + [1] * 4)
PROJ0 = Phase(LATENT, 1, [FOX_W] * 4 + [UKV_W, UQ_W], [3] * 4 + [1] * 2)
HEADS = Phase(PROJ0, H - 1, [PIECE] * 4 + [FOX_W] * 4 + [UKV_W, UQ_W], [1] * 4 + [3] * 4 + [1] * 2)
LAST = Phase(HEADS, 1, [PIECE] * 4)
MERGE = Phase(LAST, 4, [PIECE] * 4)
OUT = Phase(MERGE, 2, [PIECE] * 8)
FFN_IN = Phase(OUT, FF // 512, [PIECE] * 8, [2] * 8)
FFN_OUT = Phase(FFN_IN, 2, [PIECE] * 22)

READ_A = {MERGE: 1 + H}
READ_B = {MERGE: 1}
for _phase, _before in ((OUT, MERGE), (FFN_IN, OUT), (FFN_OUT, FFN_IN)):
    READ_A[_phase] = READ_A[_before] + _before.trips
    READ_B[_phase] = READ_B[_before] + _before.trips


TILES_AT = {3: (4, 10), 4: (10, 12), 5: (12, 14), 6: (14, 16), 7: (0, 0)}


class Chain:

    def __init__(self, engine, sem):
        self.engine, self.sem, self.base, self.i, self.n, self.per_body = engine, sem, 0, 0, 0, 0

    def body(self, i, per_body, base=None):
        if base is not None:
            self.base = base
        self.i, self.per_body, self.n = i, per_body, 0

    def done(self, instruction):
        self.n += 1
        instruction.then_inc(self.sem, 1)

    def wait(self, back=0):
        self.engine.wait_ge(self.sem, self.i * self.per_body + (self.base + self.n - back))

    def link(self, instruction):
        self.done(instruction)
        self.wait()


def hybrid_layer(nc, x, positions, norm_mix, w_in, b_forget, norm_q_a, w_uq, norm_kv_a, w_ukv, w_proj_mla,
                 w_proj_fox, w_out, norm_ffn, w_ffn_in, w_conv, b_conv, w_ffn_out, norm_final, y):
    F32, F32R, I32 = mybir.dt.float32, mybir.dt.float32r, mybir.dt.int32
    ACT, AX = mybir.ActivationFunctionType, mybir.AxisListType
    ctx = ExitStack()
    with ctx:
        base = 16512
        RAW_AT = base
        SPLIT_AT = RAW_AT + 32 * KIB
        XT_AT = SPLIT_AT + 32 * KIB
        BIG_AT = XT_AT + 32 * KIB
        RES_AT = BIG_AT + 88 * KIB
        SMALL_AT = RES_AT + 16 * KIB
        small = [SMALL_AT]

        def at(name, shape, offset, dtype=F32):
            return nc.alloc_sbuf_tensor_at(name, shape, dtype, offset=offset)

        def keep(name, shape, dtype=F32):
            t = at(name, shape, small[0], dtype)
            small[0] += -(-4 * int(np.prod(shape[1:])) // 32) * 32
            return t

        raw = [at(f"raw_{s}", [P, CHUNK], RAW_AT + s * 8 * KIB) for s in range(RAW_SLOTS)]
        w_hi = [at(f"w_hi_{s}", [P, PIECE], SPLIT_AT + s * 8 * KIB, F32R) for s in range(SPLIT_SLOTS)]
        w_lo = [at(f"w_lo_{s}", [P, PIECE], SPLIT_AT + s * 8 * KIB + 4 * KIB, F32R) for s in range(SPLIT_SLOTS)]
        xT_hi = at("xT_hi", [P, KD, S], XT_AT, F32R)
        xT_lo = at("xT_lo", [P, KD, S], XT_AT + 16 * KIB, F32R)
        oT_hi = at("oT_hi", [P, 2, H, S], XT_AT, F32R)
        oT_lo = at("oT_lo", [P, 2, H, S], XT_AT + 16 * KIB, F32R)
        gain_final = at("gain_final", [P, D], XT_AT)
        y_out = at("y_out", [P, NB, D], XT_AT + 8 * KIB)
        squares = at("squares", [P, 2, NB, 512], XT_AT + 24 * KIB)
        x_in = at("x_in", [P, NB, D], BIG_AT)
        ckv_n = at("ckv_n", [P, NB, RANK], BIG_AT)
        junk = at("junk", [P, D], BIG_AT + 16 * KIB)
        conv_rows = at("conv_rows", [2 * KF, 4, P], BIG_AT + 24 * KIB)
        gain_rows = at("gain_rows", [2 * KD + 2 * KR, P], BIG_AT + 26 * KIB)
        cq_n = at("cq_n", [P, NB, RANK], BIG_AT + 27 * KIB)
        gates = at("gates", [P, 2 * KD, S], BIG_AT)
        cT_hi = at("cT_hi", [P, 2, KR, S], BIG_AT + 32 * KIB, F32R)
        cT_lo = at("cT_lo", [P, 2, KR, S], BIG_AT + 40 * KIB, F32R)
        stage = [BIG_AT + 48 * KIB]

        def staged(name, shape, dtype=F32):
            t = at(name, shape, stage[0], dtype)
            stage[0] += -(-4 * int(np.prod(shape[1:])) // 32) * 32
            return t

        fqk_hi, fqk_lo = (staged(f"fqk_{n}", [P, 2, S], F32R) for n in ("hi", "lo"))
        fv_hi, fv_lo = (staged(f"fv_{n}", [P, NB, HD], F32R) for n in ("hi", "lo"))
        mqk_hi, mqk_lo = (staged(f"mqk_{n}", [P, 2, S], F32R) for n in ("hi", "lo"))
        mv_hi, mv_lo = (staged(f"mv_{n}", [P, NB, HD], F32R) for n in ("hi", "lo"))
        qr_hi, qr_lo = (staged(f"qr_{n}", [ROPE, S], F32R) for n in ("hi", "lo"))
        kr_hi, kr_lo = (staged(f"kr_{n}", [ROPE, S], F32R) for n in ("hi", "lo"))
        prob = [staged(f"prob_{n}", [P, SCORES]) for n in ("fox", "mla")]
        pT_hi, pT_lo = ([staged(f"pT_{n}_{m}", [P, SCORES], F32R) for n in ("fox", "mla")] for m in ("hi", "lo"))
        fox_bias = staged("fox_bias", [P, SCORES])
        q_rot = staged("q_rot", [P, NB, ROPE])
        rot_a, rot_b = (staged(f"rot_{n}", [P, NB, ROPE]) for n in ("a", "b"))
        cos_t, sin_t = (staged(n, [P, NB, HALF]) for n in ("cos_t", "sin_t"))
        mask = staged("mask", [P, SCORES])
        decay = staged("decay", [P, H, S])
        cum_q = staged("cum_q", [P, NB, H])
        cum_now = staged("cum_now", [P, NB])
        top, den, rden = (staged(n, [P, 2, NB]) for n in ("top", "den", "rden"))
        assert stage[0] <= BIG_AT + 87 * KIB + 512
        ident = at("ident", [P, P], BIG_AT + 87 * KIB + 512)
        mT_hi = at("mT_hi", [P, KD, S], BIG_AT + 32 * KIB, F32R)
        mT_lo = at("mT_lo", [P, KD, S], BIG_AT + 48 * KIB, F32R)
        x_again = at("x_again", [P, NB, D], BIG_AT + 64 * KIB)
        h_n = at("h_n", [P, NB, D], BIG_AT)
        aT_hi = at("aT_hi", [P, KF, S], BIG_AT, F32R)
        aT_lo = at("aT_lo", [P, KF, S], BIG_AT + 44 * KIB, F32R)
        oT = at("oT", [P, 2, H, S], RES_AT)
        h = at("h", [P, NB, D], RES_AT)
        early = [RES_AT]

        def early_at(name, shape, dtype=F32):
            t = at(name, shape, early[0], dtype)
            early[0] += -(-4 * int(np.prod(shape[1:])) // 32) * 32
            return t

        upto = early_at("upto", [P, S])
        inv_freq = early_at("inv_freq", [P, HALF])
        pos_i = early_at("pos_i", [P, NB], I32)
        pos = early_at("pos", [P, NB])
        ang, turns, redu = (early_at(n, [P, 2, NB, HALF]) for n in ("ang", "turns", "redu"))
        bf = early_at("bf", [P, H])
        zf, zabs, zexp, zln, nlf = (early_at(n, [P, NB, H]) for n in ("zf", "zabs", "zexp", "zln", "nlf"))
        k_rot = early_at("k_rot", [P, NB, ROPE])
        nlf_wide = early_at("nlf_wide", [P, NB, P])

        gain_T = keep("gain_T", [P, 2 * KD + 2 * KR])
        conv_T = keep("conv_T", [P, 4, 2, KF])
        conv_now = keep("conv_now", [P, 2, 4, 2, 2])
        ss = keep("ss", [P, NB, 4])
        var, root, rstd, newt = (keep(n, [P, NB]) for n in ("var", "root", "rstd", "newt"))
        hidden = keep("hidden", [P, 2, 2, S])
        th = keep("th", [P, 2, S])
        assert small[0] <= nc.sbuf_usable_end, small[0] - nc.sbuf_usable_end

        bank = ctx.enter_context(nc.psum_tensor("bank", [P, 8, 512], F32))

        def sem(name):
            return ctx.enter_context(nc.semaphore(name))

        def sems(*names):
            return [sem(n) for n in names]

        raw_landed = [sem(f"raw_landed_{s}") for s in range(RAW_SLOTS)]
        hi_done, lo_done, piece_used = sems("hi_done", "lo_done", "piece_used")
        pair_read = sems("pair_a_read", "pair_b_read")
        dve_chain, pool_chain = sems("dve_chain", "pool_chain")
        x_landed = sems("x_landed_0", "x_landed_1")
        rows_landed, pos_landed, bf_landed, x_again_landed, gain_landed, y_landed = sems(
            "rows_landed", "pos_landed", "bf_landed", "x_again_landed", "gain_landed", "y_landed")
        tables_built, rows_turned, rows_read = sems("tables_built", "rows_turned", "rows_read")
        angles_ready, tables_ready, f_abs, f_exp, misc_read, krot_ready, kr_turned, kr_hi_ready, kr_ready = sems(
            "angles_ready", "tables_ready", "f_abs", "f_exp", "misc_read", "krot_ready", "kr_turned", "kr_hi_ready",
            "kr_ready")
        nlf_ready, cumq_done, cumq_read, wide_ready, decay_done, decay_read = sems(
            "nlf_ready", "cumq_done", "cumq_read", "wide_ready", "decay_done", "decay_read")

        class Norm:

            def __init__(self, n):
                self.squared, self.varied, self.rooted, self.scaled, self.turned, self.hi, self.lo = sems(
                    *(f"{n}_{m}" for m in ("squared", "varied", "rooted", "scaled", "turned", "hi", "lo")))

        norm_x, norm_h, norm_cq, norm_ckv, norm_y = (Norm(n) for n in ("x", "h", "cq", "ckv", "y"))
        fox_hi, fox_lo, rope_read, qrot_ready, qr_turned, qr_hi_ready, qr_ready, mqk_hi_ready, mv_hi_ready, mla_lo = \
            sems("fox_hi", "fox_lo", "rope_read", "qrot_ready", "qr_turned", "qr_hi_ready", "qr_ready",
                 "mqk_hi_ready", "mv_hi_ready", "mla_lo")
        scores_done, shifted, expd, normed, p_turned, p_hi, p_lo, o_done, o_read = (
            sems(f"{n}_fox", f"{n}_mla") for n in
            ("scores_done", "shifted", "expd", "normed", "p_turned", "p_hi", "p_lo", "o_done", "o_read"))
        o_split_hi, o_split, merged, m_hi, m_lo = sems("o_split_hi", "o_split", "merged", "m_hi", "m_lo")
        taps_on, first_tap, th_ready, act_ready, a_hi, a_lo, y_ready = sems(
            "taps_on", "first_tap", "th_ready", "act_ready", "a_hi", "a_lo", "y_ready")

        block = ctx.enter_context(nc.Block())

        def tiled(w):
            return w[0].rearrange("(k p) n -> p k n", p=P)

        w_in_v, w_uq_v, w_ukv_v, w_pm_v, w_pf_v, w_out_v, w_fi_v, w_fo_v = (
            tiled(w) for w in (w_in, w_uq, w_ukv, w_proj_mla, w_proj_fox, w_out, w_ffn_in, w_ffn_out))

        @block.sync
        def _(sp):
            def load(phase, i, c, *parts):
                slot, freed = phase.slot(c), phase.freed(i, c)
                if freed is not None:
                    sp.wait_ge(lo_done, freed)
                k, n = parts[0].shape[1:]
                wide = len(parts) * n
                rows = raw[slot][:, 0:k * wide].rearrange("p (k n) -> p k n", k=k)
                for t, part in enumerate(parts):
                    sp.dma_start(rows[:, :, t * n:(t + 1) * n], part).then_inc(raw_landed[slot], 16)

            def load_proj(phase, i, c0, j):
                for c in range(4):
                    load(phase, i, c0 + c, *(w_in_v[:, 4 * c:4 * c + 4, bass.ds(j * HD + (COL_FQ + t * H * HD), HD)]
                                             for t in range(3)))
                load(phase, i, c0 + 4, w_ukv_v[:, :, bass.ds(j * (2 * HD), 2 * HD)])
                load(phase, i, c0 + 5, w_uq_v[:, :, bass.ds(j * (HD + ROPE), HD + ROPE)])

            def load_gate(phase, i, j):
                for c in range(4):
                    load(phase, i, c, w_in_v[:, 4 * c:4 * c + 4, bass.ds(j * 512 + COL_GATE, 512)])

            for b in range(NB):
                sp.dma_start(x_in[:, b, :], x[0, b * P:(b + 1) * P, :]).then_inc(x_landed[b], 16)
            row = 0
            for vec, n in ((norm_mix, KD), (norm_ffn, KD), (norm_q_a, KR), (norm_kv_a, KR)):
                sp.dma_start(gain_rows[row:row + n, :], vec[0].rearrange("(t p) -> t p", p=P)).then_inc(rows_landed, 16)
                row += n
            sp.dma_start(conv_rows[:, 0:3, :], w_conv[0].rearrange("a (t p) -> t a p", p=P)).then_inc(rows_landed, 16)
            sp.dma_start(conv_rows[:, 3, :], b_conv[0].rearrange("(t p) -> t p", p=P)).then_inc(rows_landed, 16)
            for c in range(4):
                load(LATENT, 0, c, w_in_v[:, 4 * c:4 * c + 4, COL_CQ:COL_CQ + RANK])
            for b in range(NB):
                sp.dma_start(pos_i[:, b:b + 1], positions[0, b * P:(b + 1) * P].unsqueeze(1)).then_inc(pos_landed, 16)
            sp.dma_start(bf[:, :], b_forget[0].partition_broadcast(P)).then_inc(bf_landed, 16)
            sp.wait_ge(lo_done, LATENT.freed(0, 4))
            misc = raw[LATENT.slot(4)][:, 0:2 * MISC_W].rearrange("p (k n) -> p k n", k=KD)
            for at0, col, n in ((0, COL_KROPE, ROPE), (ROPE, COL_F, H)):
                sp.dma_start(misc[:, :, at0:at0 + n], w_in_v[:, :, col:col + n]).then_inc(
                    raw_landed[LATENT.slot(4)], 16)
            for c in range(4):
                load(LATENT, 0, 5 + c, w_in_v[:, 4 * c:4 * c + 4, COL_CKV:COL_CKV + RANK])
            load_proj(PROJ0, 0, 0, 0)
            with sp.Fori(0, HEADS.trips) as i:
                load_gate(HEADS, i, i)
                load_proj(HEADS, i, 4, i + 1)
            load_gate(LAST, 0, H - 1)
            with sp.Fori(0, MERGE.trips) as i:
                for c in range(4):
                    k0 = 4 * (c % 2)
                    load(MERGE, i, c, (w_pm_v, w_pf_v)[c // 2][:, k0:k0 + 4, bass.ds(i * 512, 512)])
            sp.wait_ge(o_read[1], H)
            sp.dma_start(x_again[:, :, :], x[0].rearrange("(b p) d -> p b d", p=P)).then_inc(x_again_landed, 16)
            with sp.Fori(0, OUT.trips) as i:
                for c in range(8):
                    k0 = 4 * (c % 4)
                    load(OUT, i, c, w_out_v[:, k0:k0 + 4, bass.ds(i * 1024 + c // 4 * 512, 512)])
            with sp.Fori(0, FFN_IN.trips) as i:
                for c in range(8):
                    k0 = 4 * (c % 4)
                    load(FFN_IN, i, c, *(w_fi_v[:, k0:k0 + 4, bass.ds(i * 512 + (t * FF + c // 4 * 256), 256)]
                                         for t in range(2)))
            with sp.Fori(0, FFN_OUT.trips) as i:
                for c in range(22):
                    k0 = 4 * (c % 11)
                    load(FFN_OUT, i, c, w_fo_v[:, k0:k0 + 4, bass.ds(i * 1024 + c // 11 * 512, 512)])
            sp.wait_ge(piece_used, FFN_IN.piece(FFN_IN.trips - 1, 15))
            sp.dma_start(gain_final[:, :], norm_final.partition_broadcast(P)).then_inc(gain_landed, 16)
            for b in range(NB):
                sp.wait_ge(y_ready, b + 1)
                sp.dma_start(y[0, b * P:(b + 1) * P, :], y_out[:, b, :]).then_inc(y_landed, 16)
            sp.wait_ge(y_landed, 16 * NB)

        @block.gpsimd
        def _(pool):
            nc.gpsimd.memset(ident[:, :], 0.0).then_inc(pool_chain, 1)
            nc.gpsimd.memset(upto[:, :], 1.0).then_inc(pool_chain, 1)
            nc.gpsimd.memset(mask[:, :], 0.0).then_inc(pool_chain, 1)
            pool.wait_ge(pool_chain, 3)
            nc.gpsimd.affine_select(out=ident[:, :], in_=ident[:, :], compare_op=ALU.not_equal, fill=1.0, base=0,
                                    pattern=[[-1, P]], channel_multiplier=1).then_inc(tables_built, 1)
            nc.gpsimd.affine_select(out=upto[:, 0:P], in_=upto[:, 0:P], compare_op=ALU.is_ge, fill=0.0, base=0,
                                    pattern=[[1, P]], channel_multiplier=-1).then_inc(tables_built, 1)
            for diagonal in (0, 2 * P):
                block_of = mask[:, diagonal:diagonal + P]
                nc.gpsimd.affine_select(out=block_of, in_=block_of, compare_op=ALU.is_ge, fill=MASKED, base=0,
                                        pattern=[[-1, P]], channel_multiplier=1).then_inc(tables_built, 1)
            for f in range(HALF):
                last = nc.gpsimd.memset(inv_freq[:, f:f + 1], float(np.float32(THETA ** (-2.0 * f / ROPE))))
            last.then_inc(tables_built, 1)

        def spread_bank(k):
            return bank[:, 4 + k % 4, 0:S]

        def latent_bank(first):
            return lambda k: bank[:, first + k // 2, k % 2 * S:k % 2 * S + S]

        @block.scalar
        def _(act):
            def split_hi(phase, i, p):
                c, n, s = p // 2, phase.widths[p // 2], phase.split_slot(p)
                if p % 2 == 0:
                    act.wait_ge(raw_landed[phase.slot(c)], phase.landed(i, c))
                if phase is not LATENT or p >= SPLIT_SLOTS:
                    act.wait_ge(piece_used, phase.piece(i, p - SPLIT_SLOTS))
                nc.scalar.activation(w_hi[s][:, 0:n], raw[phase.slot(c)][:, p % 2 * n:p % 2 * n + n],
                                     ACT.Copy).then_inc(hi_done, 1)

            def turned_hi(norm, source, gain, out, tiles, at_once=False):
                for k in tiles:
                    act.wait_ge(norm.turned, KR if at_once else k + 1)
                    nc.scalar.activation(out(k), source(k), ACT.Copy,
                                         scale=gain_T[:, gain + k:gain + k + 1]).then_inc(norm.hi, 1)

            def take_root(norm):
                act.wait_ge(norm.varied, 1)
                nc.scalar.activation(root[:, :], var[:, :], ACT.Sqrt).then_inc(norm.rooted, 1)

            def latent_squares(norm, first, done):
                act.wait_ge(piece_used, done)
                for b in range(NB):
                    nc.scalar.activation(junk[:, b * RANK:(b + 1) * RANK], bank[:, first + b, :], ACT.Square,
                                         accum_out=ss[:, b, 0:1]).then_inc(norm.squared, 1)

            for b in range(NB):
                act.wait_ge(x_landed[b], 16)
                if b:
                    act.wait_ge(norm_x.squared, b)
                nc.scalar.activation(junk[:, :], x_in[:, b, :], ACT.Square,
                                     accum_out=ss[:, b, 0:1]).then_inc(norm_x.squared, 1)
            take_root(norm_x)
            act.wait_ge(rows_read, 1)
            for p in range(2):
                split_hi(LATENT, 0, p)
            turned_hi(norm_x, spread_bank, 0, lambda k: xT_hi[:, k, :], range(4))
            for p in range(2, 4):
                split_hi(LATENT, 0, p)
            turned_hi(norm_x, spread_bank, 0, lambda k: xT_hi[:, k, :], range(*TILES_AT[3]))
            for p in range(4, 8):
                split_hi(LATENT, 0, p)
                turned_hi(norm_x, spread_bank, 0, lambda k: xT_hi[:, k, :], range(*TILES_AT[p]))
            act.wait_ge(angles_ready, 1)
            nc.scalar.activation(sin_t[:, :, :], redu[:, 0, :, :], ACT.Sin)
            nc.scalar.activation(cos_t[:, :, :], redu[:, 1, :, :], ACT.Sin).then_inc(tables_ready, 1)
            for p in range(8, 12):
                split_hi(LATENT, 0, p)
            latent_squares(norm_cq, 0, LATENT.piece(0, 7))
            take_root(norm_cq)
            for p in range(12, 14):
                split_hi(LATENT, 0, p)
            act.wait_ge(f_abs, 1)
            nc.scalar.activation(zexp[:, :, :], zabs[:, :, :], ACT.Exp, scale=-1.0).then_inc(f_exp, 1)
            act.wait_ge(f_exp, 1)
            nc.scalar.activation(zln[:, :, :], zexp[:, :, :], ACT.Ln, bias=1.0).then_inc(f_exp, 1)
            for p in range(14, 17):
                split_hi(LATENT, 0, p)
            turned_hi(norm_cq, latent_bank(6), 2 * KD, lambda k: cT_hi[:, 0, k, :], range(KR), at_once=True)
            split_hi(LATENT, 0, 17)
            act.wait_ge(kr_turned, 1)
            nc.scalar.activation(kr_hi[:, :], bank[0:ROPE, 5, 0:S], ACT.Copy).then_inc(kr_hi_ready, 1)
            for p in range(4):
                split_hi(PROJ0, 0, p)
            latent_squares(norm_ckv, 2, LATENT.piece(0, 17))
            take_root(norm_ckv)
            for p in range(4, 8):
                split_hi(PROJ0, 0, p)
            turned_hi(norm_ckv, latent_bank(2), 2 * KD + KR, lambda k: cT_hi[:, 1, k, :], range(KR), at_once=True)
            for p in range(8, 12):
                split_hi(PROJ0, 0, p)

            def stage_fox_hi(projected):
                act.wait_ge(piece_used, projected)
                nc.scalar.activation(fqk_hi[:, :, :].rearrange("p a b -> p (a b)"), bank[:, 4, :], ACT.Copy)
                nc.scalar.activation(fv_hi[:, :, :].rearrange("p a b -> p (a b)"), bank[:, 5, 0:S],
                                     ACT.Copy).then_inc(fox_hi, 1)

            stage_fox_hi(PROJ0.piece(0, 7))

            def exponentials(branch, n):
                act.wait_ge(shifted[branch], n)
                for b, cols in enumerate((slice(0, P), slice(P, SCORES))):
                    last = nc.scalar.activation(prob[branch][:, cols], prob[branch][:, cols], ACT.Exp,
                                                bias=top[:, branch, b:b + 1], accum_out=den[:, branch, b:b + 1])
                last.then_inc(expd[branch], 1)

            def heads_body(phase, i, n):
                for p in range(4):
                    split_hi(phase, i, p)
                act.wait_ge(piece_used, phase.piece(i, -1))
                nc.scalar.activation(mqk_hi[:, :, :].rearrange("p a b -> p (a b)"), bank[:, 6, :],
                                     ACT.Copy).then_inc(mqk_hi_ready, 1)
                act.wait_ge(rope_read, n)
                nc.scalar.activation(mv_hi[:, :, :].rearrange("p a b -> p (a b)"), bank[:, 7, 0:S],
                                     ACT.Copy).then_inc(mv_hi_ready, 1)
                split_hi(phase, i, 4)
                split_hi(phase, i, 5)
                act.wait_ge(qr_turned, n)
                nc.scalar.activation(qr_hi[:, :], bank[0:ROPE, 5, S:2 * S], ACT.Copy).then_inc(qr_hi_ready, 1)
                exponentials(0, n)
                split_hi(phase, i, 6)
                split_hi(phase, i, 7)
                exponentials(1, n)
                after, j, p0 = (phase, i, 8) if phase is HEADS else (MERGE, 0, 0)
                split_hi(after, j, p0)
                split_hi(after, j, p0 + 1)
                for branch in range(2):
                    act.wait_ge(p_turned[branch], n)
                    nc.scalar.activation(pT_hi[branch][:, :], bank[:, 5 + 2 * branch, 0:SCORES],
                                         ACT.Copy).then_inc(p_hi[branch], 1)
                split_hi(after, j, p0 + 2)
                split_hi(after, j, p0 + 3)
                act.wait_ge(piece_used, phase.piece(i, 7))
                for b in range(2):
                    last = nc.scalar.activation(gates[:, bass.ds((n - 1) * 4 + 2 * b, 2), :].rearrange(
                        "p a b -> p (a b)"), bank[:, b, :], ACT.Tanh, scale=0.5)
                last.then_inc(pair_read[0], 1)
                if phase is HEADS:
                    for p in range(12, 20):
                        split_hi(phase, i, p)
                    stage_fox_hi(phase.piece(i, 15))

            with act.Fori(0, HEADS.trips) as i:
                heads_body(HEADS, i, i + 1)
            heads_body(LAST, 0, H)

            act.wait_ge(piece_used, LAST.piece(0, 7))
            for branch in (1, 0):
                act.wait_ge(o_read[branch], H)
                for half in range(2):
                    cols = (slice(None), branch, slice(4 * half, 4 * half + 4), slice(None))
                    nc.scalar.activation(oT_hi[cols], oT[cols], ACT.Copy).then_inc(o_split_hi, 1)

            def merged_hi(n):
                act.wait_ge(merged, n)
                panel = bass.ds((n - 1) * 4, 4)
                nc.scalar.activation(mT_hi[:, panel, :], gates[:, panel, :], ACT.Copy, scale=0.5).then_inc(m_hi, 1)

            for p in range(4, 8):
                split_hi(MERGE, 0, p)
            with act.Fori(1, MERGE.trips) as i:
                for p in range(8):
                    split_hi(MERGE, i, p)
                    if p == 4:
                        merged_hi(i)

            def residual_squares(norm, pair, read, panel):
                act.wait_ge(pair_read[pair], read)
                for b in range(NB):
                    last = nc.scalar.activation(squares[:, pair, b, :],
                                                h[:, b, panel * 512:panel * 512 + 512], ACT.Square,
                                                accum_out=ss[:, b, panel:panel + 1])
                last.then_inc(norm.squared, 1)

            for i in range(OUT.trips):
                for p in range(16):
                    split_hi(OUT, i, p)
                    if i == 0 and p == 4:
                        merged_hi(MERGE.trips)
                    if i and p == 3:
                        residual_squares(norm_h, 1, READ_B[OUT] + i, 2 * i - 1)
                    if p == 11:
                        residual_squares(norm_h, 0, READ_A[OUT] + i + 1, 2 * i)
            for p in range(4):
                split_hi(FFN_IN, 0, p)
            residual_squares(norm_h, 1, READ_B[OUT] + 2, 3)
            take_root(norm_h)
            turned_hi(norm_h, spread_bank, KD, lambda k: xT_hi[:, k, :], range(KD))

            def hidden_panel(i, b, n, between):
                act.wait_ge(piece_used, FFN_IN.piece(i, 8 * b + 7))
                act.wait_ge(taps_on, n)
                for part in range(2):
                    for t in range(2):
                        last = nc.scalar.activation(hidden[:, part, t, :], bank[:, 2 * b + part, t * S:t * S + S],
                                                    ACT.Identity, bias=conv_now[:, b, 3, part, t:t + 1],
                                                    scale=conv_now[:, b, 2, part, t:t + 1])
                    last.then_inc(first_tap, 1)
                between(0)
                act.wait_ge(pair_read[b], i + (READ_A, READ_B)[b][FFN_IN] + 1)
                nc.scalar.activation(th[:, :, :], hidden[:, 0, :, :], ACT.Tanh, scale=0.5).then_inc(th_ready, 1)
                between(1)
                act.wait_ge(act_ready, n)
                nc.scalar.activation(aT_hi[:, bass.ds((n - 1) * 2, 2), :], hidden[:, 0, :, :], ACT.Copy,
                                     scale=0.5).then_inc(a_hi, 1)

            def ffn_in_body(i, first):
                if not first:
                    for p in range(4):
                        split_hi(FFN_IN, i, p)
                    hidden_panel(i - 1, 1, i * 2, lambda step: split_hi(FFN_IN, i, 4 + step))
                else:
                    split_hi(FFN_IN, i, 4)
                    split_hi(FFN_IN, i, 5)
                for p in range(6, 12):
                    split_hi(FFN_IN, i, p)
                hidden_panel(i, 0, i * 2 + 1, lambda step: split_hi(FFN_IN, i, 12 + step))
                split_hi(FFN_IN, i, 14)
                split_hi(FFN_IN, i, 15)

            ffn_in_body(0, True)
            with act.Fori(1, FFN_IN.trips) as i:
                ffn_in_body(i, False)

            for i in range(FFN_OUT.trips):
                for p in range(4):
                    split_hi(FFN_OUT, i, p)
                if i == 0:
                    hidden_panel(FFN_IN.trips - 1, 1, 2 * FFN_IN.trips, lambda step: split_hi(FFN_OUT, 0, 4 + step))
                else:
                    residual_squares(norm_y, 1, READ_B[FFN_OUT] + i, 2 * i - 1)
                    split_hi(FFN_OUT, i, 4)
                    split_hi(FFN_OUT, i, 5)
                for p in range(6, 44):
                    split_hi(FFN_OUT, i, p)
                    if p == 25:
                        residual_squares(norm_y, 0, READ_A[FFN_OUT] + i + 1, 2 * i)
            residual_squares(norm_y, 1, READ_B[FFN_OUT] + 2, 3)
            take_root(norm_y)

        @block.vector
        def _(dve):
            chain = Chain(dve, dve_chain)

            def split_lo(phase, i, p):
                c, n, s = p // 2, phase.widths[p // 2], phase.split_slot(p)
                dve.wait_ge(hi_done, phase.piece(i, p))
                nc.vector.tensor_tensor(w_lo[s][:, 0:n], raw[phase.slot(c)][:, p % 2 * n:p % 2 * n + n],
                                        w_hi[s][:, 0:n].bitcast(F32), ALU.subtract).then_inc(lo_done, 1)

            def reciprocal_root(norm, squares, panels, width):
                dve.wait_ge(norm.squared, squares)
                source = ss[:, :, 0]
                if panels > 1:
                    chain.link(nc.vector.reduce_sum(newt[:, :], ss[:, :, 0:panels], AX.X))
                    source = newt[:, :]
                nc.vector.tensor_scalar(var[:, :], source, 1.0 / width, EPS, ALU.mult, ALU.add).then_inc(norm.varied, 1)
                dve.wait_ge(norm.rooted, 1)
                chain.link(nc.vector.reciprocal(rstd[:, :], root[:, :]))
                chain.link(nc.vector.tensor_tensor(newt[:, :], rstd[:, :], rstd[:, :], ALU.mult))
                chain.link(nc.vector.tensor_tensor(newt[:, :], newt[:, :], var[:, :], ALU.mult))
                chain.link(nc.vector.tensor_scalar(newt[:, :], newt[:, :], -0.5, 1.5, ALU.mult, ALU.add))
                chain.link(nc.vector.tensor_tensor(rstd[:, :], rstd[:, :], newt[:, :], ALU.mult))

            def turned_lo(norm, source, gain, hi, lo, tiles, at_once=False):
                for k in tiles:
                    dve.wait_ge(norm.hi, KR if at_once else k + 1)
                    nc.vector.scalar_tensor_tensor(out=lo(k), in0=source(k), scalar=gain_T[:, gain + k:gain + k + 1],
                                                   in1=hi(k).bitcast(F32), op0=ALU.mult,
                                                   op1=ALU.subtract).then_inc(norm.lo, 1)

            def rotate(out, source, source_read, n, ready):
                cos_2, sin_2 = (t[:, :, :].unsqueeze(2).to_broadcast([P, NB, 2, HALF]) for t in (cos_t, sin_t))
                halves = source.rearrange("p b (t f) -> p b t f", t=2)
                nc.vector.tensor_tensor(rot_a[:, :, :].rearrange("p b (t f) -> p b t f", t=2), halves, cos_2, ALU.mult)
                nc.vector.tensor_tensor(rot_b[:, :, :].rearrange("p b (t f) -> p b t f", t=2), halves, sin_2,
                                        ALU.mult).then_inc(source_read, 1)
                dve.wait_ge(source_read, n)
                nc.vector.tensor_tensor(out[:, :, 0:HALF], rot_a[:, :, 0:HALF], rot_b[:, :, HALF:ROPE], ALU.subtract)
                nc.vector.tensor_tensor(out[:, :, HALF:ROPE], rot_a[:, :, HALF:ROPE], rot_b[:, :, 0:HALF],
                                        ALU.add).then_inc(ready, 1)

            dve.wait_ge(rows_turned, 1)
            nc.vector.tensor_copy(conv_T[:, :, :, :].rearrange("p a h t -> p (a h t)"), bank[:, 4, 0:8 * KF])
            nc.vector.tensor_copy(gain_T[:, :], bank[:, 4, 8 * KF:8 * KF + 2 * KD + 2 * KR]).then_inc(rows_read, 1)
            reciprocal_root(norm_x, NB, 1, D)
            for b in range(NB):
                nc.vector.tensor_scalar(x_in[:, b, :], x_in[:, b, :], rstd[:, b:b + 1], None,
                                        ALU.mult).then_inc(norm_x.scaled, 1)
            for p in range(2):
                split_lo(LATENT, 0, p)
            x_tiles = (norm_x, spread_bank, 0, lambda k: xT_hi[:, k, :], lambda k: xT_lo[:, k, :])
            turned_lo(*x_tiles, range(4))
            for p in range(2, 4):
                split_lo(LATENT, 0, p)
            turned_lo(*x_tiles, range(*TILES_AT[3]))
            for p in range(4, 8):
                split_lo(LATENT, 0, p)
                turned_lo(*x_tiles, range(*TILES_AT[p]))
            dve.wait_ge(pos_landed, 16 * NB)
            dve.wait_ge(tables_built, 5)
            chain.link(nc.vector.tensor_copy(pos[:, :], pos_i[:, :]))
            for b in range(NB):
                for t in range(2):
                    last = nc.vector.tensor_scalar(ang[:, t, b, :], inv_freq[:, :], pos[:, b:b + 1], None, ALU.mult)
            chain.link(last)
            for t in range(2):
                last = nc.vector.tensor_scalar(turns[:, t, :, :], ang[:, t, :, :], 1.0 / (2 * math.pi), 0.25 * t,
                                               ALU.mult, ALU.add)
            chain.link(last)
            to_whole = 1.5 * 2.0 ** 23
            for step in (to_whole, -to_whole):
                chain.link(nc.vector.tensor_scalar(turns[:, :, :, :], turns[:, :, :, :], step, None, ALU.add))
            rest, source = 2 * math.pi, ang
            for bits in (5, 13, 21, None):
                part = rest if bits is None else math.floor(rest * 2.0 ** bits) / 2.0 ** bits
                rest -= part
                chain.link(nc.vector.scalar_tensor_tensor(
                    out=redu[:, :, :, :].rearrange("p a b f -> p (a b f)"),
                    in0=turns[:, :, :, :].rearrange("p a b f -> p (a b f)"), scalar=-part,
                    in1=source[:, :, :, :].rearrange("p a b f -> p (a b f)"), op0=ALU.mult, op1=ALU.add))
                source = redu
            chain.link(nc.vector.tensor_scalar(redu[:, 1, :, :], redu[:, 1, :, :], math.pi / 2, None, ALU.add))
            limit = 3.1415925
            nc.vector.tensor_scalar(redu[:, :, :, :], redu[:, :, :, :], limit, -limit, ALU.min,
                                    ALU.max).then_inc(angles_ready, 1)
            for p in range(8, 12):
                split_lo(LATENT, 0, p)
            reciprocal_root(norm_cq, NB, 1, RANK)
            for b in range(NB):
                last = nc.vector.tensor_scalar(cq_n[:, b, :], bank[:, b, :], rstd[:, b:b + 1], None, ALU.mult)
            last.then_inc(pair_read[0], 1)
            for p in range(12, 14):
                split_lo(LATENT, 0, p)
            dve.wait_ge(piece_used, LATENT.piece(0, 9))
            dve.wait_ge(bf_landed, 16)
            dve.wait_ge(tables_ready, 1)
            for b in range(NB):
                last = nc.vector.tensor_tensor(zf[:, b, :], bank[:, 4, b * P + ROPE:b * P + ROPE + H], bf[:, :], ALU.add)
            chain.link(last)
            nc.vector.scalar_tensor_tensor(out=zabs[:, :, :], in0=zf[:, :, :], scalar=-1.0, in1=zf[:, :, :],
                                           op0=ALU.mult, op1=ALU.max).then_inc(f_abs, 1)
            nc.vector.tensor_scalar(nlf[:, :, :], zf[:, :, :], -1.0, 0.0, ALU.mult, ALU.max)
            rotate(k_rot, bank[:, 4, 0:S].rearrange("p (b n) -> p b n", b=NB)[:, :, 0:ROPE], misc_read, 1, krot_ready)
            split_lo(LATENT, 0, 14)
            split_lo(LATENT, 0, 15)
            dve.wait_ge(f_exp, 2)
            nc.vector.tensor_tensor(nlf[:, :, :], nlf[:, :, :], zln[:, :, :], ALU.add).then_inc(nlf_ready, 1)
            split_lo(LATENT, 0, 16)
            turned_lo(norm_cq, latent_bank(6), 2 * KD, lambda k: cT_hi[:, 0, k, :], lambda k: cT_lo[:, 0, k, :],
                      range(KR), at_once=True)
            split_lo(LATENT, 0, 17)
            dve.wait_ge(kr_hi_ready, 1)
            nc.vector.tensor_tensor(kr_lo[:, :], bank[0:ROPE, 5, 0:S], kr_hi[:, :].bitcast(F32),
                                    ALU.subtract).then_inc(kr_ready, 1)
            dve.wait_ge(cumq_done, 1)
            nc.vector.tensor_scalar(cum_q[:, :, :].rearrange("p b h -> p (b h)"), bank[:, 4, 0:NB * H], -1.0, None,
                                    ALU.mult).then_inc(cumq_read, 1)
            for p in range(4):
                split_lo(PROJ0, 0, p)
            reciprocal_root(norm_ckv, NB, 1, RANK)
            for b in range(NB):
                last = nc.vector.tensor_scalar(ckv_n[:, b, :], bank[:, 2 + b, :], rstd[:, b:b + 1], None, ALU.mult)
            last.then_inc(pair_read[1], 1)
            for head in range(H + 1):
                if head:
                    dve.wait_ge(decay_done, head)
                if head < H:
                    nc.vector.tensor_copy(nlf_wide[:, :, :],
                                          nlf[:, :, head:head + 1].to_broadcast([P, NB, P])).then_inc(wide_ready, 1)
                if head:
                    nc.vector.tensor_copy(decay[:, head - 1, :],
                                          bank[:, 6 + (head - 1) % 2, 0:S]).then_inc(decay_read, 1)
                if head < H:
                    split_lo(PROJ0, 0, 4 + head)
                if head == 3:
                    turned_lo(norm_ckv, latent_bank(2), 2 * KD + KR, lambda k: cT_hi[:, 1, k, :],
                              lambda k: cT_lo[:, 1, k, :], range(KR), at_once=True)

            def stage_fox_lo(n):
                dve.wait_ge(fox_hi, n)
                for hi, lo, source in ((fqk_hi, fqk_lo, bank[:, 4, :]), (fv_hi, fv_lo, bank[:, 5, 0:S])):
                    last = nc.vector.tensor_tensor(lo[:, :, :].rearrange("p a b -> p (a b)"), source,
                                                   hi[:, :, :].rearrange("p a b -> p (a b)").bitcast(F32), ALU.subtract)
                last.then_inc(fox_lo, 1)

            stage_fox_lo(1)
            before_heads, HEAD_STEPS = chain.n, 8

            def shift(branch, n, scale, bias):
                dve.wait_ge(scores_done[branch], n)
                chain.link(nc.vector.scalar_tensor_tensor(
                    out=prob[branch][:, :], in0=bank[:, 4 + 2 * branch, 0:SCORES], scalar=scale, in1=bias[:, :],
                    op0=ALU.mult, op1=ALU.add))
                nc.vector.reduce_max(top[:, branch, 0:1], prob[branch][:, 0:P], AX.X)
                chain.link(nc.vector.reduce_max(top[:, branch, 1:2], prob[branch][:, P:SCORES], AX.X))
                nc.vector.tensor_scalar(top[:, branch, :], top[:, branch, :], -1.0, None,
                                        ALU.mult).then_inc(shifted[branch], 1)

            def normalise(branch, n):
                dve.wait_ge(expd[branch], n)
                chain.link(nc.vector.reciprocal(rden[:, branch, :], den[:, branch, :]))
                for b, cols in enumerate((slice(0, P), slice(P, SCORES))):
                    last = nc.vector.tensor_scalar(prob[branch][:, cols], prob[branch][:, cols],
                                                   rden[:, branch, b:b + 1], None, ALU.mult)
                last.then_inc(normed[branch], 1)

            def heads_body(phase, i, n):
                chain.body(n - 1, HEAD_STEPS, before_heads)
                for p in range(4):
                    split_lo(phase, i, p)
                dve.wait_ge(piece_used, phase.piece(i, -1))
                rotate(q_rot, bank[:, 7, S:S + NB * ROPE].rearrange("p (b n) -> p b n", b=NB), rope_read, n, qrot_ready)
                chain.link(nc.vector.tensor_copy(cum_now[:, :], cum_q[:, :, bass.ds(n - 1, 1)]))
                for b, cols in enumerate((slice(0, P), slice(P, SCORES))):
                    last = nc.vector.scalar_tensor_tensor(
                        out=fox_bias[:, cols], in0=decay[:, bass.ds(n - 1, 1), 0:P * (b + 1)],
                        scalar=cum_now[:, b:b + 1], in1=mask[:, cols], op0=ALU.add, op1=ALU.add)
                chain.done(last)
                dve.wait_ge(mqk_hi_ready, n)
                nc.vector.tensor_tensor(mqk_lo[:, :, :].rearrange("p a b -> p (a b)"), bank[:, 6, :],
                                        mqk_hi[:, :, :].rearrange("p a b -> p (a b)").bitcast(F32), ALU.subtract)
                dve.wait_ge(mv_hi_ready, n)
                nc.vector.tensor_tensor(mv_lo[:, :, :].rearrange("p a b -> p (a b)"), bank[:, 7, 0:S],
                                        mv_hi[:, :, :].rearrange("p a b -> p (a b)").bitcast(F32),
                                        ALU.subtract).then_inc(mla_lo, 1)
                split_lo(phase, i, 4)
                split_lo(phase, i, 5)
                dve.wait_ge(qr_hi_ready, n)
                nc.vector.tensor_tensor(qr_lo[:, :], bank[0:ROPE, 5, S:2 * S], qr_hi[:, :].bitcast(F32),
                                        ALU.subtract).then_inc(qr_ready, 1)
                chain.wait()
                shift(0, n, FOX_SCALE, fox_bias)
                split_lo(phase, i, 6)
                normalise(0, n)
                split_lo(phase, i, 7)
                shift(1, n, MLA_SCALE, mask)
                after, j, p0 = (phase, i, 8) if phase is HEADS else (MERGE, 0, 0)
                split_lo(after, j, p0)
                normalise(1, n)
                split_lo(after, j, p0 + 1)
                for branch in range(2):
                    dve.wait_ge(p_hi[branch], n)
                    nc.vector.tensor_tensor(pT_lo[branch][:, :], bank[:, 5 + 2 * branch, 0:SCORES],
                                            pT_hi[branch][:, :].bitcast(F32), ALU.subtract).then_inc(p_lo[branch], 1)
                split_lo(after, j, p0 + 2)
                split_lo(after, j, p0 + 3)
                for branch in range(2):
                    dve.wait_ge(o_done[branch], n)
                    nc.vector.tensor_copy(oT[:, branch, bass.ds(n - 1, 1), :],
                                          bank[:, 6 + branch, 0:S]).then_inc(o_read[branch], 1)
                if phase is HEADS:
                    for p in range(12, 20):
                        split_lo(phase, i, p)
                    stage_fox_lo(n + 1)
                assert chain.n == HEAD_STEPS, chain.n

            with dve.Fori(0, HEADS.trips) as i:
                heads_body(HEADS, i, i + 1)
            heads_body(LAST, 0, H)
            chain.body(0, 0, before_heads + H * HEAD_STEPS)

            for step, branch in enumerate((1, 0)):
                for half in range(2):
                    dve.wait_ge(o_split_hi, 2 * step + half + 1)
                    cols = (slice(None), branch, slice(4 * half, 4 * half + 4), slice(None))
                    nc.vector.tensor_tensor(oT_lo[cols], oT[cols], oT_hi[cols].bitcast(F32),
                                            ALU.subtract).then_inc(o_split, 1)

            def panel_of(n, first):
                return (slice(None), bass.ds((n - 1) * 4 + first, 4), slice(None))

            def weigh(pair, first, n, done):
                dve.wait_ge(piece_used, done)
                for b in range(2):
                    g = gates[:, bass.ds((n - 1) * 4 + first + 2 * b, 2), :].rearrange("p a b -> p (a b)")
                    last = nc.vector.scalar_tensor_tensor(out=g, in0=g, scalar=1.0, in1=bank[:, 2 * pair + b, :],
                                                          op0=ALU.add, op1=ALU.mult)
                last.then_inc(pair_read[pair], 1)

            def merge_panel(n, done, between):
                weigh(1, KD, n, done)
                dve.wait_ge(pair_read[1], READ_B[MERGE] + n)
                nc.vector.tensor_tensor(gates[panel_of(n, 0)], gates[panel_of(n, 0)], gates[panel_of(n, KD)],
                                        ALU.add).then_inc(merged, 1)
                between()
                dve.wait_ge(m_hi, n)
                nc.vector.scalar_tensor_tensor(out=mT_lo[panel_of(n, 0)], in0=gates[panel_of(n, 0)], scalar=0.5,
                                               in1=mT_hi[panel_of(n, 0)].bitcast(F32), op0=ALU.mult,
                                               op1=ALU.subtract).then_inc(m_lo, 1)

            for p in range(4, 8):
                split_lo(MERGE, 0, p)
            weigh(0, 0, 1, MERGE.piece(0, 3))
            with dve.Fori(1, MERGE.trips) as i:
                for p in range(4):
                    split_lo(MERGE, i, p)
                merge_panel(i, MERGE.piece(i - 1, 7), lambda: split_lo(MERGE, i, 4))
                for p in range(5, 8):
                    split_lo(MERGE, i, p)
                weigh(0, 0, i + 1, MERGE.piece(i, 3))

            def add_residual(pair, done, source, panel):
                dve.wait_ge(piece_used, done)
                cols = slice(panel * 512, panel * 512 + 512)
                for b in range(NB):
                    last = nc.vector.tensor_tensor(h[:, b, cols], bank[:, 2 * pair + b, :], source[:, b, cols], ALU.add)
                last.then_inc(pair_read[pair], 1)

            for i in range(OUT.trips):
                for p in range(16):
                    if i == 0 and p == 4:
                        merge_panel(MERGE.trips, MERGE.piece(MERGE.trips - 1, 7), lambda: split_lo(OUT, 0, 4))
                        dve.wait_ge(x_again_landed, 16)
                    else:
                        split_lo(OUT, i, p)
                    if i and p == 3:
                        add_residual(1, OUT.piece(i - 1, 15), x_again, 2 * i - 1)
                    if p == 11:
                        add_residual(0, OUT.piece(i, 7), x_again, 2 * i)
            for p in range(4):
                split_lo(FFN_IN, 0, p)
            add_residual(1, OUT.piece(1, 15), x_again, 3)
            reciprocal_root(norm_h, 4, 4, D)
            for b in range(NB):
                nc.vector.tensor_scalar(h_n[:, b, :], h[:, b, :], rstd[:, b:b + 1], None,
                                        ALU.mult).then_inc(norm_h.scaled, 1)
            turned_lo(norm_h, spread_bank, KD, lambda k: xT_hi[:, k, :], lambda k: xT_lo[:, k, :], range(KD))
            before_ffn, PANEL_STEPS = chain.base + chain.n, 3

            def hidden_panel(i, b, n, between):
                chain.body(n - 1, PANEL_STEPS, before_ffn)
                nc.vector.tensor_copy(conv_now[:, b, :, :, :],
                                      conv_T[:, :, :, bass.ds((n - 1) * 2, 2)]).then_inc(taps_on, 1)
                for part in range(2):
                    dve.wait_ge(first_tap, (n - 1) * 2 + (part + 1))
                    for back in (1, 2):
                        for t in range(2):
                            out = hidden[:, part, t, back:S]
                            last = nc.vector.scalar_tensor_tensor(
                                out=out, in0=bank[:, 2 * b + part, t * S:t * S + S - back],
                                scalar=conv_now[:, b, 2 - back, part, t:t + 1], in1=out, op0=ALU.mult, op1=ALU.add)
                        if back == 1:
                            chain.link(last)
                last.then_inc(pair_read[b], 1)
                between(0)
                dve.wait_ge(th_ready, n)
                chain.link(nc.vector.scalar_tensor_tensor(out=hidden[:, 0, :, :], in0=th[:, :, :], scalar=1.0,
                                                          in1=hidden[:, 0, :, :], op0=ALU.add, op1=ALU.mult))
                nc.vector.tensor_tensor(hidden[:, 0, :, :], hidden[:, 0, :, :], hidden[:, 1, :, :],
                                        ALU.mult).then_inc(act_ready, 1)
                between(1)
                dve.wait_ge(a_hi, n)
                tiles = bass.ds((n - 1) * 2, 2)
                nc.vector.scalar_tensor_tensor(out=aT_lo[:, tiles, :], in0=hidden[:, 0, :, :], scalar=0.5,
                                               in1=aT_hi[:, tiles, :].bitcast(F32), op0=ALU.mult,
                                               op1=ALU.subtract).then_inc(a_lo, 1)
                assert chain.n == PANEL_STEPS

            def ffn_in_body(i, first):
                if not first:
                    for p in range(4):
                        split_lo(FFN_IN, i, p)
                    hidden_panel(i - 1, 1, i * 2, lambda step: split_lo(FFN_IN, i, 4 + step))
                else:
                    split_lo(FFN_IN, i, 4)
                    split_lo(FFN_IN, i, 5)
                for p in range(6, 12):
                    split_lo(FFN_IN, i, p)
                hidden_panel(i, 0, i * 2 + 1, lambda step: split_lo(FFN_IN, i, 12 + step))
                split_lo(FFN_IN, i, 14)
                split_lo(FFN_IN, i, 15)

            ffn_in_body(0, True)
            with dve.Fori(1, FFN_IN.trips) as i:
                ffn_in_body(i, False)

            for i in range(FFN_OUT.trips):
                for p in range(4):
                    split_lo(FFN_OUT, i, p)
                if i == 0:
                    hidden_panel(FFN_IN.trips - 1, 1, 2 * FFN_IN.trips, lambda step: split_lo(FFN_OUT, 0, 4 + step))
                    chain.body(0, 0, before_ffn + 2 * FFN_IN.trips * PANEL_STEPS)
                else:
                    add_residual(1, FFN_OUT.piece(i - 1, 43), h, 2 * i - 1)
                    split_lo(FFN_OUT, i, 4)
                    split_lo(FFN_OUT, i, 5)
                for p in range(6, 44):
                    split_lo(FFN_OUT, i, p)
                    if p == 25:
                        add_residual(0, FFN_OUT.piece(i, 21), h, 2 * i)
            add_residual(1, FFN_OUT.piece(1, 43), h, 3)
            reciprocal_root(norm_y, 4, 4, D)
            dve.wait_ge(gain_landed, 16)
            for b in range(NB):
                nc.vector.scalar_tensor_tensor(out=y_out[:, b, :], in0=h[:, b, :], scalar=rstd[:, b:b + 1],
                                               in1=gain_final[:, :], op0=ALU.mult, op1=ALU.mult).then_inc(y_ready, 1)

        @block.tensor
        def _(pe):
            def mm(out, still, moving, start, stop):
                return nc.tensor.matmul(out, still, moving, start=start, stop=stop, skip_group_check=True)

            def product(out, still, moving, start, stop):
                mm(out, still[0], moving[0], start, False)
                mm(out, still[0], moving[1], False, False)
                return mm(out, still[1], moving[0], False, stop)

            def weights(phase, p, col, n):
                s = phase.split_slot(p)
                return w_hi[s][:, col:col + n], w_lo[s][:, col:col + n]

            def piece(phase, i, p, products):
                pe.wait_ge(lo_done, phase.piece(i, p))
                products().then_inc(piece_used, 1)

            def still_tiles(phase, p, k0, tiles, wide, outs, xk, k_last):
                def run():
                    for kk in range(2):
                        k = k0 + kk
                        for t in range(tiles):
                            last = product(outs(t), weights(phase, p, kk * wide + t * P, P), xk(k),
                                           k == 0 and t % 2 == 0, k == k_last)
                    return last
                return run

            def moving_tiles(phase, p, k0, wide, outs, xk, k_last, col=0, n=None, shared=False):
                def run():
                    for kk in range(2):
                        k = k0 + kk
                        for b in range(NB):
                            hi, lo = xk(k)
                            last = product(outs(b), (hi[:, b * P:(b + 1) * P], lo[:, b * P:(b + 1) * P]),
                                           weights(phase, p, kk * wide + col, n or wide),
                                           k == 0 and not (shared and b), k == k_last)
                    return last
                return run

            def xk(k):
                return xT_hi[:, k, :], xT_lo[:, k, :]

            def turn(norm, source, target, tiles):
                for k in tiles:
                    if k >= 4:
                        pe.wait_ge(norm.lo, k - 3)
                    for b in range(NB):
                        last = nc.tensor.transpose(target(k)[:, b * P:(b + 1) * P], source[:, b, k * P:(k + 1) * P],
                                                   ident[:, :])
                    last.then_inc(norm.turned, 1)

            pe.wait_ge(tables_built, 5)
            pe.wait_ge(rows_landed, 6 * 16)
            for a in range(4):
                nc.tensor.transpose(bank[:, 4, a * 2 * KF:(a + 1) * 2 * KF], conv_rows[:, a, :], ident[0:2 * KF, 0:2 * KF])
            n_rows = 2 * KD + 2 * KR
            nc.tensor.transpose(bank[:, 4, 8 * KF:8 * KF + n_rows], gain_rows[:, :],
                                ident[0:n_rows, 0:n_rows]).then_inc(rows_turned, 1)
            pe.wait_ge(rows_read, 1)
            pe.wait_ge(norm_x.scaled, NB)
            turn(norm_x, x_in, spread_bank, range(4))
            for p in range(8):
                pe.wait_ge(norm_x.lo, 2 * p + 2)
                piece(LATENT, 0, p, moving_tiles(LATENT, p, 2 * p, RANK, lambda b: bank[:, b, :], xk, KD - 1))
                if 2 * p + 4 < KD:
                    turn(norm_x, x_in, spread_bank, range(2 * p + 4, 2 * p + 6))
            for p in range(8, 10):
                def run():
                    for kk in range(8):
                        k = 8 * (p - 8) + kk
                        for b in range(NB):
                            hi, lo = xk(k)
                            last = product(bank[:, 4, b * P:b * P + ROPE + H],
                                           (hi[:, b * P:(b + 1) * P], lo[:, b * P:(b + 1) * P]),
                                           weights(LATENT, p, kk * (ROPE + H), ROPE + H), k == 0 and b == 0, k == KD - 1)
                    return last
                piece(LATENT, 0, p, run)
            for p in range(10, 18):
                piece(LATENT, 0, p, moving_tiles(LATENT, p, 2 * (p - 10), RANK, lambda b: bank[:, 2 + b, :], xk, KD - 1))
                if p == 12:
                    pe.wait_ge(pair_read[0], 1)
                    turn(norm_cq, cq_n, latent_bank(6), range(KR))
                if p == 14:
                    pe.wait_ge(krot_ready, 1)
                    for b in range(NB):
                        last = nc.tensor.transpose(bank[0:ROPE, 5, b * P:(b + 1) * P], k_rot[:, b, :], ident[:, :])
                    last.then_inc(kr_turned, 1)
                if p == 16:
                    pe.wait_ge(nlf_ready, 1)
                    nc.tensor.matmul(bank[:, 4, 0:H], upto[:, 0:P], nlf[:, 0, :], start=True, stop=True)
                    nc.tensor.matmul(bank[:, 4, H:2 * H], upto[:, P:S], nlf[:, 0, :], start=True, stop=False)
                    nc.tensor.matmul(bank[:, 4, H:2 * H], upto[:, 0:P], nlf[:, 1, :], start=False,
                                     stop=True).then_inc(cumq_done, 1)

            def project_fox(phase, i, p0, after=lambda p: None):
                for q in range(8):
                    p = p0 + q
                    wide = 3 * HD

                    def run():
                        still_tiles(phase, p, 2 * q, 2, wide, lambda t: bank[:, 4, t * S:t * S + S], xk, KD - 1)()
                        return moving_tiles(phase, p, 2 * q, wide, lambda b: bank[:, 5, b * HD:(b + 1) * HD], xk, KD - 1,
                                            col=2 * HD, n=HD, shared=True)()

                    piece(phase, i, p, run)
                    after(q)

            def project_mla(phase, i, p0):
                def latent(which):
                    return lambda k: (cT_hi[:, which, k, :], cT_lo[:, which, k, :])

                for q in range(2):
                    def run():
                        for kk in range(2):
                            k = 2 * q + kk
                            hi, lo = latent(1)(k)
                            product(bank[:, 6, S:2 * S], weights(phase, p0 + q, kk * 2 * HD, HD), (hi, lo), k == 0,
                                    k == KR - 1)
                            for b in range(NB):
                                last = product(bank[:, 7, b * HD:(b + 1) * HD],
                                               (hi[:, b * P:(b + 1) * P], lo[:, b * P:(b + 1) * P]),
                                               weights(phase, p0 + q, kk * 2 * HD + HD, HD), k == 0 and b == 0,
                                               k == KR - 1)
                        return last
                    piece(phase, i, p0 + q, run)
                for q in range(2):
                    def run():
                        for kk in range(2):
                            k = 2 * q + kk
                            hi, lo = latent(0)(k)
                            product(bank[:, 6, 0:S], weights(phase, p0 + 2 + q, kk * (HD + ROPE), HD), (hi, lo), False,
                                    k == KR - 1)
                            for b in range(NB):
                                last = product(bank[:, 7, S + b * ROPE:S + (b + 1) * ROPE],
                                               (hi[:, b * P:(b + 1) * P], lo[:, b * P:(b + 1) * P]),
                                               weights(phase, p0 + 2 + q, kk * (HD + ROPE) + HD, ROPE), False,
                                               k == KR - 1)
                        return last
                    piece(phase, i, p0 + 2 + q, run)

            def decay_of(head):
                pe.wait_ge(wide_ready, head + 1)
                if head >= 2:
                    pe.wait_ge(decay_read, head - 1)
                out = bank[:, 6 + head % 2, 0:S]
                nc.tensor.matmul(out, nlf_wide[:, 0, :], upto[:, :], start=True, stop=False)
                nc.tensor.matmul(out[:, P:S], nlf_wide[:, 1, :], upto[:, 0:P], start=False,
                                 stop=True).then_inc(decay_done, 1)
                if head == 3:
                    pe.wait_ge(pair_read[1], 1)
                    turn(norm_ckv, ckv_n, latent_bank(2), range(KR))

            pe.wait_ge(norm_cq.lo, KR)
            pe.wait_ge(kr_ready, 1)
            pe.wait_ge(cumq_read, 1)
            project_fox(PROJ0, 0, 0, decay_of)
            pe.wait_ge(norm_ckv.lo, KR)
            pe.wait_ge(decay_read, H)
            project_mla(PROJ0, 0, 8)

            def scores(branch, n, qk_hi, qk_lo, rotary):
                for b in range(NB):
                    out = bank[:, 4 + 2 * branch, b * P:b * P + (b + 1) * P]
                    qs, ks = slice(b * P, (b + 1) * P), slice(0, (b + 1) * P)
                    last = product(out, (qk_hi[:, 0, qs], qk_lo[:, 0, qs]), (qk_hi[:, 1, ks], qk_lo[:, 1, ks]), True,
                                   not rotary)
                    if rotary:
                        last = product(out, (qr_hi[:, qs], qr_lo[:, qs]), (kr_hi[:, ks], kr_lo[:, ks]), False, True)
                last.then_inc(scores_done[branch], 1)

            def turn_probabilities(branch, n):
                pe.wait_ge(normed[branch], n)
                for blk in range(3):
                    last = nc.tensor.transpose(bank[:, 5 + 2 * branch, blk * P:(blk + 1) * P],
                                               prob[branch][:, blk * P:(blk + 1) * P], ident[:, :])
                last.then_inc(p_turned[branch], 1)

            def outputs(branch, n, v_hi, v_lo):
                pe.wait_ge(p_lo[branch], n)
                out = bank[:, 6 + branch, 0:S]
                product(out, (v_hi[:, 0, :], v_lo[:, 0, :]), (pT_hi[branch][:, 0:S], pT_lo[branch][:, 0:S]), True, False)
                product(out[:, P:S], (v_hi[:, 1, :], v_lo[:, 1, :]),
                        (pT_hi[branch][:, S:SCORES], pT_lo[branch][:, S:SCORES]), False, True).then_inc(o_done[branch], 1)

            def heads_body(phase, i, n):
                pe.wait_ge(pair_read[0], n)
                for p in range(8):
                    piece(phase, i, p, still_tiles(phase, p, 2 * p, 4, 4 * P,
                                                   lambda t: bank[:, t // 2, t % 2 * S:t % 2 * S + S], xk, KD - 1))
                    if p == 1:
                        pe.wait_ge(qrot_ready, n)
                        pe.wait_ge(fox_lo, n)
                        scores(0, n, fqk_hi, fqk_lo, False)
                        for b in range(NB):
                            last = nc.tensor.transpose(bank[0:ROPE, 5, S + b * P:S + (b + 1) * P], q_rot[:, b, :],
                                                       ident[:, :])
                        last.then_inc(qr_turned, 1)
                    if p == 3:
                        pe.wait_ge(mla_lo, n)
                        pe.wait_ge(qr_ready, n)
                        scores(1, n, mqk_hi, mqk_lo, True)
                    if p == 5:
                        turn_probabilities(0, n)
                        turn_probabilities(1, n)
                outputs(0, n, fv_hi, fv_lo)
                outputs(1, n, mv_hi, mv_lo)
                if phase is HEADS:
                    project_fox(phase, i, 8)
                    pe.wait_ge(o_read[0], n)
                    pe.wait_ge(o_read[1], n)
                    project_mla(phase, i, 16)

            with pe.Fori(0, HEADS.trips) as i:
                heads_body(HEADS, i, i + 1)
            heads_body(LAST, 0, H)

            def bank_of(pair):
                return lambda t: bank[:, 2 * pair + t // 2, t % 2 * S:t % 2 * S + S]

            with pe.Fori(0, MERGE.trips) as i:
                for p in range(8):
                    pair, q = p // 4, p % 4
                    if q == 0:
                        pe.wait_ge(pair_read[pair], i + (READ_A, READ_B)[pair][MERGE])
                    pe.wait_ge(o_split, p // 2 + 1)
                    piece(MERGE, i, p, still_tiles(
                        MERGE, p, 2 * q, 4, 4 * P, bank_of(pair),
                        lambda k: (oT_hi[:, 1 - pair, k, :], oT_lo[:, 1 - pair, k, :]), H - 1))

            def moving_panels(phase, i, per_panel, activation, ready, k_last):
                for p in range(2 * per_panel):
                    pair, q = p // per_panel, p % per_panel
                    if q == 0:
                        pe.wait_ge(pair_read[pair], i + (READ_A, READ_B)[pair][phase])
                    pe.wait_ge(*ready(q))
                    piece(phase, i, p, moving_tiles(phase, p, 2 * q, 512, lambda b: bank[:, 2 * pair + b, :],
                                                    activation, k_last))

            with pe.Fori(0, OUT.trips) as i:
                moving_panels(OUT, i, 8, lambda k: (mT_hi[:, k, :], mT_lo[:, k, :]), lambda q: (m_lo, q // 2 + 1), KD - 1)

            pe.wait_ge(norm_h.scaled, NB)
            turn(norm_h, h_n, spread_bank, range(KD))
            with pe.Fori(0, FFN_IN.trips) as i:
                for p in range(16):
                    pair, q = p // 8, p % 8
                    if q == 0:
                        pe.wait_ge(pair_read[pair], i + (READ_A, READ_B)[pair][FFN_IN])
                    if pair == 0:
                        pe.wait_ge(norm_h.lo, 2 * q + 2)
                    piece(FFN_IN, i, p, still_tiles(FFN_IN, p, 2 * q, 4, 4 * P, bank_of(pair), xk, KD - 1))
            with pe.Fori(0, FFN_OUT.trips) as i:
                moving_panels(FFN_OUT, i, 22, lambda k: (aT_hi[:, k, :], aT_lo[:, k, :]), lambda q: (a_lo, q + 1), KF - 1)


NAMES = ["x", "positions", "norm_mix", "w_in", "b_forget", "norm_q_a", "w_uq", "norm_kv_a", "w_ukv", "w_proj_mla",
         "w_proj_fox", "w_out", "norm_ffn", "w_ffn_in", "w_conv", "b_conv", "w_ffn_out", "norm_final"]


def kernel(**inputs):
    import concourse.bacc as bacc
    from concourse.bass_utils import run_bass_kernel_spmd

    nc = bacc.Bacc("TRN2", target_bir_lowering=False, num_devices=1)
    arrays, args = {}, []
    for name in NAMES:
        a = np.ascontiguousarray(inputs[name])
        arrays[name] = a
        args.append(nc.dram_tensor(name, a.shape, mybir.dt.from_np(a.dtype), kind="ExternalInput").ap())
    y = nc.dram_tensor("y", (1, S, D), mybir.dt.float32, kind="ExternalOutput").ap()
    hybrid_layer(nc, *args, y)
    result = run_bass_kernel_spmd(nc, [arrays], core_ids=[0])
    return result.results[0]["y"]
```

```python
import math
from contextlib import ExitStack

import numpy as np
import concourse.bass as bass
from concourse import mybir
from concourse.alu_op_type import AluOpType as ALU

P = 128
S = 256
D = 2048
NB = S // P
KD = D // P
RANK = 512
KR = RANK // P
H = 8
HD = 128
ROPE = 64
HALF = ROPE // 2
FF = 5632
KF = FF // P
EPS = 1e-6
THETA = 10000.0
MASKED = -3.0e38
MLA_SCALE = float((HD + ROPE) ** -0.5)
FOX_SCALE = float(HD ** -0.5)

COL_CQ, COL_CKV, COL_KROPE = 0, RANK, 2 * RANK
COL_FQ = COL_KROPE + ROPE
COL_FV = COL_FQ + 2 * H * HD
COL_F = COL_FQ + 3 * H * HD
COL_GATE = COL_F + H

RAW_SLOTS = 4
SPLIT_SLOTS = 4
CHUNK = 2048
PIECE = CHUNK // 2
SCORES = 3 * P
KIB = 1024


class Phase:

    def __init__(self, before, trips, widths, dmas=None):
        self.trips, self.widths, self.chunks = trips, widths, len(widths)
        dmas = dmas or [1] * self.chunks
        self.chunk0 = before.chunk0 + before.trips * before.chunks if before else 0
        self.offset = (before.offset + before.chunks) % RAW_SLOTS if before else 0
        base = before.landed_after if before else [0] * RAW_SLOTS
        self.per_body = [0] * RAW_SLOTS
        self.local = []
        for c in range(self.chunks):
            self.per_body[self.slot(c)] += 16 * dmas[c]
            self.local.append(base[self.slot(c)] + self.per_body[self.slot(c)])
        self.landed_after = [b + trips * n for b, n in zip(base, self.per_body)]

    def slot(self, c):
        return (self.offset + c) % RAW_SLOTS

    def landed(self, i, c):
        return i * self.per_body[self.slot(c)] + self.local[c]

    def piece(self, i, p):
        return i * (2 * self.chunks) + (2 * self.chunk0 + p + 1)

    def split_slot(self, p):
        return (2 * self.chunk0 + p) % SPLIT_SLOTS

    def freed(self, i, c):
        seam = self.chunks % RAW_SLOTS
        distance = seam if self.trips > 1 and seam and c < seam else RAW_SLOTS
        if isinstance(i, int) and 2 * (self.chunk0 + i * self.chunks + c - distance + 1) <= 0:
            return None
        return i * (2 * self.chunks) + 2 * (self.chunk0 + c - distance + 1)


MISC = ROPE + H
FOX_W, UKV_W, UQ_W, MISC_W = 2 * 3 * HD, 2 * 2 * HD, 2 * HD, KD // 2 * MISC
LATENT = Phase(None, 1, [PIECE] * 4 + [MISC_W] + [PIECE] * 4, [1] * 4 + [2] + [1] * 4)
PROJ0 = Phase(LATENT, 1, [FOX_W] * 4 + [PIECE, UKV_W, UQ_W], [3] * 4 + [KR, 1, 1])
HEAD_CHUNKS, HEAD_DMAS = [PIECE] * 4 + [FOX_W] * 4 + [UKV_W, UQ_W], [1] * 4 + [3] * 4 + [1] * 2
HEAD_PIECES = 2 * len(HEAD_CHUNKS)
HEADS = Phase(PROJ0, (H - 2) // 2, HEAD_CHUNKS * 2, HEAD_DMAS * 2)
SEVENTH = Phase(HEADS, 1, HEAD_CHUNKS, HEAD_DMAS)
LAST = Phase(SEVENTH, 1, [PIECE] * 4)
MERGE = Phase(LAST, 4, [PIECE] * 4)
OUT = Phase(MERGE, 2, [PIECE] * 8)
FFN_IN = Phase(OUT, FF // 512, [PIECE] * 8, [2] * 8)
FFN_OUT = Phase(FFN_IN, 2, [PIECE] * 22)

READ_A = {MERGE: 1 + H}
READ_B = {MERGE: 1}
for _phase, _before in ((OUT, MERGE), (FFN_IN, OUT), (FFN_OUT, FFN_IN)):
    READ_A[_phase] = READ_A[_before] + _before.trips
    READ_B[_phase] = READ_B[_before] + _before.trips


O_GROUPS = ((1, slice(0, 4)), (1, slice(4, H - 1)), (1, slice(H - 1, H)), (0, slice(0, 4)), (0, slice(4, H)))
GROUPS_READ = (1, 1, 2, 3, 4, 4, 5, 5)

TILES_AT = {3: (4, 10), 4: (10, 12), 5: (12, 14), 6: (14, 16), 7: (0, 0)}


class Chain:

    def __init__(self, engine, sem):
        self.engine, self.sem, self.base, self.i, self.n, self.per_body = engine, sem, 0, 0, 0, 0

    def body(self, i, per_body, base=None):
        if base is not None:
            self.base = base
        self.i, self.per_body, self.n = i, per_body, 0

    def done(self, instruction):
        self.n += 1
        instruction.then_inc(self.sem, 1)

    def wait(self, back=0):
        self.engine.wait_ge(self.sem, self.i * self.per_body + (self.base + self.n - back))

    def link(self, instruction):
        self.done(instruction)
        self.wait()


def hybrid_layer(nc, x, positions, norm_mix, w_in, b_forget, norm_q_a, w_uq, norm_kv_a, w_ukv, w_proj_mla,
                 w_proj_fox, w_out, norm_ffn, w_ffn_in, w_conv, b_conv, w_ffn_out, norm_final, y):
    F32, F32R, I32 = mybir.dt.float32, mybir.dt.float32r, mybir.dt.int32
    ACT, AX = mybir.ActivationFunctionType, mybir.AxisListType
    ctx = ExitStack()
    with ctx:
        base = 16512
        RAW_AT = base
        SPLIT_AT = RAW_AT + 32 * KIB
        XT_AT = SPLIT_AT + 32 * KIB
        BIG_AT = XT_AT + 32 * KIB
        RES_AT = BIG_AT + 88 * KIB
        SMALL_AT = RES_AT + 16 * KIB
        small = [SMALL_AT]

        def at(name, shape, offset, dtype=F32):
            return nc.alloc_sbuf_tensor_at(name, shape, dtype, offset=offset)

        def keep(name, shape, dtype=F32):
            t = at(name, shape, small[0], dtype)
            small[0] += -(-4 * int(np.prod(shape[1:])) // 32) * 32
            return t

        raw = [at(f"raw_{s}", [P, CHUNK], RAW_AT + s * 8 * KIB) for s in range(RAW_SLOTS)]
        w_hi = [at(f"w_hi_{s}", [P, PIECE], SPLIT_AT + s * 8 * KIB, F32R) for s in range(SPLIT_SLOTS)]
        w_lo = [at(f"w_lo_{s}", [P, PIECE], SPLIT_AT + s * 8 * KIB + 4 * KIB, F32R) for s in range(SPLIT_SLOTS)]
        xT_hi = at("xT_hi", [P, KD, S], XT_AT, F32R)
        xT_lo = at("xT_lo", [P, KD, S], XT_AT + 16 * KIB, F32R)
        mT_hi = at("mT_hi", [P, KD, S], XT_AT, F32R)
        mT_lo = at("mT_lo", [P, KD, S], XT_AT + 16 * KIB, F32R)
        gain_final = at("gain_final", [P, D], XT_AT)
        y_out = at("y_out", [P, NB, D], XT_AT + 8 * KIB)
        squares_y = at("squares_y", [P, 2, NB, 512], XT_AT + 24 * KIB)
        x_in = at("x_in", [P, NB, D], BIG_AT)
        ckv_n = at("ckv_n", [P, NB, RANK], BIG_AT)
        junk = at("junk", [P, D], BIG_AT + 16 * KIB)
        conv_rows = at("conv_rows", [2 * KF, 4, P], BIG_AT + 24 * KIB)
        gain_rows = at("gain_rows", [2 * KD + 2 * KR, P], BIG_AT + 26 * KIB)
        cq_n = at("cq_n", [P, NB, RANK], BIG_AT + 27 * KIB)
        gates = at("gates", [P, 2 * KD, S], BIG_AT)
        cT_hi = at("cT_hi", [P, 2, KR, S], BIG_AT + 32 * KIB, F32R)
        cT_lo = at("cT_lo", [P, 2, KR, S], BIG_AT + 40 * KIB, F32R)
        stage = [BIG_AT + 48 * KIB]

        def staged(name, shape, dtype=F32):
            t = at(name, shape, stage[0], dtype)
            stage[0] += -(-4 * int(np.prod(shape[1:])) // 32) * 32
            return t

        fqk_hi, fqk_lo = (staged(f"fqk_{n}", [P, 2, S], F32R) for n in ("hi", "lo"))
        fv_hi, fv_lo = (staged(f"fv_{n}", [P, NB, HD], F32R) for n in ("hi", "lo"))
        mqk_hi, mqk_lo = (staged(f"mqk_{n}", [P, 2, S], F32R) for n in ("hi", "lo"))
        mv_hi, mv_lo = (staged(f"mv_{n}", [P, NB, HD], F32R) for n in ("hi", "lo"))
        qr_hi, qr_lo = (staged(f"qr_{n}", [ROPE, S], F32R) for n in ("hi", "lo"))
        kr_hi, kr_lo = (staged(f"kr_{n}", [ROPE, S], F32R) for n in ("hi", "lo"))
        prob = [staged(f"prob_{n}", [P, SCORES]) for n in ("fox", "mla")]
        pT_hi, pT_lo = ([staged(f"pT_{n}_{m}", [P, SCORES], F32R) for n in ("fox", "mla")] for m in ("hi", "lo"))
        fox_bias = staged("fox_bias", [P, SCORES])
        q_rot = staged("q_rot", [P, NB, ROPE])
        vT = [staged(f"vT_{n}", [P, S]) for n in ("fox", "mla")]
        mask = staged("mask", [P, SCORES])
        decay = staged("decay", [P, H, S])
        cum_q = staged("cum_q", [P, NB, H])
        cum_now = staged("cum_now", [P, NB])
        top, den, rden = (staged(n, [P, 2, NB]) for n in ("top", "den", "rden"))
        assert stage[0] <= BIG_AT + 87 * KIB, stage[0] - BIG_AT - 87 * KIB
        ones = at("ones", [P, P], BIG_AT + 87 * KIB)
        ident = at("ident", [P, P], BIG_AT + 87 * KIB + 512)
        oT_split = [[at(f"oT_{n}_{m}", [P, H, S], BIG_AT + place * KIB, F32R) for m, place in halves]
                    for n, halves in (("fox", (("hi", 48), ("lo", 56))), ("mla", (("hi", 32), ("lo", 40))))]
        x_again = at("x_again", [P, NB, D], BIG_AT + 64 * KIB)
        hT = at("hT", [P, KD, S], BIG_AT)
        squares_h = at("squares_h", [P, 2, NB, 512], BIG_AT + 16 * KIB)
        rstd_wide = at("rstd_wide", [P, S], BIG_AT + 80 * KIB)
        rstd_diag = at("rstd_diag", [P, NB, P], BIG_AT + 81 * KIB)
        aT_hi = at("aT_hi", [P, KF, S], BIG_AT, F32R)
        aT_lo = at("aT_lo", [P, KF, S], BIG_AT + 44 * KIB, F32R)
        oT = at("oT", [P, 2, H, S], RES_AT)
        h = at("h", [P, NB, D], RES_AT)
        early = [RES_AT]

        def early_at(name, shape, dtype=F32):
            t = at(name, shape, early[0], dtype)
            early[0] += -(-4 * int(np.prod(shape[1:])) // 32) * 32
            return t

        upto = early_at("upto", [P, S])
        inv_freq = early_at("inv_freq", [P, HALF])
        pos_i = early_at("pos_i", [P, NB], I32)
        pos = early_at("pos", [P, NB])
        ang, turns, redu = (early_at(n, [P, 2, NB, HALF]) for n in ("ang", "turns", "redu"))
        bf = early_at("bf", [P, H])
        zf, zabs, zexp, zln, nlf = (early_at(n, [P, NB, H]) for n in ("zf", "zabs", "zexp", "zln", "nlf"))
        k_rot = early_at("k_rot", [P, NB, ROPE])
        cos_t, sin_t = (early_at(n, [P, NB, HALF]) for n in ("cos_t", "sin_t"))
        misc_T = early_at("misc_T", [MISC, S])
        rot_a, rot_b = (early_at(f"rot_{n}", [P, NB, H * ROPE]) for n in ("a", "b"))
        nlf_wide = early_at("nlf_wide", [P, NB, P])

        assert early[0] <= SMALL_AT
        gain_T = keep("gain_T", [P, 2 * KD + 2 * KR])
        conv_T = keep("conv_T", [P, 4, 2, KF])
        conv_now = keep("conv_now", [P, 2, 4, 2, 2])
        ss = keep("ss", [P, NB, 4])
        var, root, rstd, newt = (keep(n, [P, NB]) for n in ("var", "root", "rstd", "newt"))
        q_rot_all = at("q_rot_all", [P, NB, H, ROPE], small[0])
        hidden = keep("hidden", [P, 2, 2, S])
        th = keep("th", [P, 2, S])
        assert small[0] <= nc.sbuf_usable_end, small[0] - nc.sbuf_usable_end

        bank = ctx.enter_context(nc.psum_tensor("bank", [P, 8, 512], F32))

        def sem(name):
            return ctx.enter_context(nc.semaphore(name))

        def sems(*names):
            return [sem(n) for n in names]

        raw_landed = [sem(f"raw_landed_{s}") for s in range(RAW_SLOTS)]
        hi_done, lo_done, piece_used = sems("hi_done", "lo_done", "piece_used")
        pair_read = sems("pair_a_read", "pair_b_read")
        dve_chain, pool_chain = sems("dve_chain", "pool_chain")
        x_landed = sems("x_landed_0", "x_landed_1")
        rows_landed, pos_landed, bf_landed, x_again_landed, gain_landed, y_landed = sems(
            "rows_landed", "pos_landed", "bf_landed", "x_again_landed", "gain_landed", "y_landed")
        tables_built, rows_turned, rows_read = sems("tables_built", "rows_turned", "rows_read")
        angles_ready, tables_ready, f_abs, f_exp, misc_read, krot_ready, kr_turned, kr_hi_ready, kr_ready = sems(
            "angles_ready", "tables_ready", "f_abs", "f_exp", "misc_read", "krot_ready", "kr_turned", "kr_hi_ready",
            "kr_ready")
        nlf_ready, cumq_done, cumq_read, wide_ready, decay_done, decay_read = sems(
            "nlf_ready", "cumq_done", "cumq_read", "wide_ready", "decay_done", "decay_read")

        class Norm:

            def __init__(self, n):
                self.squared, self.varied, self.rooted, self.scaled, self.turned, self.hi, self.lo = sems(
                    *(f"{n}_{m}" for m in ("squared", "varied", "rooted", "scaled", "turned", "hi", "lo")))

        norm_x, norm_h, norm_cq, norm_ckv, norm_y = (Norm(n) for n in ("x", "h", "cq", "ckv", "y"))
        fox_hi, fox_lo, mla_hi, mla_lo, qrope_ready, qrot_ready, v_turned, bank5_hi, bank7_hi, bank5_lo, bank7_lo = \
            sems("fox_hi", "fox_lo", "mla_hi", "mla_lo", "qrope_ready", "qrot_ready", "v_turned", "bank5_hi",
                 "bank7_hi", "bank5_lo", "bank7_lo")
        misc_copied, misc_turned, hT_turned, hT_read, diag_ready, wide_rstd, spread_ready, gained, second_scaled = sems(
            "misc_copied", "misc_turned", "hT_turned", "hT_read", "diag_ready", "wide_rstd", "spread_ready", "gained",
            "second_scaled")
        scores_done, shifted, expd, normed, p_turned, p_hi, p_lo, o_done, o_read = (
            sems(f"{n}_fox", f"{n}_mla") for n in
            ("scores_done", "shifted", "expd", "normed", "p_turned", "p_hi", "p_lo", "o_done", "o_read"))
        o_split_hi, o_split, merged, m_hi, m_lo = sems("o_split_hi", "o_split", "merged", "m_hi", "m_lo")
        taps_on, first_tap, th_ready, act_ready, a_hi, a_lo, y_ready = sems(
            "taps_on", "first_tap", "th_ready", "act_ready", "a_hi", "a_lo", "y_ready")

        block = ctx.enter_context(nc.Block())

        def tiled(w):
            return w[0].rearrange("(k p) n -> p k n", p=P)

        w_in_v, w_uq_v, w_ukv_v, w_pm_v, w_pf_v, w_out_v, w_fi_v, w_fo_v = (
            tiled(w) for w in (w_in, w_uq, w_ukv, w_proj_mla, w_proj_fox, w_out, w_ffn_in, w_ffn_out))

        @block.sync
        def _(sp):
            def load(phase, i, c, *parts):
                slot, freed = phase.slot(c), phase.freed(i, c)
                if freed is not None:
                    sp.wait_ge(lo_done, freed)
                k, n = parts[0].shape[1:]
                wide = len(parts) * n
                rows = raw[slot][:, 0:k * wide].rearrange("p (k n) -> p k n", k=k)
                for t, part in enumerate(parts):
                    sp.dma_start(rows[:, :, t * n:(t + 1) * n], part).then_inc(raw_landed[slot], 16)

            def load_proj(phase, i, c0, j):
                for c in range(4):
                    load(phase, i, c0 + c, *(w_in_v[:, 4 * c:4 * c + 4, bass.ds(j * HD + (COL_FQ + t * H * HD), HD)]
                                             for t in range(3)))
                if phase is PROJ0:
                    c0 += 1
                    slot, of_heads = phase.slot(4), w_uq_v.rearrange("p k (h n) -> p k h n", h=H)
                    sp.wait_ge(lo_done, phase.freed(0, 4))
                    for k in range(KR):
                        sp.dma_start(raw[slot][:, k * H * ROPE:(k + 1) * H * ROPE].rearrange("p (h n) -> p h n", h=H),
                                     of_heads[:, k, :, HD:HD + ROPE]).then_inc(raw_landed[slot], 16)
                load(phase, i, c0 + 4, w_ukv_v[:, :, bass.ds(j * (2 * HD), 2 * HD)])
                load(phase, i, c0 + 5, w_uq_v[:, :, bass.ds(j * (HD + ROPE), HD)])

            def load_gate(phase, i, c0, j):
                for c in range(4):
                    load(phase, i, c0 + c, w_in_v[:, 4 * c:4 * c + 4, bass.ds(j * 512 + COL_GATE, 512)])

            for b in range(NB):
                sp.dma_start(x_in[:, b, :], x[0, b * P:(b + 1) * P, :]).then_inc(x_landed[b], 16)
            row = 0
            for vec, n in ((norm_mix, KD), (norm_ffn, KD), (norm_q_a, KR), (norm_kv_a, KR)):
                sp.dma_start(gain_rows[row:row + n, :], vec[0].rearrange("(t p) -> t p", p=P)).then_inc(rows_landed, 16)
                row += n
            sp.dma_start(conv_rows[:, 0:3, :], w_conv[0].rearrange("a (t p) -> t a p", p=P)).then_inc(rows_landed, 16)
            sp.dma_start(conv_rows[:, 3, :], b_conv[0].rearrange("(t p) -> t p", p=P)).then_inc(rows_landed, 16)
            for c in range(4):
                load(LATENT, 0, c, w_in_v[:, 4 * c:4 * c + 4, COL_CQ:COL_CQ + RANK])
            for b in range(NB):
                sp.dma_start(pos_i[:, b:b + 1], positions[0, b * P:(b + 1) * P].unsqueeze(1)).then_inc(pos_landed, 16)
            sp.dma_start(bf[:, :], b_forget[0].partition_broadcast(P)).then_inc(bf_landed, 16)
            sp.wait_ge(lo_done, LATENT.freed(0, 4))
            misc = raw[LATENT.slot(4)][:, 0:2 * MISC_W].rearrange("p (k n) -> p k n", k=KD)
            for at0, col, n in ((0, COL_KROPE, ROPE), (ROPE, COL_F, H)):
                sp.dma_start(misc[:, :, at0:at0 + n], w_in_v[:, :, col:col + n]).then_inc(
                    raw_landed[LATENT.slot(4)], 16)
            for c in range(4):
                load(LATENT, 0, 5 + c, w_in_v[:, 4 * c:4 * c + 4, COL_CKV:COL_CKV + RANK])
            load_proj(PROJ0, 0, 0, 0)
            with sp.Fori(0, HEADS.trips) as i:
                for half in range(2):
                    c0 = half * len(HEAD_CHUNKS)
                    load_gate(HEADS, i, c0, i * 2 + half)
                    load_proj(HEADS, i, c0 + 4, i * 2 + (half + 1))
            load_gate(SEVENTH, 0, 0, H - 2)
            load_proj(SEVENTH, 0, 4, H - 1)
            load_gate(LAST, 0, 0, H - 1)
            with sp.Fori(0, MERGE.trips) as i:
                for c in range(4):
                    k0 = 4 * (c % 2)
                    load(MERGE, i, c, (w_pm_v, w_pf_v)[c // 2][:, k0:k0 + 4, bass.ds(i * 512, 512)])
            sp.wait_ge(o_read[1], H)
            sp.dma_start(x_again[:, :, :], x[0].rearrange("(b p) d -> p b d", p=P)).then_inc(x_again_landed, 16)
            with sp.Fori(0, OUT.trips) as i:
                for c in range(8):
                    k0 = 4 * (c % 4)
                    load(OUT, i, c, w_out_v[:, k0:k0 + 4, bass.ds(i * 1024 + c // 4 * 512, 512)])
            with sp.Fori(0, FFN_IN.trips) as i:
                for c in range(8):
                    k0 = 4 * (c % 4)
                    load(FFN_IN, i, c, *(w_fi_v[:, k0:k0 + 4, bass.ds(i * 512 + (t * FF + c // 4 * 256), 256)]
                                         for t in range(2)))
            for i in range(FFN_OUT.trips):
                for c in range(22):
                    k0 = 4 * (c % 11)
                    load(FFN_OUT, i, c, w_fo_v[:, k0:k0 + 4, bass.ds(i * 1024 + c // 11 * 512, 512)])
                    if i == 0 and c == 8:
                        sp.wait_ge(piece_used, FFN_IN.piece(FFN_IN.trips - 1, 15))
                        sp.dma_start(gain_final[:, :], norm_final.partition_broadcast(P)).then_inc(gain_landed, 16)
            for b in range(NB):
                sp.wait_ge((y_ready, second_scaled)[b], 1)
                sp.dma_start(y[0, b * P:(b + 1) * P, :], y_out[:, b, :]).then_inc(y_landed, 16)
            sp.wait_ge(y_landed, 16 * NB)

        @block.gpsimd
        def _(pool):
            nc.gpsimd.memset(ident[:, :], 0.0).then_inc(pool_chain, 1)
            nc.gpsimd.memset(upto[:, :], 1.0).then_inc(pool_chain, 1)
            nc.gpsimd.memset(mask[:, :], 0.0).then_inc(pool_chain, 1)
            nc.gpsimd.memset(ones[:, :], 1.0)
            pool.wait_ge(pool_chain, 3)
            nc.gpsimd.affine_select(out=ident[:, :], in_=ident[:, :], compare_op=ALU.not_equal, fill=1.0, base=0,
                                    pattern=[[-1, P]], channel_multiplier=1).then_inc(tables_built, 1)
            nc.gpsimd.affine_select(out=upto[:, 0:P], in_=upto[:, 0:P], compare_op=ALU.is_ge, fill=0.0, base=0,
                                    pattern=[[1, P]], channel_multiplier=-1).then_inc(tables_built, 1)
            for diagonal in (0, 2 * P):
                block_of = mask[:, diagonal:diagonal + P]
                nc.gpsimd.affine_select(out=block_of, in_=block_of, compare_op=ALU.is_ge, fill=MASKED, base=0,
                                        pattern=[[-1, P]], channel_multiplier=1).then_inc(tables_built, 1)
            for f in range(HALF):
                last = nc.gpsimd.memset(inv_freq[:, f:f + 1], float(np.float32(THETA ** (-2.0 * f / ROPE))))
            last.then_inc(tables_built, 1)

        def spread_bank(k):
            return bank[:, 4 + k % 4, 0:S]

        def panel_bank(n, t):
            return bank[:, 4 + n % 2 * 2 + t // 2, t % 2 * S:t % 2 * S + S]

        def latent_bank(first):
            return lambda k: bank[:, first + k // 2, k % 2 * S:k % 2 * S + S]

        @block.scalar
        def _(act):
            def split_hi(phase, i, p):
                c, n, s = p // 2, phase.widths[p // 2], phase.split_slot(p)
                if p % 2 == 0:
                    act.wait_ge(raw_landed[phase.slot(c)], phase.landed(i, c))
                if phase is not LATENT or p >= SPLIT_SLOTS:
                    act.wait_ge(piece_used, phase.piece(i, p - SPLIT_SLOTS))
                nc.scalar.activation(w_hi[s][:, 0:n], raw[phase.slot(c)][:, p % 2 * n:p % 2 * n + n],
                                     ACT.Copy).then_inc(hi_done, 1)

            def turned_hi(norm, source, gain, out, tiles, at_once=False):
                for k in tiles:
                    act.wait_ge(norm.turned, KR if at_once else k + 1)
                    nc.scalar.activation(out(k), source(k), ACT.Copy,
                                         scale=gain_T[:, gain + k:gain + k + 1]).then_inc(norm.hi, 1)

            def take_root(norm):
                act.wait_ge(norm.varied, 1)
                nc.scalar.activation(root[:, :], var[:, :], ACT.Sqrt).then_inc(norm.rooted, 1)

            def latent_squares(norm, first, done):
                act.wait_ge(piece_used, done)
                for b in range(NB):
                    nc.scalar.activation(junk[:, b * RANK:(b + 1) * RANK], bank[:, first + b, :], ACT.Square,
                                         accum_out=ss[:, b, 0:1]).then_inc(norm.squared, 1)

            for b in range(NB):
                act.wait_ge(x_landed[b], 16)
                if b:
                    act.wait_ge(norm_x.squared, b)
                nc.scalar.activation(junk[:, :], x_in[:, b, :], ACT.Square,
                                     accum_out=ss[:, b, 0:1]).then_inc(norm_x.squared, 1)
            take_root(norm_x)
            act.wait_ge(rows_read, 1)
            for p in range(2):
                split_hi(LATENT, 0, p)
            turned_hi(norm_x, spread_bank, 0, lambda k: xT_hi[:, k, :], range(4))
            for p in range(2, 4):
                split_hi(LATENT, 0, p)
            turned_hi(norm_x, spread_bank, 0, lambda k: xT_hi[:, k, :], range(*TILES_AT[3]))
            for p in range(4, 8):
                split_hi(LATENT, 0, p)
                turned_hi(norm_x, spread_bank, 0, lambda k: xT_hi[:, k, :], range(*TILES_AT[p]))
            act.wait_ge(angles_ready, 1)
            nc.scalar.activation(sin_t[:, :, :], redu[:, 0, :, :], ACT.Sin)
            nc.scalar.activation(cos_t[:, :, :], redu[:, 1, :, :], ACT.Sin).then_inc(tables_ready, 1)
            for p in range(8, 12):
                split_hi(LATENT, 0, p)
            latent_squares(norm_cq, 0, LATENT.piece(0, 7))
            take_root(norm_cq)
            for p in range(12, 14):
                split_hi(LATENT, 0, p)
            act.wait_ge(piece_used, LATENT.piece(0, 9))
            nc.scalar.activation(misc_T[:, :], bank[0:MISC, 4, 0:S], ACT.Copy).then_inc(misc_copied, 1)
            for p in range(14, 16):
                split_hi(LATENT, 0, p)
            turned_hi(norm_cq, latent_bank(6), 2 * KD, lambda k: cT_hi[:, 0, k, :], range(KR), at_once=True)
            act.wait_ge(f_abs, 1)
            nc.scalar.activation(zexp[:, :, :], zabs[:, :, :], ACT.Exp, scale=-1.0).then_inc(f_exp, 1)
            act.wait_ge(f_exp, 1)
            nc.scalar.activation(zln[:, :, :], zexp[:, :, :], ACT.Ln, bias=1.0).then_inc(f_exp, 1)
            for p in range(16, 18):
                split_hi(LATENT, 0, p)
            for p in range(2):
                split_hi(PROJ0, 0, p)
            act.wait_ge(kr_turned, 1)
            nc.scalar.activation(kr_hi[:, :], bank[0:ROPE, 6, 0:S], ACT.Copy).then_inc(kr_hi_ready, 1)
            for p in range(2, 4):
                split_hi(PROJ0, 0, p)
            latent_squares(norm_ckv, 2, LATENT.piece(0, 17))
            for p in range(4, 6):
                split_hi(PROJ0, 0, p)
            take_root(norm_ckv)
            for p in range(6, 10):
                split_hi(PROJ0, 0, p)
            turned_hi(norm_ckv, latent_bank(2), 2 * KD + KR, lambda k: cT_hi[:, 1, k, :], range(KR), at_once=True)
            for p in range(10, 14):
                split_hi(PROJ0, 0, p)

            def stage_fox_hi(projected):
                act.wait_ge(piece_used, projected)
                nc.scalar.activation(fqk_hi[:, :, :].rearrange("p a b -> p (a b)"), bank[:, 4, :], ACT.Copy)
                nc.scalar.activation(vT[0][:, :], bank[:, 5, 0:S], ACT.Copy).then_inc(fox_hi, 1)

            def exponentials(branch, n):
                act.wait_ge(shifted[branch], n)
                for b, cols in enumerate((slice(0, P), slice(P, SCORES))):
                    last = nc.scalar.activation(prob[branch][:, cols], prob[branch][:, cols], ACT.Exp,
                                                bias=top[:, branch, b:b + 1], accum_out=den[:, branch, b:b + 1])
                last.then_inc(expd[branch], 1)

            def one_head(phase, i, n, first):
                for p in range(2):
                    split_hi(phase, i, first + p)
                stage_fox_hi(phase.piece(i, first - 5))
                for p in range(2, 4):
                    split_hi(phase, i, first + p)
                act.wait_ge(piece_used, phase.piece(i, first - 1))
                nc.scalar.activation(mqk_hi[:, :, :].rearrange("p a b -> p (a b)"), bank[:, 6, :], ACT.Copy)
                nc.scalar.activation(vT[1][:, :], bank[:, 7, 0:S], ACT.Copy).then_inc(mla_hi, 1)
                split_hi(phase, i, first + 4)
                split_hi(phase, i, first + 5)
                act.wait_ge(v_turned, n)
                nc.scalar.activation(qr_hi[:, :], bank[0:ROPE, 5, S:2 * S], ACT.Copy)
                nc.scalar.activation(fv_hi[:, :, :].rearrange("p a b -> p (a b)"), bank[:, 5, 0:S],
                                     ACT.Copy).then_inc(bank5_hi, 1)
                nc.scalar.activation(mv_hi[:, :, :].rearrange("p a b -> p (a b)"), bank[:, 7, 0:S],
                                     ACT.Copy).then_inc(bank7_hi, 1)
                exponentials(0, n)
                split_hi(phase, i, first + 6)
                split_hi(phase, i, first + 7)
                exponentials(1, n)
                after, j, p0 = (MERGE, 0, 0) if phase is LAST else (phase, i, first + 8)
                split_hi(after, j, p0)
                split_hi(after, j, p0 + 1)
                for branch in range(2):
                    act.wait_ge(p_turned[branch], n)
                    nc.scalar.activation(pT_hi[branch][:, :], bank[:, 5 + 2 * branch, 0:SCORES],
                                         ACT.Copy).then_inc(p_hi[branch], 1)
                    split_hi(after, j, p0 + 2 + branch)
                if phase is LAST:
                    act.wait_ge(o_read[1], H - 1)
                    for group in O_GROUPS[:2]:
                        output_hi(*group)
                act.wait_ge(piece_used, phase.piece(i, first + 7))
                for b in range(2):
                    last = nc.scalar.activation(gates[:, bass.ds((n - 1) * 4 + 2 * b, 2), :].rearrange(
                        "p a b -> p (a b)"), bank[:, b, :], ACT.Tanh, scale=0.5)
                last.then_inc(pair_read[0], 1)
                if phase is not LAST:
                    for p in range(12, HEAD_PIECES):
                        split_hi(phase, i, first + p)

            def output_hi(branch, heads):
                nc.scalar.activation(oT_split[branch][0][:, heads, :], oT[:, branch, heads, :],
                                     ACT.Copy).then_inc(o_split_hi, 1)

            with act.Fori(0, HEADS.trips) as i:
                for half in range(2):
                    one_head(HEADS, i, i * 2 + (half + 1), half * HEAD_PIECES)
            one_head(SEVENTH, 0, H - 1, 0)
            one_head(LAST, 0, H, 0)

            act.wait_ge(o_read[1], H)
            for group in O_GROUPS[2:]:
                output_hi(*group)

            def merged_hi(n):
                act.wait_ge(merged, n)
                panel = bass.ds((n - 1) * 4, 4)
                nc.scalar.activation(mT_hi[:, panel, :], gates[:, panel, :], ACT.Copy, scale=0.5).then_inc(m_hi, 1)

            for p in range(4, 8):
                split_hi(MERGE, 0, p)
            with act.Fori(1, MERGE.trips) as i:
                for p in range(8):
                    split_hi(MERGE, i, p)
                    if p == 4:
                        merged_hi(i)

            def residual_squares(norm, pair, read, panel):
                squares = squares_h if norm is norm_h else squares_y
                act.wait_ge(pair_read[pair], read)
                for b in range(NB):
                    last = nc.scalar.activation(squares[:, pair, b, :],
                                                h[:, b, panel * 512:panel * 512 + 512], ACT.Square,
                                                accum_out=ss[:, b, panel:panel + 1])
                last.then_inc(norm.squared, 1)

            def take_hT(n):
                act.wait_ge(hT_turned, n + 1)
                for t in range(4):
                    k = 4 * n + t
                    last = nc.scalar.activation(hT[:, k, :], panel_bank(n, t), ACT.Copy,
                                                scale=gain_T[:, KD + k:KD + k + 1])
                last.then_inc(hT_read, 1)

            for i in range(OUT.trips):
                for p in range(16):
                    split_hi(OUT, i, p)
                    if i == 0 and p == 4:
                        merged_hi(MERGE.trips)
                    if i and p == 3:
                        residual_squares(norm_h, 1, READ_B[OUT] + i, 2 * i - 1)
                    if i and p == 5:
                        take_hT(1)
                    if p == 11:
                        residual_squares(norm_h, 0, READ_A[OUT] + i + 1, 2 * i)
                    if p == 13:
                        take_hT(2 * i)
            act.wait_ge(norm_h.squared, 3)
            nc.scalar.activation(root[:, 0:1], ss[:, 0, 0:1], ACT.Sqrt)
            for p in range(4):
                split_hi(FFN_IN, 0, p)
            residual_squares(norm_h, 1, READ_B[OUT] + 2, 3)
            take_hT(3)
            take_root(norm_h)
            act.wait_ge(wide_rstd, 1)
            nc.scalar.activation(rstd_wide[:, :], bank[:, 4, 0:S], ACT.Copy).then_inc(spread_ready, 1)

            def norm_pair_hi(q):
                act.wait_ge(norm_h.scaled, q + 1)
                nc.scalar.activation(xT_hi[:, 2 * q:2 * q + 2, :], hT[:, 2 * q:2 * q + 2, :],
                                     ACT.Copy).then_inc(norm_h.hi, 1)

            for q in range(4):
                norm_pair_hi(q)
            for q in range(4, 8):
                split_hi(FFN_IN, 0, q)
                norm_pair_hi(q)

            def hidden_panel(i, b, n, between):
                act.wait_ge(piece_used, FFN_IN.piece(i, 8 * b + 7))
                act.wait_ge(taps_on, n)
                for part in range(2):
                    for t in range(2):
                        last = nc.scalar.activation(hidden[:, part, t, :], bank[:, 2 * b + part, t * S:t * S + S],
                                                    ACT.Identity, bias=conv_now[:, b, 3, part, t:t + 1],
                                                    scale=conv_now[:, b, 2, part, t:t + 1])
                    last.then_inc(first_tap, 1)
                between(0)
                act.wait_ge(pair_read[b], i + (READ_A, READ_B)[b][FFN_IN] + 1)
                nc.scalar.activation(th[:, :, :], hidden[:, 0, :, :], ACT.Tanh, scale=0.5).then_inc(th_ready, 1)
                between(1)
                act.wait_ge(act_ready, n)
                nc.scalar.activation(aT_hi[:, bass.ds((n - 1) * 2, 2), :], hidden[:, 0, :, :], ACT.Copy,
                                     scale=0.5).then_inc(a_hi, 1)

            def ffn_in_body(i, first):
                if not first:
                    for p in range(4):
                        split_hi(FFN_IN, i, p)
                    hidden_panel(i - 1, 1, i * 2, lambda step: split_hi(FFN_IN, i, 4 + step))
                for p in range(8 if first else 6, 12):
                    split_hi(FFN_IN, i, p)
                hidden_panel(i, 0, i * 2 + 1, lambda step: split_hi(FFN_IN, i, 12 + step))
                split_hi(FFN_IN, i, 14)
                split_hi(FFN_IN, i, 15)

            ffn_in_body(0, True)
            with act.Fori(1, FFN_IN.trips) as i:
                ffn_in_body(i, False)

            for i in range(FFN_OUT.trips):
                for p in range(4):
                    split_hi(FFN_OUT, i, p)
                if i == 0:
                    hidden_panel(FFN_IN.trips - 1, 1, 2 * FFN_IN.trips, lambda step: split_hi(FFN_OUT, 0, 4 + step))
                else:
                    residual_squares(norm_y, 1, READ_B[FFN_OUT] + i, 2 * i - 1)
                    split_hi(FFN_OUT, i, 4)
                    split_hi(FFN_OUT, i, 5)
                for p in range(6, 44):
                    split_hi(FFN_OUT, i, p)
                    if p == 25:
                        residual_squares(norm_y, 0, READ_A[FFN_OUT] + i + 1, 2 * i)
            act.wait_ge(norm_y.squared, 3)
            nc.scalar.activation(root[:, 0:1], ss[:, 0, 0:1], ACT.Sqrt)
            residual_squares(norm_y, 1, READ_B[FFN_OUT] + 2, 3)
            take_root(norm_y)
            act.wait_ge(norm_y.scaled, 1)
            nc.scalar.activation(y_out[:, 1, :], y_out[:, 1, :], ACT.Copy, scale=rstd[:, 1:2]).then_inc(second_scaled, 1)

        @block.vector
        def _(dve):
            chain = Chain(dve, dve_chain)

            def split_lo(phase, i, p):
                c, n, s = p // 2, phase.widths[p // 2], phase.split_slot(p)
                dve.wait_ge(hi_done, phase.piece(i, p))
                nc.vector.tensor_tensor(w_lo[s][:, 0:n], raw[phase.slot(c)][:, p % 2 * n:p % 2 * n + n],
                                        w_hi[s][:, 0:n].bitcast(F32), ALU.subtract).then_inc(lo_done, 1)

            def reciprocal_root(norm, squares, panels, width, ready=None):
                dve.wait_ge(norm.squared, squares)
                source = ss[:, :, 0]
                if panels > 1:
                    chain.link(nc.vector.reduce_sum(newt[:, :], ss[:, :, 0:panels], AX.X))
                    source = newt[:, :]
                nc.vector.tensor_scalar(var[:, :], source, 1.0 / width, EPS, ALU.mult, ALU.add).then_inc(norm.varied, 1)
                dve.wait_ge(norm.rooted, 1)
                chain.link(nc.vector.reciprocal(rstd[:, :], root[:, :]))
                chain.link(nc.vector.scalar_tensor_tensor(out=newt[:, :], in0=rstd[:, :], scalar=-0.5,
                                                          in1=rstd[:, :], op0=ALU.mult, op1=ALU.mult))
                chain.link(nc.vector.tensor_tensor(newt[:, :], newt[:, :], var[:, :], ALU.mult))
                last = nc.vector.scalar_tensor_tensor(out=rstd[:, :], in0=newt[:, :], scalar=1.5, in1=rstd[:, :],
                                                      op0=ALU.add, op1=ALU.mult)
                if ready is None:
                    chain.link(last)
                else:
                    last.then_inc(ready, 1)
                    dve.wait_ge(ready, 1)

            def turned_lo(norm, source, gain, hi, lo, tiles, at_once=False):
                for k in tiles:
                    dve.wait_ge(norm.hi, KR if at_once else k + 1)
                    nc.vector.scalar_tensor_tensor(out=lo(k), in0=source(k), scalar=gain_T[:, gain + k:gain + k + 1],
                                                   in1=hi(k).bitcast(F32), op0=ALU.mult,
                                                   op1=ALU.subtract).then_inc(norm.lo, 1)

            def rotate(out, source, heads, read, n, ready):
                for b in range(NB):
                    pairs = source(b).rearrange("p (t f) -> p t f", f=HALF)
                    for table, product in ((cos_t, rot_a), (sin_t, rot_b)):
                        last = nc.vector.tensor_tensor(
                            product[:, b, 0:heads * ROPE].rearrange("p (t f) -> p t f", f=HALF), pairs,
                            table[:, b, :].unsqueeze(1).to_broadcast([P, 2 * heads, HALF]), ALU.mult)
                last.then_inc(read, 1)
                dve.wait_ge(read, n)
                for b in range(NB):
                    ac, bs = (t[:, b, 0:heads * ROPE].rearrange("p (h n) -> p h n", n=ROPE) for t in (rot_a, rot_b))
                    nc.vector.tensor_tensor(out(b)[:, :, 0:HALF], ac[:, :, 0:HALF], bs[:, :, HALF:ROPE], ALU.subtract)
                    last = nc.vector.tensor_tensor(out(b)[:, :, HALF:ROPE], ac[:, :, HALF:ROPE], bs[:, :, 0:HALF],
                                                   ALU.add)
                last.then_inc(ready, 1)

            dve.wait_ge(rows_turned, 1)
            nc.vector.tensor_copy(conv_T[:, :, :, :].rearrange("p a h t -> p (a h t)"), bank[:, 4, 0:8 * KF])
            nc.vector.tensor_copy(gain_T[:, :], bank[:, 4, 8 * KF:8 * KF + 2 * KD + 2 * KR]).then_inc(rows_read, 1)
            reciprocal_root(norm_x, NB, 1, D)
            for b in range(NB):
                nc.vector.tensor_scalar(x_in[:, b, :], x_in[:, b, :], rstd[:, b:b + 1], None,
                                        ALU.mult).then_inc(norm_x.scaled, 1)
            for p in range(2):
                split_lo(LATENT, 0, p)
            x_tiles = (norm_x, spread_bank, 0, lambda k: xT_hi[:, k, :], lambda k: xT_lo[:, k, :])
            turned_lo(*x_tiles, range(4))
            for p in range(2, 4):
                split_lo(LATENT, 0, p)
            turned_lo(*x_tiles, range(*TILES_AT[3]))
            for p in range(4, 8):
                split_lo(LATENT, 0, p)
                turned_lo(*x_tiles, range(*TILES_AT[p]))
            dve.wait_ge(pos_landed, 16 * NB)
            dve.wait_ge(tables_built, 5)
            chain.link(nc.vector.tensor_copy(pos[:, :], pos_i[:, :]))
            for b in range(NB):
                for t in range(2):
                    last = nc.vector.tensor_scalar(ang[:, t, b, :], inv_freq[:, :], pos[:, b:b + 1], None, ALU.mult)
            chain.link(last)
            for t in range(2):
                last = nc.vector.tensor_scalar(turns[:, t, :, :], ang[:, t, :, :], 1.0 / (2 * math.pi), 0.25 * t,
                                               ALU.mult, ALU.add)
            chain.link(last)
            to_whole = 1.5 * 2.0 ** 23
            for step in (to_whole, -to_whole):
                chain.link(nc.vector.tensor_scalar(turns[:, :, :, :], turns[:, :, :, :], step, None, ALU.add))
            rest, source = 2 * math.pi, ang
            for bits in (5, 13, 21, None):
                part = rest if bits is None else math.floor(rest * 2.0 ** bits) / 2.0 ** bits
                rest -= part
                chain.link(nc.vector.scalar_tensor_tensor(
                    out=redu[:, :, :, :].rearrange("p a b f -> p (a b f)"),
                    in0=turns[:, :, :, :].rearrange("p a b f -> p (a b f)"), scalar=-part,
                    in1=source[:, :, :, :].rearrange("p a b f -> p (a b f)"), op0=ALU.mult, op1=ALU.add))
                source = redu
            chain.link(nc.vector.tensor_scalar(redu[:, 1, :, :], redu[:, 1, :, :], math.pi / 2, None, ALU.add))
            limit = 3.1415925
            nc.vector.tensor_scalar(redu[:, :, :, :], redu[:, :, :, :], limit, -limit, ALU.min,
                                    ALU.max).then_inc(angles_ready, 1)
            for p in range(8, 12):
                split_lo(LATENT, 0, p)
            reciprocal_root(norm_cq, NB, 1, RANK)
            for b in range(NB):
                last = nc.vector.tensor_scalar(cq_n[:, b, :], bank[:, b, :], rstd[:, b:b + 1], None, ALU.mult)
            last.then_inc(pair_read[0], 1)
            for p in range(12, 16):
                split_lo(LATENT, 0, p)
            turned_lo(norm_cq, latent_bank(6), 2 * KD, lambda k: cT_hi[:, 0, k, :], lambda k: cT_lo[:, 0, k, :],
                      range(KR), at_once=True)
            dve.wait_ge(misc_turned, 1)
            dve.wait_ge(bf_landed, 16)
            dve.wait_ge(tables_ready, 1)

            def misc_of(b, cols):
                return bank[:, 5, b * MISC + cols.start:b * MISC + cols.stop]

            for b in range(NB):
                last = nc.vector.tensor_tensor(zf[:, b, :], misc_of(b, slice(ROPE, MISC)), bf[:, :], ALU.add)
            chain.link(last)
            nc.vector.scalar_tensor_tensor(out=zabs[:, :, :], in0=zf[:, :, :], scalar=-1.0, in1=zf[:, :, :],
                                           op0=ALU.mult, op1=ALU.max).then_inc(f_abs, 1)
            nc.vector.tensor_scalar(nlf[:, :, :], zf[:, :, :], -1.0, 0.0, ALU.mult, ALU.max)
            rotate(lambda b: k_rot[:, b:b + 1, :], lambda b: misc_of(b, slice(0, ROPE)), 1, misc_read, 1, krot_ready)
            split_lo(LATENT, 0, 16)
            split_lo(LATENT, 0, 17)
            dve.wait_ge(f_exp, 2)
            nc.vector.tensor_tensor(nlf[:, :, :], nlf[:, :, :], zln[:, :, :], ALU.add).then_inc(nlf_ready, 1)
            for p in range(2):
                split_lo(PROJ0, 0, p)
            dve.wait_ge(kr_hi_ready, 1)
            nc.vector.tensor_tensor(kr_lo[:, :], bank[0:ROPE, 6, 0:S], kr_hi[:, :].bitcast(F32),
                                    ALU.subtract).then_inc(kr_ready, 1)
            split_lo(PROJ0, 0, 2)
            dve.wait_ge(cumq_done, 1)
            nc.vector.tensor_scalar(cum_q[:, :, :].rearrange("p b h -> p (b h)"), bank[:, 7, 0:NB * H], -1.0, None,
                                    ALU.mult).then_inc(cumq_read, 1)

            def widen(head):
                nc.vector.tensor_copy(nlf_wide[:, :, :],
                                      nlf[:, :, head:head + 1].to_broadcast([P, NB, P])).then_inc(wide_ready, 1)

            widen(0)
            split_lo(PROJ0, 0, 3)
            for head in range(H):
                split_lo(PROJ0, 0, 4 + head)
                dve.wait_ge(decay_done, head + 1)
                if head + 1 < H:
                    widen(head + 1)
                nc.vector.tensor_copy(decay[:, head, :], bank[:, 6 + head % 2, 0:S]).then_inc(decay_read, 1)
                if head == 1:
                    reciprocal_root(norm_ckv, NB, 1, RANK)
                    for b in range(NB):
                        last = nc.vector.tensor_scalar(ckv_n[:, b, :], bank[:, 2 + b, :], rstd[:, b:b + 1], None,
                                                       ALU.mult)
                    last.then_inc(pair_read[1], 1)
                if head == 5:
                    turned_lo(norm_ckv, latent_bank(2), 2 * KD + KR, lambda k: cT_hi[:, 1, k, :],
                              lambda k: cT_lo[:, 1, k, :], range(KR), at_once=True)
            split_lo(PROJ0, 0, 12)
            split_lo(PROJ0, 0, 13)
            dve.wait_ge(piece_used, PROJ0.piece(0, 9))
            rotate(lambda b: q_rot_all[:, b, :, :], lambda b: bank[:, 2 + b, :], H, misc_read, 2, qrope_ready)
            dve.wait_ge(qrope_ready, 1)

            def lo_of(hi, lo, source):
                return nc.vector.tensor_tensor(lo[:, :, :].rearrange("p a b -> p (a b)"), source,
                                               hi[:, :, :].rearrange("p a b -> p (a b)").bitcast(F32), ALU.subtract)

            def stage_fox_lo(n):
                dve.wait_ge(fox_hi, n)
                lo_of(fqk_hi, fqk_lo, bank[:, 4, :]).then_inc(fox_lo, 1)

            before_heads, HEAD_STEPS = chain.n, 8

            def shift(branch, n, scale, bias):
                dve.wait_ge(scores_done[branch], n)
                chain.link(nc.vector.scalar_tensor_tensor(
                    out=prob[branch][:, :], in0=bank[:, 4 + 2 * branch, 0:SCORES], scalar=scale, in1=bias[:, :],
                    op0=ALU.mult, op1=ALU.add))
                nc.vector.reduce_max(top[:, branch, 0:1], prob[branch][:, 0:P], AX.X)
                chain.link(nc.vector.reduce_max(top[:, branch, 1:2], prob[branch][:, P:SCORES], AX.X))
                nc.vector.tensor_scalar(top[:, branch, :], top[:, branch, :], -1.0, None,
                                        ALU.mult).then_inc(shifted[branch], 1)

            def normalise(branch, n):
                dve.wait_ge(expd[branch], n)
                chain.link(nc.vector.reciprocal(rden[:, branch, :], den[:, branch, :]))
                for b, cols in enumerate((slice(0, P), slice(P, SCORES))):
                    last = nc.vector.tensor_scalar(prob[branch][:, cols], prob[branch][:, cols],
                                                   rden[:, branch, b:b + 1], None, ALU.mult)
                last.then_inc(normed[branch], 1)

            def one_head(phase, i, n, first):
                chain.body(n - 1, HEAD_STEPS, before_heads)
                for p in range(2):
                    split_lo(phase, i, first + p)
                stage_fox_lo(n)
                for p in range(2, 4):
                    split_lo(phase, i, first + p)
                nc.vector.tensor_copy(q_rot[:, :, :], q_rot_all[:, :, bass.ds(n - 1, 1), :].rearrange(
                    "p b h n -> p b (h n)")).then_inc(qrot_ready, 1)
                chain.link(nc.vector.tensor_copy(cum_now[:, :], cum_q[:, :, bass.ds(n - 1, 1)]))
                for b, cols in enumerate((slice(0, P), slice(P, SCORES))):
                    last = nc.vector.scalar_tensor_tensor(
                        out=fox_bias[:, cols], in0=decay[:, bass.ds(n - 1, 1), 0:P * (b + 1)],
                        scalar=cum_now[:, b:b + 1], in1=mask[:, cols], op0=ALU.add, op1=ALU.add)
                chain.done(last)
                dve.wait_ge(mla_hi, n)
                lo_of(mqk_hi, mqk_lo, bank[:, 6, :]).then_inc(mla_lo, 1)
                split_lo(phase, i, first + 4)
                split_lo(phase, i, first + 5)
                dve.wait_ge(bank5_hi, n)
                nc.vector.tensor_tensor(qr_lo[:, :], bank[0:ROPE, 5, S:2 * S], qr_hi[:, :].bitcast(F32), ALU.subtract)
                lo_of(fv_hi, fv_lo, bank[:, 5, 0:S]).then_inc(bank5_lo, 1)
                dve.wait_ge(bank7_hi, n)
                lo_of(mv_hi, mv_lo, bank[:, 7, 0:S]).then_inc(bank7_lo, 1)
                chain.wait()
                shift(0, n, FOX_SCALE, fox_bias)
                split_lo(phase, i, first + 6)
                normalise(0, n)
                split_lo(phase, i, first + 7)
                shift(1, n, MLA_SCALE, mask)
                after, j, p0 = (MERGE, 0, 0) if phase is LAST else (phase, i, first + 8)
                split_lo(after, j, p0)
                normalise(1, n)
                split_lo(after, j, p0 + 1)
                for branch in range(2):
                    dve.wait_ge(p_hi[branch], n)
                    nc.vector.tensor_tensor(pT_lo[branch][:, :], bank[:, 5 + 2 * branch, 0:SCORES],
                                            pT_hi[branch][:, :].bitcast(F32), ALU.subtract).then_inc(p_lo[branch], 1)
                    split_lo(after, j, p0 + 2 + branch)
                if phase is LAST:
                    for done, group in enumerate(O_GROUPS[:2]):
                        output_lo(*group, done + 1)
                for branch in range(2):
                    dve.wait_ge(o_done[branch], n)
                    nc.vector.tensor_copy(oT[:, branch, bass.ds(n - 1, 1), :],
                                          bank[:, 6 + branch, 0:S]).then_inc(o_read[branch], 1)
                if phase is not LAST:
                    for p in range(12, HEAD_PIECES):
                        split_lo(phase, i, first + p)
                assert chain.n == HEAD_STEPS, chain.n

            def output_lo(branch, heads, done):
                dve.wait_ge(o_split_hi, done)
                nc.vector.tensor_tensor(oT_split[branch][1][:, heads, :], oT[:, branch, heads, :],
                                        oT_split[branch][0][:, heads, :].bitcast(F32), ALU.subtract).then_inc(o_split, 1)

            with dve.Fori(0, HEADS.trips) as i:
                for half in range(2):
                    one_head(HEADS, i, i * 2 + (half + 1), half * HEAD_PIECES)
            one_head(SEVENTH, 0, H - 1, 0)
            one_head(LAST, 0, H, 0)
            chain.body(0, 0, before_heads + H * HEAD_STEPS)

            for done, group in enumerate(O_GROUPS[2:]):
                output_lo(*group, done + 3)

            def panel_of(n, first):
                return (slice(None), bass.ds((n - 1) * 4 + first, 4), slice(None))

            def weigh(pair, first, n, done):
                dve.wait_ge(piece_used, done)
                for b in range(2):
                    g = gates[:, bass.ds((n - 1) * 4 + first + 2 * b, 2), :].rearrange("p a b -> p (a b)")
                    last = nc.vector.scalar_tensor_tensor(out=g, in0=g, scalar=1.0, in1=bank[:, 2 * pair + b, :],
                                                          op0=ALU.add, op1=ALU.mult)
                last.then_inc(pair_read[pair], 1)

            def merge_panel(n, done, between):
                weigh(1, KD, n, done)
                dve.wait_ge(pair_read[1], READ_B[MERGE] + n)
                nc.vector.tensor_tensor(gates[panel_of(n, 0)], gates[panel_of(n, 0)], gates[panel_of(n, KD)],
                                        ALU.add).then_inc(merged, 1)
                between()
                dve.wait_ge(m_hi, n)
                nc.vector.scalar_tensor_tensor(out=mT_lo[panel_of(n, 0)], in0=gates[panel_of(n, 0)], scalar=0.5,
                                               in1=mT_hi[panel_of(n, 0)].bitcast(F32), op0=ALU.mult,
                                               op1=ALU.subtract).then_inc(m_lo, 1)

            for p in range(4, 8):
                split_lo(MERGE, 0, p)
            weigh(0, 0, 1, MERGE.piece(0, 3))
            with dve.Fori(1, MERGE.trips) as i:
                for p in range(4):
                    split_lo(MERGE, i, p)
                merge_panel(i, MERGE.piece(i - 1, 7), lambda: split_lo(MERGE, i, 4))
                for p in range(5, 8):
                    split_lo(MERGE, i, p)
                weigh(0, 0, i + 1, MERGE.piece(i, 3))

            def add_residual(pair, done, source, panel):
                dve.wait_ge(piece_used, done)
                cols = slice(panel * 512, panel * 512 + 512)
                for b in range(NB):
                    last = nc.vector.tensor_tensor(h[:, b, cols], bank[:, 2 * pair + b, :], source[:, b, cols], ALU.add)
                last.then_inc(pair_read[pair], 1)

            for i in range(OUT.trips):
                for p in range(16):
                    if i == 0 and p == 4:
                        merge_panel(MERGE.trips, MERGE.piece(MERGE.trips - 1, 7), lambda: split_lo(OUT, 0, 4))
                        dve.wait_ge(x_again_landed, 16)
                    else:
                        split_lo(OUT, i, p)
                    if i and p == 3:
                        add_residual(1, OUT.piece(i - 1, 15), x_again, 2 * i - 1)
                    if p == 11:
                        add_residual(0, OUT.piece(i, 7), x_again, 2 * i)
            for p in range(4):
                split_lo(FFN_IN, 0, p)
            add_residual(1, OUT.piece(1, 15), x_again, 3)
            reciprocal_root(norm_h, 4, 4, D)
            for b in range(NB):
                last = nc.vector.tensor_scalar(rstd_diag[:, b, :], ident[:, :], rstd[:, b:b + 1], None, ALU.mult)
            last.then_inc(diag_ready, 1)
            dve.wait_ge(hT_read, 4)
            dve.wait_ge(spread_ready, 1)

            def norm_pair(q):
                pair = hT[:, 2 * q:2 * q + 2, :]
                nc.vector.tensor_tensor(pair, pair, rstd_wide[:, :].unsqueeze(1).to_broadcast([P, 2, S]),
                                        ALU.mult).then_inc(norm_h.scaled, 1)

            def norm_pair_lo(q):
                dve.wait_ge(norm_h.hi, q + 1)
                nc.vector.tensor_tensor(xT_lo[:, 2 * q:2 * q + 2, :], hT[:, 2 * q:2 * q + 2, :],
                                        xT_hi[:, 2 * q:2 * q + 2, :].bitcast(F32), ALU.subtract).then_inc(norm_h.lo, 1)

            norm_pair(0)
            for q in range(4):
                norm_pair(q + 1)
                norm_pair_lo(q)
            for q in range(4, 8):
                split_lo(FFN_IN, 0, q)
                if q < 7:
                    norm_pair(q + 1)
                norm_pair_lo(q)
            before_ffn, PANEL_STEPS = chain.base + chain.n, 3

            def hidden_panel(i, b, n, between):
                chain.body(n - 1, PANEL_STEPS, before_ffn)
                nc.vector.tensor_copy(conv_now[:, b, :, :, :],
                                      conv_T[:, :, :, bass.ds((n - 1) * 2, 2)]).then_inc(taps_on, 1)
                for part in range(2):
                    dve.wait_ge(first_tap, (n - 1) * 2 + (part + 1))
                    for back in (1, 2):
                        for t in range(2):
                            out = hidden[:, part, t, back:S]
                            last = nc.vector.scalar_tensor_tensor(
                                out=out, in0=bank[:, 2 * b + part, t * S:t * S + S - back],
                                scalar=conv_now[:, b, 2 - back, part, t:t + 1], in1=out, op0=ALU.mult, op1=ALU.add)
                        if back == 1:
                            chain.link(last)
                last.then_inc(pair_read[b], 1)
                between(0)
                dve.wait_ge(th_ready, n)
                chain.link(nc.vector.scalar_tensor_tensor(out=hidden[:, 0, :, :], in0=th[:, :, :], scalar=1.0,
                                                          in1=hidden[:, 0, :, :], op0=ALU.add, op1=ALU.mult))
                nc.vector.tensor_tensor(hidden[:, 0, :, :], hidden[:, 0, :, :], hidden[:, 1, :, :],
                                        ALU.mult).then_inc(act_ready, 1)
                between(1)
                dve.wait_ge(a_hi, n)
                tiles = bass.ds((n - 1) * 2, 2)
                nc.vector.scalar_tensor_tensor(out=aT_lo[:, tiles, :], in0=hidden[:, 0, :, :], scalar=0.5,
                                               in1=aT_hi[:, tiles, :].bitcast(F32), op0=ALU.mult,
                                               op1=ALU.subtract).then_inc(a_lo, 1)
                assert chain.n == PANEL_STEPS

            def ffn_in_body(i, first):
                if not first:
                    for p in range(4):
                        split_lo(FFN_IN, i, p)
                    hidden_panel(i - 1, 1, i * 2, lambda step: split_lo(FFN_IN, i, 4 + step))
                for p in range(8 if first else 6, 12):
                    split_lo(FFN_IN, i, p)
                hidden_panel(i, 0, i * 2 + 1, lambda step: split_lo(FFN_IN, i, 12 + step))
                split_lo(FFN_IN, i, 14)
                split_lo(FFN_IN, i, 15)

            ffn_in_body(0, True)
            with dve.Fori(1, FFN_IN.trips) as i:
                ffn_in_body(i, False)

            def gain_panel(pair, panel):
                dve.wait_ge(pair_read[pair], (READ_A, READ_B)[pair][FFN_OUT] + panel // 2 + 1)
                cols = slice(panel * 512, panel * 512 + 512)
                for b in range(NB):
                    last = nc.vector.tensor_tensor(y_out[:, b, cols], h[:, b, cols], gain_final[:, cols], ALU.mult)
                last.then_inc(gained, 1)

            for i in range(FFN_OUT.trips):
                for p in range(4):
                    split_lo(FFN_OUT, i, p)
                if i == 0:
                    hidden_panel(FFN_IN.trips - 1, 1, 2 * FFN_IN.trips, lambda step: split_lo(FFN_OUT, 0, 4 + step))
                    chain.body(0, 0, before_ffn + 2 * FFN_IN.trips * PANEL_STEPS)
                else:
                    add_residual(1, FFN_OUT.piece(i - 1, 43), h, 2 * i - 1)
                    split_lo(FFN_OUT, i, 4)
                    split_lo(FFN_OUT, i, 5)
                    dve.wait_ge(gain_landed, 16)
                    gain_panel(0, 0)
                for p in range(6, 44):
                    split_lo(FFN_OUT, i, p)
                    if i and p == 8:
                        gain_panel(1, 1)
                    if p == 25:
                        add_residual(0, FFN_OUT.piece(i, 21), h, 2 * i)
                    if i and p == 27:
                        gain_panel(0, 2)
            add_residual(1, FFN_OUT.piece(1, 43), h, 3)
            gain_panel(1, 3)
            reciprocal_root(norm_y, 4, 4, D, norm_y.scaled)
            nc.vector.tensor_scalar(y_out[:, 0, :], y_out[:, 0, :], rstd[:, 0:1], None, ALU.mult).then_inc(y_ready, 1)

        @block.tensor
        def _(pe):
            def mm(out, still, moving, start, stop):
                return nc.tensor.matmul(out, still, moving, start=start, stop=stop, skip_group_check=True)

            def product(out, still, moving, start, stop):
                mm(out, still[0], moving[0], start, False)
                mm(out, still[0], moving[1], False, False)
                return mm(out, still[1], moving[0], False, stop)

            def weights(phase, p, col, n):
                s = phase.split_slot(p)
                return w_hi[s][:, col:col + n], w_lo[s][:, col:col + n]

            def piece(phase, i, p, products):
                pe.wait_ge(lo_done, phase.piece(i, p))
                products().then_inc(piece_used, 1)

            def still_tiles(phase, p, k0, tiles, wide, outs, xk, k_last):
                def run():
                    for kk in range(2):
                        k = k0 + kk
                        for t in range(tiles):
                            last = product(outs(t), weights(phase, p, kk * wide + t * P, P), xk(k),
                                           k == 0 and t % 2 == 0, k == k_last)
                    return last
                return run

            def moving_tiles(phase, p, k0, wide, outs, xk, k_last):
                def run():
                    for kk in range(2):
                        k = k0 + kk
                        for b in range(NB):
                            hi, lo = xk(k)
                            last = product(outs(b), (hi[:, b * P:(b + 1) * P], lo[:, b * P:(b + 1) * P]),
                                           weights(phase, p, kk * wide, wide), k == 0, k == k_last)
                    return last
                return run

            def xk(k):
                return xT_hi[:, k, :], xT_lo[:, k, :]

            def turn(norm, source, target, tiles):
                for k in tiles:
                    if k >= 4:
                        pe.wait_ge(norm.lo, k - 3)
                    for b in range(NB):
                        last = nc.tensor.transpose(target(k)[:, b * P:(b + 1) * P], source[:, b, k * P:(k + 1) * P],
                                                   ident[:, :])
                    last.then_inc(norm.turned, 1)

            pe.wait_ge(tables_built, 5)
            pe.wait_ge(rows_landed, 6 * 16)
            for a in range(4):
                nc.tensor.transpose(bank[:, 4, a * 2 * KF:(a + 1) * 2 * KF], conv_rows[:, a, :], ident[0:2 * KF, 0:2 * KF])
            n_rows = 2 * KD + 2 * KR
            nc.tensor.transpose(bank[:, 4, 8 * KF:8 * KF + n_rows], gain_rows[:, :],
                                ident[0:n_rows, 0:n_rows]).then_inc(rows_turned, 1)
            pe.wait_ge(rows_read, 1)
            pe.wait_ge(norm_x.scaled, NB)
            turn(norm_x, x_in, spread_bank, range(4))
            for p in range(8):
                pe.wait_ge(norm_x.lo, 2 * p + 2)
                piece(LATENT, 0, p, moving_tiles(LATENT, p, 2 * p, RANK, lambda b: bank[:, b, :], xk, KD - 1))
                if 2 * p + 4 < KD:
                    turn(norm_x, x_in, spread_bank, range(2 * p + 4, 2 * p + 6))
            for p in range(8, 10):
                def run():
                    for kk in range(8):
                        k = 8 * (p - 8) + kk
                        last = product(bank[0:MISC, 4, 0:S], weights(LATENT, p, kk * MISC, MISC), xk(k), k == 0,
                                       k == KD - 1)
                    return last
                piece(LATENT, 0, p, run)
            for p in range(10, 18):
                piece(LATENT, 0, p, moving_tiles(LATENT, p, 2 * (p - 10), RANK, lambda b: bank[:, 2 + b, :], xk, KD - 1))
                if p == 12:
                    pe.wait_ge(misc_copied, 1)
                    for b in range(NB):
                        last = nc.tensor.transpose(bank[:, 5, b * MISC:(b + 1) * MISC], misc_T[:, b * P:(b + 1) * P],
                                                   ident[0:MISC, 0:MISC])
                    last.then_inc(misc_turned, 1)
                    pe.wait_ge(pair_read[0], 1)
                    turn(norm_cq, cq_n, latent_bank(6), range(KR))
                if p == 15:
                    pe.wait_ge(norm_cq.lo, KR)
                    pe.wait_ge(krot_ready, 1)
                    for b in range(NB):
                        last = nc.tensor.transpose(bank[0:ROPE, 6, b * P:(b + 1) * P], k_rot[:, b, :], ident[:, :])
                    last.then_inc(kr_turned, 1)
                if p == 16:
                    pe.wait_ge(nlf_ready, 1)
                    nc.tensor.matmul(bank[:, 7, 0:H], upto[:, 0:P], nlf[:, 0, :], start=True, stop=True)
                    nc.tensor.matmul(bank[:, 7, H:2 * H], upto[:, P:S], nlf[:, 0, :], start=True, stop=False)
                    nc.tensor.matmul(bank[:, 7, H:2 * H], upto[:, 0:P], nlf[:, 1, :], start=False,
                                     stop=True).then_inc(cumq_done, 1)
            def project_fox(phase, i, p0, after=lambda p: None):
                for q in range(8):
                    piece(phase, i, p0 + q, still_tiles(phase, p0 + q, 2 * q, 3, 3 * HD,
                                                        lambda t: bank[:, 4 + t // 2, t % 2 * S:t % 2 * S + S], xk, KD - 1))
                    after(q)

            def latent(which):
                return lambda k: (cT_hi[:, which, k, :], cT_lo[:, which, k, :])

            def project_mla(phase, i, p0):
                for q in range(2):
                    def run():
                        for kk in range(2):
                            k = 2 * q + kk
                            product(bank[:, 6, 0:S], weights(phase, p0 + q, kk * 2 * HD, HD), latent(1)(k), k == 0,
                                    k == KR - 1)
                            last = product(bank[:, 7, 0:S], weights(phase, p0 + q, kk * 2 * HD + HD, HD), latent(1)(k),
                                           k == 0, k == KR - 1)
                        return last
                    piece(phase, i, p0 + q, run)
                for q in range(2):
                    def run():
                        for kk in range(2):
                            k = 2 * q + kk
                            last = product(bank[:, 6, S:2 * S], weights(phase, p0 + 2 + q, kk * HD, HD), latent(0)(k),
                                           False, k == KR - 1)
                        return last
                    piece(phase, i, p0 + 2 + q, run)

            def decay_of(head):
                pe.wait_ge(wide_ready, head + 1)
                if head >= 2:
                    pe.wait_ge(decay_read, head - 1)
                else:
                    pe.wait_ge((kr_ready, cumq_read)[head], 1)
                out = bank[:, 6 + head % 2, 0:S]
                nc.tensor.matmul(out, nlf_wide[:, 0, :], upto[:, :], start=True, stop=False)
                nc.tensor.matmul(out[:, P:S], nlf_wide[:, 1, :], upto[:, 0:P], start=False,
                                 stop=True).then_inc(decay_done, 1)
                if head == 5:
                    pe.wait_ge(pair_read[1], 1)
                    turn(norm_ckv, ckv_n, latent_bank(2), range(KR))

            pe.wait_ge(misc_read, 1)
            project_fox(PROJ0, 0, 0, decay_of)
            pe.wait_ge(norm_ckv.lo, KR)
            for p in range(8, 10):
                piece(PROJ0, 0, p, moving_tiles(PROJ0, p, 2 * (p - 8), H * ROPE, lambda b: bank[:, 2 + b, :], latent(0),
                                                KR - 1))
            pe.wait_ge(decay_read, H)
            project_mla(PROJ0, 0, 10)

            def scores(branch, n, qk_hi, qk_lo, rotary, q_at=0):
                for b in range(NB):
                    out = bank[:, 4 + 2 * branch, b * P:b * P + (b + 1) * P]
                    qs, ks = slice(b * P, (b + 1) * P), slice(0, (b + 1) * P)
                    last = product(out, (qk_hi[:, q_at, qs], qk_lo[:, q_at, qs]),
                                   (qk_hi[:, 1 - q_at, ks], qk_lo[:, 1 - q_at, ks]), True, not rotary)
                    if rotary:
                        last = product(out, (qr_hi[:, qs], qr_lo[:, qs]), (kr_hi[:, ks], kr_lo[:, ks]), False, True)
                last.then_inc(scores_done[branch], 1)

            def turn_probabilities(branch, n):
                pe.wait_ge(normed[branch], n)
                for blk in range(3):
                    last = nc.tensor.transpose(bank[:, 5 + 2 * branch, blk * P:(blk + 1) * P],
                                               prob[branch][:, blk * P:(blk + 1) * P], ident[:, :])
                last.then_inc(p_turned[branch], 1)

            def outputs(branch, n, v_hi, v_lo):
                pe.wait_ge(p_lo[branch], n)
                out = bank[:, 6 + branch, 0:S]
                product(out, (v_hi[:, 0, :], v_lo[:, 0, :]), (pT_hi[branch][:, 0:S], pT_lo[branch][:, 0:S]), True, False)
                product(out[:, P:S], (v_hi[:, 1, :], v_lo[:, 1, :]),
                        (pT_hi[branch][:, S:SCORES], pT_lo[branch][:, S:SCORES]), False, True).then_inc(o_done[branch], 1)

            def one_head(phase, i, n, first):
                pe.wait_ge(pair_read[0], n)
                for p in range(8):
                    piece(phase, i, first + p, still_tiles(phase, first + p, 2 * p, 4, 4 * P,
                                                   lambda t: bank[:, t // 2, t % 2 * S:t % 2 * S + S], xk, KD - 1))
                    if p == 1:
                        pe.wait_ge(qrot_ready, n)
                        pe.wait_ge(mla_hi, n)
                        pe.wait_ge(fox_lo, n)
                        scores(0, n, fqk_hi, fqk_lo, False)
                        for b in range(NB):
                            cols = slice(b * P, (b + 1) * P)
                            nc.tensor.transpose(bank[:, 5, cols], vT[0][:, cols], ident[:, :])
                            nc.tensor.transpose(bank[:, 7, cols], vT[1][:, cols], ident[:, :])
                            last = nc.tensor.transpose(bank[0:ROPE, 5, S + b * P:S + (b + 1) * P], q_rot[:, b, :],
                                                       ident[:, :])
                        last.then_inc(v_turned, 1)
                    if p == 3:
                        pe.wait_ge(mla_lo, n)
                        pe.wait_ge(bank5_lo, n)
                        scores(1, n, mqk_hi, mqk_lo, True, q_at=1)
                    if p == 5:
                        pe.wait_ge(bank7_lo, n)
                        turn_probabilities(0, n)
                    if p == 6:
                        turn_probabilities(1, n)
                outputs(0, n, fv_hi, fv_lo)
                outputs(1, n, mv_hi, mv_lo)
                if phase is not LAST:
                    project_fox(phase, i, first + 8)
                    pe.wait_ge(o_read[0], n)
                    pe.wait_ge(o_read[1], n)
                    project_mla(phase, i, first + 16)

            with pe.Fori(0, HEADS.trips) as i:
                for half in range(2):
                    one_head(HEADS, i, i * 2 + (half + 1), half * HEAD_PIECES)
            one_head(SEVENTH, 0, H - 1, 0)
            one_head(LAST, 0, H, 0)

            def bank_of(pair):
                return lambda t: bank[:, 2 * pair + t // 2, t % 2 * S:t % 2 * S + S]

            with pe.Fori(0, MERGE.trips) as i:
                for p in range(8):
                    pair, q = p // 4, p % 4
                    if q == 0:
                        pe.wait_ge(pair_read[pair], i + (READ_A, READ_B)[pair][MERGE])
                    pe.wait_ge(o_split, GROUPS_READ[p])
                    piece(MERGE, i, p, still_tiles(
                        MERGE, p, 2 * q, 4, 4 * P, bank_of(pair),
                        lambda k: tuple(part[:, k, :] for part in oT_split[1 - pair]), H - 1))

            def moving_panels(phase, i, per_panel, activation, ready, k_last, after=lambda i, p: None):
                for p in range(2 * per_panel):
                    pair, q = p // per_panel, p % per_panel
                    if q == 0:
                        pe.wait_ge(pair_read[pair], i + (READ_A, READ_B)[pair][phase])
                    pe.wait_ge(*ready(q))
                    piece(phase, i, p, moving_tiles(phase, p, 2 * q, 512, lambda b: bank[:, 2 * pair + b, :],
                                                    activation, k_last))
                    after(i, p)

            def turn_residual(n):
                pe.wait_ge(pair_read[n % 2], (READ_A, READ_B)[n % 2][OUT] + n // 2 + 1)
                if n >= 2:
                    pe.wait_ge(hT_read, n - 1)
                for t in range(4):
                    k = 4 * n + t
                    for b in range(NB):
                        last = nc.tensor.transpose(panel_bank(n, t)[:, b * P:(b + 1) * P], h[:, b, k * P:(k + 1) * P],
                                                   ident[:, :])
                last.then_inc(hT_turned, 1)

            def residual_beside(i, p):
                if i and p == 1:
                    turn_residual(1)
                if p == 10:
                    turn_residual(2 * i)

            for i in range(OUT.trips):
                moving_panels(OUT, i, 8, lambda k: (mT_hi[:, k, :], mT_lo[:, k, :]), lambda q: (m_lo, q // 2 + 1),
                              KD - 1, residual_beside)
            turn_residual(3)
            pe.wait_ge(diag_ready, 1)
            pe.wait_ge(hT_read, 3)
            for b in range(NB):
                last = nc.tensor.matmul(bank[:, 4, b * P:(b + 1) * P], ones[:, :], rstd_diag[:, b, :], start=True,
                                        stop=True)
            last.then_inc(wide_rstd, 1)
            with pe.Fori(0, FFN_IN.trips) as i:
                for p in range(16):
                    pair, q = p // 8, p % 8
                    if q == 0:
                        pe.wait_ge(pair_read[pair], i + (READ_A, READ_B)[pair][FFN_IN])
                    if pair == 0:
                        pe.wait_ge(norm_h.lo, q + 1)
                    piece(FFN_IN, i, p, still_tiles(FFN_IN, p, 2 * q, 4, 4 * P, bank_of(pair), xk, KD - 1))
            with pe.Fori(0, FFN_OUT.trips) as i:
                moving_panels(FFN_OUT, i, 22, lambda k: (aT_hi[:, k, :], aT_lo[:, k, :]), lambda q: (a_lo, q + 1), KF - 1)


NAMES = ["x", "positions", "norm_mix", "w_in", "b_forget", "norm_q_a", "w_uq", "norm_kv_a", "w_ukv", "w_proj_mla",
         "w_proj_fox", "w_out", "norm_ffn", "w_ffn_in", "w_conv", "b_conv", "w_ffn_out", "norm_final"]


def kernel(**inputs):
    import concourse.bacc as bacc
    from concourse.bass_utils import run_bass_kernel_spmd

    nc = bacc.Bacc("TRN2", target_bir_lowering=False, num_devices=1)
    arrays, args = {}, []
    for name in NAMES:
        a = np.ascontiguousarray(inputs[name])
        arrays[name] = a
        args.append(nc.dram_tensor(name, a.shape, mybir.dt.from_np(a.dtype), kind="ExternalInput").ap())
    y = nc.dram_tensor("y", (1, S, D), mybir.dt.float32, kind="ExternalOutput").ap()
    hybrid_layer(nc, *args, y)
    result = run_bass_kernel_spmd(nc, [arrays], core_ids=[0])
    return result.results[0]["y"]
```

```python
import math
from contextlib import ExitStack

import numpy as np
import concourse.bass as bass
from concourse import mybir
from concourse.alu_op_type import AluOpType as ALU

P = 128
S = 256
D = 2048
NB = S // P
KD = D // P
RANK = 512
KR = RANK // P
H = 8
HD = 128
ROPE = 64
HALF = ROPE // 2
FF = 5632
KF = FF // P
EPS = 1e-6
THETA = 10000.0
MASKED = -3.0e38
MLA_SCALE = float((HD + ROPE) ** -0.5)
FOX_SCALE = float(HD ** -0.5)

COL_CQ, COL_CKV, COL_KROPE = 0, RANK, 2 * RANK
COL_FQ = COL_KROPE + ROPE
COL_F = COL_FQ + 3 * H * HD
COL_GATE = COL_F + H

RAW_SLOTS = 4
SPLIT_SLOTS = 4
CHUNK = 2048
PIECE = CHUNK // 2
SCORES = 3 * P
KIB = 1024


class Phase:

    def __init__(self, before, trips, widths, dmas=None):
        self.trips, self.widths, self.chunks = trips, widths, len(widths)
        dmas = dmas or [1] * self.chunks
        self.chunk0 = before.chunk0 + before.trips * before.chunks if before else 0
        self.offset = (before.offset + before.chunks) % RAW_SLOTS if before else 0
        base = before.landed_after if before else [0] * RAW_SLOTS
        self.per_body = [0] * RAW_SLOTS
        self.local = []
        for c in range(self.chunks):
            self.per_body[self.slot(c)] += 16 * dmas[c]
            self.local.append(base[self.slot(c)] + self.per_body[self.slot(c)])
        self.landed_after = [b + trips * n for b, n in zip(base, self.per_body)]

    def slot(self, c):
        return (self.offset + c) % RAW_SLOTS

    def landed(self, i, c):
        return i * self.per_body[self.slot(c)] + self.local[c]

    def piece(self, i, p):
        return i * (2 * self.chunks) + (2 * self.chunk0 + p + 1)

    def split_slot(self, p):
        return (2 * self.chunk0 + p) % SPLIT_SLOTS

    def freed(self, i, c):
        seam = self.chunks % RAW_SLOTS
        distance = seam if self.trips > 1 and seam and c < seam else RAW_SLOTS
        if isinstance(i, int) and 2 * (self.chunk0 + i * self.chunks + c - distance + 1) <= 0:
            return None
        return i * (2 * self.chunks) + 2 * (self.chunk0 + c - distance + 1)


MISC = ROPE + H
FOX_W, UKV_W, UQ_W, MISC_W = 2 * 3 * HD, 2 * 2 * HD, 2 * HD, KD // 2 * MISC
LATENT = Phase(None, 1, [PIECE] * 4 + [MISC_W] + [PIECE] * 4, [1] * 4 + [2] + [1] * 4)
PROJ0 = Phase(LATENT, 1, [PIECE] + [FOX_W] * 4 + [UKV_W, UQ_W], [KR] + [3] * 4 + [1, 1])
HEAD_CHUNKS, HEAD_DMAS = [PIECE] * 4 + [FOX_W] * 4 + [UKV_W, UQ_W], [1] * 4 + [3] * 4 + [1] * 2
HEAD_PIECES = 2 * len(HEAD_CHUNKS)
HEADS = Phase(PROJ0, (H - 2) // 2, HEAD_CHUNKS * 2, HEAD_DMAS * 2)
SEVENTH = Phase(HEADS, 1, HEAD_CHUNKS, HEAD_DMAS)
LAST = Phase(SEVENTH, 1, [PIECE] * 4)
MERGE = Phase(LAST, 4, [PIECE] * 4)
OUT = Phase(MERGE, 2, [PIECE] * 8)
FFN_IN = Phase(OUT, FF // 512, [PIECE] * 8, [2] * 8)
FFN_OUT = Phase(FFN_IN, 2, [PIECE] * 22)

READ_A = {MERGE: 1}
READ_B = {MERGE: 1 + H}
for _phase, _before in ((OUT, MERGE), (FFN_IN, OUT), (FFN_OUT, FFN_IN)):
    READ_A[_phase] = READ_A[_before] + _before.trips
    READ_B[_phase] = READ_B[_before] + _before.trips


O_GROUPS = ((1, slice(0, 4)), (1, slice(4, H - 1)), (1, slice(H - 1, H)), (0, slice(0, 4)), (0, slice(4, H)))
GROUPS_READ = (1, 1, 2, 3, 4, 4, 5, 5)

TILES_AT = {1: (4, 6), 3: (6, 8), 6: (8, 10), 7: (10, 12), 8: (12, 14), 9: (14, 16)}


class Chain:

    def __init__(self, engine, sem):
        self.engine, self.sem, self.base, self.i, self.n, self.per_body = engine, sem, 0, 0, 0, 0

    def body(self, i, per_body, base=None):
        if base is not None:
            self.base = base
        self.i, self.per_body, self.n = i, per_body, 0

    def done(self, instruction):
        self.n += 1
        instruction.then_inc(self.sem, 1)

    def wait(self, back=0):
        self.engine.wait_ge(self.sem, self.i * self.per_body + (self.base + self.n - back))

    def link(self, instruction):
        self.done(instruction)
        self.wait()


def hybrid_layer(nc, x, positions, norm_mix, w_in, b_forget, norm_q_a, w_uq, norm_kv_a, w_ukv, w_proj_mla,
                 w_proj_fox, w_out, norm_ffn, w_ffn_in, w_conv, b_conv, w_ffn_out, norm_final, y):
    F32, F32R, I32 = mybir.dt.float32, mybir.dt.float32r, mybir.dt.int32
    ACT, AX = mybir.ActivationFunctionType, mybir.AxisListType
    ctx = ExitStack()
    with ctx:
        base = 16512
        RAW_AT = base
        SPLIT_AT = RAW_AT + 32 * KIB
        XT_AT = SPLIT_AT + 32 * KIB
        BIG_AT = XT_AT + 32 * KIB
        RES_AT = BIG_AT + 88 * KIB
        SMALL_AT = RES_AT + 16 * KIB
        small = [SMALL_AT]

        def at(name, shape, offset, dtype=F32):
            return nc.alloc_sbuf_tensor_at(name, shape, dtype, offset=offset)

        def keep(name, shape, dtype=F32):
            t = at(name, shape, small[0], dtype)
            small[0] += -(-4 * int(np.prod(shape[1:])) // 32) * 32
            return t

        raw = [at(f"raw_{s}", [P, CHUNK], RAW_AT + s * 8 * KIB) for s in range(RAW_SLOTS)]
        w_hi = [at(f"w_hi_{s}", [P, PIECE], SPLIT_AT + s * 8 * KIB, F32R) for s in range(SPLIT_SLOTS)]
        w_lo = [at(f"w_lo_{s}", [P, PIECE], SPLIT_AT + s * 8 * KIB + 4 * KIB, F32R) for s in range(SPLIT_SLOTS)]
        xT_hi = at("xT_hi", [P, KD, S], XT_AT, F32R)
        xT_lo = at("xT_lo", [P, KD, S], XT_AT + 16 * KIB, F32R)
        gain_final = at("gain_final", [P, D], XT_AT)
        y_out = at("y_out", [P, NB, D], XT_AT + 8 * KIB)
        squares_y = at("squares_y", [P, 2, NB, 512], XT_AT + 24 * KIB)
        x_in = at("x_in", [P, NB, D], BIG_AT)
        ckv_n = at("ckv_n", [P, NB, RANK], BIG_AT)
        junk = at("junk", [P, D], BIG_AT + 16 * KIB)
        conv_rows = at("conv_rows", [2 * KF, 4, P], BIG_AT + 24 * KIB)
        mix_rows = at("mix_rows", [KD, P], BIG_AT + 26 * KIB)
        gain_rows = at("gain_rows", [KD + 2 * KR, P], BIG_AT + 26 * KIB + 512)
        cq_n = at("cq_n", [P, NB, RANK], BIG_AT + 27 * KIB)
        x_diag = at("x_diag", [P, NB, P], BIG_AT + 31 * KIB)
        gates = at("gates", [P, 2 * KD, S], BIG_AT)
        mT_hi = at("mT_hi", [P, KD, S], BIG_AT, F32R)
        mT_lo = at("mT_lo", [P, KD, S], BIG_AT + 16 * KIB, F32R)
        cT_hi = at("cT_hi", [P, 2, KR, S], BIG_AT + 32 * KIB, F32R)
        cT_lo = at("cT_lo", [P, 2, KR, S], BIG_AT + 40 * KIB, F32R)
        stage = [BIG_AT + 48 * KIB]

        def staged(name, shape, dtype=F32):
            t = at(name, shape, stage[0], dtype)
            stage[0] += -(-4 * int(np.prod(shape[1:])) // 32) * 32
            return t

        fqk_hi, fqk_lo = (staged(f"fqk_{n}", [P, 2, S], F32R) for n in ("hi", "lo"))
        fv_hi, fv_lo = (staged(f"fv_{n}", [P, NB, HD], F32R) for n in ("hi", "lo"))
        mqk_hi, mqk_lo = (staged(f"mqk_{n}", [P, 2, S], F32R) for n in ("hi", "lo"))
        mv_hi, mv_lo = (staged(f"mv_{n}", [P, NB, HD], F32R) for n in ("hi", "lo"))
        qr_parts, kr_hi = (staged(n, [2 * ROPE, S], F32R) for n in ("qr_parts", "kr_hi"))
        kr_lo = staged("kr_lo", [ROPE, S], F32R)
        prob = [staged(f"prob_{n}", [P, SCORES]) for n in ("fox", "mla")]
        pT_hi, pT_lo = ([staged(f"pT_{n}_{m}", [P, SCORES], F32R) for n in ("fox", "mla")] for m in ("hi", "lo"))
        q_rot = staged("q_rot", [P, NB, 2, ROPE])
        vT = [staged(f"vT_{n}", [P, S]) for n in ("fox", "mla")]
        mask = staged("mask", [P, SCORES])
        decay = staged("decay", [P, H, S])
        cum_q = staged("cum_q", [P, NB, H])
        cum_now = staged("cum_now", [P, NB])
        top, den, rden = (staged(n, [P, 2, NB]) for n in ("top", "den", "rden"))
        assert stage[0] <= BIG_AT + 87 * KIB, stage[0] - BIG_AT - 87 * KIB
        ones = at("ones", [P, P], BIG_AT + 87 * KIB)
        ident = at("ident", [P, P], BIG_AT + 87 * KIB + 512)
        oT_split = [[at(f"oT_{n}_{m}", [P, H, S], BIG_AT + place * KIB, F32R) for m, place in halves]
                    for n, halves in (("fox", (("hi", 48), ("lo", 56))), ("mla", (("hi", 32), ("lo", 40))))]
        x_again = at("x_again", [P, NB, D], BIG_AT + 64 * KIB)
        squares_h = at("squares_h", [P, 2, NB, 512], BIG_AT + 48 * KIB)
        h_diag = at("h_diag", [P, NB, P], BIG_AT + 81 * KIB)
        aT_hi = at("aT_hi", [P, KF, S], BIG_AT, F32R)
        aT_lo = at("aT_lo", [P, KF, S], BIG_AT + 44 * KIB, F32R)
        oT = at("oT", [P, 2, H, S], RES_AT)
        h = at("h", [P, NB, D], RES_AT)
        early = [RES_AT]

        def early_at(name, shape, dtype=F32):
            t = at(name, shape, early[0], dtype)
            early[0] += -(-4 * int(np.prod(shape[1:])) // 32) * 32
            return t

        upto = early_at("upto", [P, S])
        inv_freq = early_at("inv_freq", [P, HALF])
        pos_i = early_at("pos_i", [P, NB], I32)
        pos = early_at("pos", [P, NB])
        ang, turns, redu = (early_at(n, [P, 2, NB, HALF]) for n in ("ang", "turns", "redu"))
        bf = early_at("bf", [P, H])
        zf, zabs, zexp, zln, nlf = (early_at(n, [P, NB, H]) for n in ("zf", "zabs", "zexp", "zln", "nlf"))
        k_rot = early_at("k_rot", [P, NB, 2, ROPE])
        cos_t, sin_t = (early_at(n, [P, NB, HALF]) for n in ("cos_t", "sin_t"))
        misc_T = early_at("misc_T", [MISC, S])
        rot_a, rot_b = (early_at(f"rot_{n}", [P, NB, H * ROPE]) for n in ("a", "b"))
        nlf_wide = early_at("nlf_wide", [P, 2, NB, P])

        assert early[0] <= SMALL_AT
        gain_T = keep("gain_T", [P, 2 * KD + 2 * KR])
        conv_T = keep("conv_T", [P, 4, 2, KF])
        conv_now = keep("conv_now", [P, 2, 4, 2, 2])
        ss = keep("ss", [P, NB, 4])
        var, root, rstd, newt = (keep(n, [P, NB]) for n in ("var", "root", "rstd", "newt"))
        rstd_x = keep("rstd_x", [P, NB])
        spare = keep("spare", [P, 4])
        rstd_wide = keep("rstd_wide", [P, S])
        q_rot_all = at("q_rot_all", [P, NB, H, ROPE], small[0])
        hidden = keep("hidden", [P, 2, 2, S])
        assert small[0] <= nc.sbuf_usable_end, small[0] - nc.sbuf_usable_end

        bank = ctx.enter_context(nc.psum_tensor("bank", [P, 8, 512], F32))
        th = bank[:, 4, :].rearrange("p (t s) -> p t s", s=S)

        def sem(name):
            return ctx.enter_context(nc.semaphore(name))

        def sems(*names):
            return [sem(n) for n in names]

        raw_landed = [sem(f"raw_landed_{s}") for s in range(RAW_SLOTS)]
        hi_done, lo_done, piece_used = sems("hi_done", "lo_done", "piece_used")
        pair_read = sems("pair_a_read", "pair_b_read")
        dve_chain, pool_chain = sems("dve_chain", "pool_chain")
        first_landed = sem("first_landed")
        x_landed = sems(*(f"x_landed_{q}" for q in range(4)))
        mix_landed, taps_landed, pos_landed, bf_landed, x_again_landed, gain_landed, y_landed = sems(
            "mix_landed", "taps_landed", "pos_landed", "bf_landed", "x_again_landed", "gain_landed", "y_landed")
        tables_built, mix_turned, mix_read, taps_turned, taps_read = sems(
            "tables_built", "mix_turned", "mix_read", "taps_turned", "taps_read")
        angles_ready, tables_ready, f_abs, f_exp, misc_read, krot_ready, kr_turned, kr_hi_ready, kr_ready = sems(
            "angles_ready", "tables_ready", "f_abs", "f_exp", "misc_read", "krot_ready", "kr_turned", "kr_hi_ready",
            "kr_ready")
        nlf_ready, cumq_done, cumq_read, wide_ready, decay_done, decay_read = sems(
            "nlf_ready", "cumq_done", "cumq_read", "wide_ready", "decay_done", "decay_read")

        class Norm:

            def __init__(self, n):
                self.squared, self.varied, self.rooted, self.scaled, self.turned, self.hi, self.lo = sems(
                    *(f"{n}_{m}" for m in ("squared", "varied", "rooted", "scaled", "turned", "hi", "lo")))

        norm_x, norm_h, norm_cq, norm_ckv, norm_y = (Norm(n) for n in ("x", "h", "cq", "ckv", "y"))
        fox_hi, fox_lo, mla_hi, mla_lo, qrope_ready, qrot_ready, v_turned, bank5_hi, bank7_hi, bank5_lo, bank7_lo = \
            sems("fox_hi", "fox_lo", "mla_hi", "mla_lo", "qrope_ready", "qrot_ready", "v_turned", "bank5_hi",
                 "bank7_hi", "bank5_lo", "bank7_lo")
        misc_copied, misc_turned, diag_ready, wide_rstd, spread_ready = sems(
            "misc_copied", "misc_turned", "diag_ready", "wide_rstd", "spread_ready")
        q_products = sem("q_products")
        fox_by_token, gates_by_token, hidden_by_token = sems("fox_by_token", "gates_by_token", "hidden_by_token")
        scores_done, shifted, expd, normed, p_turned, p_hi, p_lo, o_done, o_read = (
            sems(f"{n}_fox", f"{n}_mla") for n in
            ("scores_done", "shifted", "expd", "normed", "p_turned", "p_hi", "p_lo", "o_done", "o_read"))
        o_split_hi, o_split, merged, m_hi, m_lo = sems("o_split_hi", "o_split", "merged", "m_hi", "m_lo")
        taps_on, first_tap, th_ready, act_ready, a_hi, a_lo = sems(
            "taps_on", "first_tap", "th_ready", "act_ready", "a_hi", "a_lo")
        last_product, last_added = sems("last_product", "last_added")
        y_ready = sems("y_ready_block_0", "y_ready_block_1_left", "y_ready_block_1_right")

        block = ctx.enter_context(nc.Block())

        def tiled(w):
            return w[0].rearrange("(k p) n -> p k n", p=P)

        w_in_v, w_uq_v, w_ukv_v, w_pm_v, w_pf_v, w_out_v, w_fi_v, w_fo_v = (
            tiled(w) for w in (w_in, w_uq, w_ukv, w_proj_mla, w_proj_fox, w_out, w_ffn_in, w_ffn_out))

        @block.sync
        def _(sp):
            def load(phase, i, c, *parts):
                slot, freed = phase.slot(c), phase.freed(i, c)
                if freed is not None:
                    sp.wait_ge(lo_done, freed)
                k, n = parts[0].shape[1:]
                wide = len(parts) * n
                rows = raw[slot][:, 0:k * wide].rearrange("p (k n) -> p k n", k=k)
                for t, part in enumerate(parts):
                    sp.dma_start(rows[:, :, t * n:(t + 1) * n], part).then_inc(raw_landed[slot], 16)

            def load_proj(phase, i, c0, j):
                if phase is PROJ0:
                    slot, of_heads = phase.slot(0), w_uq_v.rearrange("p k (h n) -> p k h n", h=H)
                    sp.wait_ge(lo_done, phase.freed(0, 0))
                    for k in range(KR):
                        sp.dma_start(raw[slot][:, k * H * ROPE:(k + 1) * H * ROPE].rearrange("p (h n) -> p h n", h=H),
                                     of_heads[:, k, :, HD:HD + ROPE]).then_inc(raw_landed[slot], 16)
                    c0 += 1
                for c in range(4):
                    load(phase, i, c0 + c, *(w_in_v[:, 4 * c:4 * c + 4, bass.ds(j * HD + (COL_FQ + t * H * HD), HD)]
                                             for t in range(3)))
                load(phase, i, c0 + 4, w_ukv_v[:, :, bass.ds(j * (2 * HD), 2 * HD)])
                load(phase, i, c0 + 5, w_uq_v[:, :, bass.ds(j * (HD + ROPE), HD)])

            def load_gate(phase, i, c0, j):
                for c in range(4):
                    load(phase, i, c0 + c, w_in_v[:, 4 * c:4 * c + 4, bass.ds(j * 512 + COL_GATE, 512)])

            x_blocks = x[0].rearrange("(b p) d -> p b d", p=P)
            sp.dma_start(mix_rows[:, :], norm_mix[0].rearrange("(t p) -> t p", p=P)).then_inc(mix_landed, 16)
            for quarter in range(4):
                cols = slice(quarter * 512, quarter * 512 + 512)
                sp.dma_start(x_in[:, :, cols], x_blocks[:, :, cols]).then_inc(x_landed[quarter], 16)
                if quarter == 0:
                    for p in range(2):
                        sp.dma_start(raw[0][:, p * PIECE:(p + 1) * PIECE].rearrange("p (k n) -> p k n", k=2),
                                     w_in_v[:, 2 * p:2 * p + 2, COL_CQ:COL_CQ + RANK]).then_inc(
                                         (first_landed, raw_landed[0])[p], 16)
                    for b in range(NB):
                        sp.dma_start(pos_i[:, b:b + 1], positions[0, b * P:(b + 1) * P].unsqueeze(1)).then_inc(
                            pos_landed, 16)
                else:
                    load(LATENT, 0, quarter, w_in_v[:, 4 * quarter:4 * quarter + 4, COL_CQ:COL_CQ + RANK])
                if quarter == 2:
                    sp.dma_start(bf[:, :], b_forget[0].partition_broadcast(P)).then_inc(bf_landed, 16)
                    row = 0
                    for vec, n in ((norm_ffn, KD), (norm_q_a, KR), (norm_kv_a, KR)):
                        sp.dma_start(gain_rows[row:row + n, :], vec[0].rearrange("(t p) -> t p", p=P)).then_inc(
                            taps_landed, 16)
                        row += n
                    sp.dma_start(conv_rows[:, 0:3, :], w_conv[0].rearrange("a (t p) -> t a p", p=P)).then_inc(
                        taps_landed, 16)
                    sp.dma_start(conv_rows[:, 3, :], b_conv[0].rearrange("(t p) -> t p", p=P)).then_inc(taps_landed, 16)
            sp.wait_ge(lo_done, LATENT.freed(0, 4))
            misc = raw[LATENT.slot(4)][:, 0:2 * MISC_W].rearrange("p (k n) -> p k n", k=KD)
            for at0, col, n in ((0, COL_KROPE, ROPE), (ROPE, COL_F, H)):
                sp.dma_start(misc[:, :, at0:at0 + n], w_in_v[:, :, col:col + n]).then_inc(
                    raw_landed[LATENT.slot(4)], 16)
            for c in range(4):
                load(LATENT, 0, 5 + c, w_in_v[:, 4 * c:4 * c + 4, COL_CKV:COL_CKV + RANK])
            load_proj(PROJ0, 0, 0, 0)
            with sp.Fori(0, HEADS.trips) as i:
                for half in range(2):
                    c0 = half * len(HEAD_CHUNKS)
                    load_gate(HEADS, i, c0, i * 2 + half)
                    load_proj(HEADS, i, c0 + 4, i * 2 + (half + 1))
            load_gate(SEVENTH, 0, 0, H - 2)
            load_proj(SEVENTH, 0, 4, H - 1)
            load_gate(LAST, 0, 0, H - 1)
            with sp.Fori(0, MERGE.trips) as i:
                for c in range(4):
                    k0 = 4 * (c % 2)
                    load(MERGE, i, c, (w_pm_v, w_pf_v)[c // 2][:, k0:k0 + 4, bass.ds(i * 512, 512)])
            sp.wait_ge(o_read[1], H)
            sp.dma_start(x_again[:, :, :], x[0].rearrange("(b p) d -> p b d", p=P)).then_inc(x_again_landed, 16)
            with sp.Fori(0, OUT.trips) as i:
                for c in range(8):
                    k0 = 4 * (c % 4)
                    load(OUT, i, c, w_out_v[:, k0:k0 + 4, bass.ds(i * 1024 + c // 4 * 512, 512)])
            with sp.Fori(0, FFN_IN.trips) as i:
                for c in range(8):
                    k0 = 4 * (c % 4)
                    load(FFN_IN, i, c, *(w_fi_v[:, k0:k0 + 4, bass.ds(i * 512 + (t * FF + c // 4 * 256), 256)]
                                         for t in range(2)))
            for i in range(FFN_OUT.trips):
                for c in range(22):
                    k0 = 4 * (c % 11)
                    load(FFN_OUT, i, c, w_fo_v[:, k0:k0 + 4, bass.ds(i * 1024 + c // 11 * 512, 512)])
                    if i == 0 and c == 8:
                        sp.wait_ge(piece_used, FFN_IN.piece(FFN_IN.trips - 1, 15))
                        sp.dma_start(gain_final[:, :], norm_final.partition_broadcast(P)).then_inc(gain_landed, 16)
            sp.wait_ge(y_ready[0], 1)
            sp.dma_start(y[0, 0:P, :], y_out[:, 0, :]).then_inc(y_landed, 16)
            for half in range(2):
                cols = slice(half * (D // 2), (half + 1) * (D // 2))
                sp.wait_ge(y_ready[1 + half], 1)
                sp.dma_start(y[0, P:S, cols], y_out[:, 1, cols]).then_inc(y_landed, 16)
            sp.wait_ge(y_landed, 3 * 16)

        def rotary_sums(engine, out, b, heads):
            of_cos, of_sin = (t[:, b, 0:heads * ROPE].rearrange("p (h n) -> p h n", n=ROPE) for t in (rot_a, rot_b))
            engine.tensor_tensor(out[:, :, 0:HALF], of_cos[:, :, 0:HALF], of_sin[:, :, HALF:ROPE], ALU.subtract)
            return engine.tensor_tensor(out[:, :, HALF:ROPE], of_cos[:, :, HALF:ROPE], of_sin[:, :, 0:HALF], ALU.add)

        @block.gpsimd
        def _(pool):
            nc.gpsimd.memset(ident[:, :], 0.0).then_inc(pool_chain, 1)
            nc.gpsimd.memset(upto[:, :], 1.0).then_inc(pool_chain, 1)
            nc.gpsimd.memset(mask[:, :], 0.0).then_inc(pool_chain, 1)
            nc.gpsimd.memset(ones[:, :], 1.0)
            pool.wait_ge(pool_chain, 3)
            nc.gpsimd.affine_select(out=ident[:, :], in_=ident[:, :], compare_op=ALU.not_equal, fill=1.0, base=0,
                                    pattern=[[-1, P]], channel_multiplier=1).then_inc(tables_built, 1)
            nc.gpsimd.affine_select(out=upto[:, 0:P], in_=upto[:, 0:P], compare_op=ALU.is_ge, fill=0.0, base=0,
                                    pattern=[[1, P]], channel_multiplier=-1).then_inc(tables_built, 1)
            for diagonal in (0, 2 * P):
                block_of = mask[:, diagonal:diagonal + P]
                nc.gpsimd.affine_select(out=block_of, in_=block_of, compare_op=ALU.is_ge, fill=MASKED, base=0,
                                        pattern=[[-1, P]], channel_multiplier=1).then_inc(tables_built, 1)
            for f in range(HALF):
                last = nc.gpsimd.memset(inv_freq[:, f:f + 1], float(np.float32(THETA ** (-2.0 * f / ROPE))))
            last.then_inc(tables_built, 1)
            pool.wait_ge(nlf_ready, 1)
            for head in range(H):
                if head >= 2:
                    pool.wait_ge(decay_done, head - 1)
                nc.gpsimd.tensor_copy(nlf_wide[:, head % 2, :, :],
                                      nlf[:, :, head:head + 1].to_broadcast([P, NB, P])).then_inc(wide_ready, 1)
            for b in range(NB):
                pool.wait_ge(q_products, b + 1)
                rotary_sums(nc.gpsimd, q_rot_all[:, b, :, :], b, H).then_inc(qrope_ready, 1)

        def tiles_of(first, tiles):
            return bank[:, first:first + 2, :].rearrange("p b (t s) -> p (b t) s", s=S)[:, 0:tiles, :]

        def spread_bank(k):
            return bank[:, 4 + k % 4, 0:S]

        def panel_bank(n, t):
            return bank[:, 4 + n % 2 * 2 + t // 2, t % 2 * S:t % 2 * S + S]

        def latent_bank(first):
            return lambda k: bank[:, first + k // 2, k % 2 * S:k % 2 * S + S]

        @block.scalar
        def _(act):
            def split_hi(phase, i, p):
                c, n, s = p // 2, phase.widths[p // 2], phase.split_slot(p)
                if phase is LATENT and c == 0:
                    act.wait_ge((first_landed, raw_landed[0])[p], 16)
                elif p % 2 == 0:
                    act.wait_ge(raw_landed[phase.slot(c)], phase.landed(i, c))
                if phase is not LATENT or p >= SPLIT_SLOTS:
                    act.wait_ge(piece_used, phase.piece(i, p - SPLIT_SLOTS))
                nc.scalar.activation(w_hi[s][:, 0:n], raw[phase.slot(c)][:, p % 2 * n:p % 2 * n + n],
                                     ACT.Copy).then_inc(hi_done, 1)

            def turned_hi(norm, source, gain, out, tiles, at_once=False):
                for k in tiles:
                    act.wait_ge(norm.turned, KR if at_once else k + 1)
                    nc.scalar.activation(out(k), source(k), ACT.Copy,
                                         scale=gain_T[:, gain + k:gain + k + 1]).then_inc(norm.hi, 1)

            def take_root(norm, blocks=slice(0, NB), n=1):
                act.wait_ge(norm.varied, n)
                nc.scalar.activation(root[:, blocks], var[:, blocks], ACT.Sqrt).then_inc(norm.rooted, 1)

            warmed = []

            def warm_up(function):
                warmed.append(function)
                nc.scalar.activation(spare[:, len(warmed) - 1:len(warmed)], ident[:, 0:1], function)

            def spread_rstd(b, n):
                act.wait_ge(wide_rstd, n)
                nc.scalar.activation(rstd_wide[:, :], bank[:, b, 0:S], ACT.Copy).then_inc(spread_ready, 1)

            def latent_squares(norm, first, done):
                act.wait_ge(piece_used, done)
                for b in range(NB):
                    nc.scalar.activation(junk[:, b * RANK:(b + 1) * RANK], bank[:, first + b, :], ACT.Square,
                                         accum_out=ss[:, b, 0:1]).then_inc(norm.squared, 1)

            act.wait_ge(tables_built, 1)
            warm_up(ACT.Copy)
            act.wait_ge(mix_read, 1)
            turned_hi(norm_x, spread_bank, 0, lambda k: xT_hi[:, k, :], range(4))
            for p in range(10):
                split_hi(LATENT, 0, p)
                if p in TILES_AT:
                    turned_hi(norm_x, spread_bank, 0, lambda k: xT_hi[:, k, :], range(*TILES_AT[p]))
                if p >= 8:
                    b = p - 8
                    if b:
                        act.wait_ge(norm_x.squared, b)
                    nc.scalar.activation(junk[:, :], x_in[:, b, :], ACT.Square,
                                         accum_out=ss[:, b, 0:1]).then_inc(norm_x.squared, 1)
            take_root(norm_x)
            split_hi(LATENT, 0, 10)
            act.wait_ge(angles_ready, 1)
            nc.scalar.activation(sin_t[:, :, :], redu[:, 0, :, :], ACT.Sin)
            nc.scalar.activation(cos_t[:, :, :], redu[:, 1, :, :], ACT.Sin).then_inc(tables_ready, 1)
            split_hi(LATENT, 0, 11)
            latent_squares(norm_cq, 2, LATENT.piece(0, 7))
            take_root(norm_cq)
            for p in range(12, 14):
                split_hi(LATENT, 0, p)
            act.wait_ge(piece_used, LATENT.piece(0, 9))
            nc.scalar.activation(misc_T[:, :], bank[0:MISC, 4, 0:S], ACT.Copy).then_inc(misc_copied, 1)
            spread_rstd(5, 1)
            for p in range(14, 16):
                split_hi(LATENT, 0, p)
            turned_hi(norm_cq, latent_bank(6), 2 * KD, lambda k: cT_hi[:, 0, k, :], range(KR), at_once=True)
            act.wait_ge(f_abs, 1)
            nc.scalar.activation(zexp[:, :, :], zabs[:, :, :], ACT.Exp, scale=-1.0).then_inc(f_exp, 1)
            act.wait_ge(f_exp, 1)
            nc.scalar.activation(zln[:, :, :], zexp[:, :, :], ACT.Ln, bias=1.0).then_inc(f_exp, 1)
            for p in range(16, 18):
                split_hi(LATENT, 0, p)
            for p in range(2):
                split_hi(PROJ0, 0, p)
            act.wait_ge(kr_turned, 1)
            nc.scalar.activation(kr_hi[:, :], bank[:, 6, 0:S], ACT.Copy).then_inc(kr_hi_ready, 1)
            for p in range(2, 4):
                split_hi(PROJ0, 0, p)
            latent_squares(norm_ckv, 0, LATENT.piece(0, 17))
            for p in range(4, 8):
                split_hi(PROJ0, 0, p)
            take_root(norm_ckv)
            for p in range(8, 12):
                split_hi(PROJ0, 0, p)
            turned_hi(norm_ckv, latent_bank(0), 2 * KD + KR, lambda k: cT_hi[:, 1, k, :], range(KR), at_once=True)
            split_hi(PROJ0, 0, 12)
            warm_up(ACT.Exp)
            split_hi(PROJ0, 0, 13)

            def stage_fox_hi(n):
                act.wait_ge(fox_by_token, n)
                nc.scalar.activation(fqk_hi[:, :, :].rearrange("p a b -> p (a b)"), bank[:, 4, :], ACT.Copy)
                nc.scalar.activation(vT[0][:, :], bank[:, 5, 0:S], ACT.Copy).then_inc(fox_hi, 1)

            def exponentials(branch, n):
                act.wait_ge(shifted[branch], n)
                for b, cols in enumerate((slice(0, P), slice(P, SCORES))):
                    last = nc.scalar.activation(prob[branch][:, cols], prob[branch][:, cols], ACT.Exp,
                                                bias=top[:, branch, b:b + 1], accum_out=den[:, branch, b:b + 1])
                last.then_inc(expd[branch], 1)

            def one_head(phase, i, n, first):
                for p in range(2):
                    split_hi(phase, i, first + p)
                stage_fox_hi(n)
                for p in range(2, 4):
                    split_hi(phase, i, first + p)
                act.wait_ge(piece_used, phase.piece(i, first - 1))
                nc.scalar.activation(mqk_hi[:, :, :].rearrange("p a b -> p (a b)"), bank[:, 6, :], ACT.Copy)
                nc.scalar.activation(vT[1][:, :], bank[:, 7, 0:S], ACT.Copy).then_inc(mla_hi, 1)
                split_hi(phase, i, first + 4)
                split_hi(phase, i, first + 5)
                act.wait_ge(v_turned, n)
                nc.scalar.activation(qr_parts[:, :], bank[:, 5, S:2 * S], ACT.Copy)
                nc.scalar.activation(fv_hi[:, :, :].rearrange("p a b -> p (a b)"), bank[:, 5, 0:S],
                                     ACT.Copy).then_inc(bank5_hi, 1)
                nc.scalar.activation(mv_hi[:, :, :].rearrange("p a b -> p (a b)"), bank[:, 7, 0:S],
                                     ACT.Copy).then_inc(bank7_hi, 1)
                if phase is LAST:
                    act.wait_ge(o_read[1], H - 1)
                    output_hi(*O_GROUPS[0])
                exponentials(0, n)
                split_hi(phase, i, first + 6)
                split_hi(phase, i, first + 7)
                if phase is LAST:
                    output_hi(*O_GROUPS[1])
                exponentials(1, n)
                after, j, p0 = (MERGE, 0, 0) if phase is LAST else (phase, i, first + 8)
                split_hi(after, j, p0)
                split_hi(after, j, p0 + 1)
                for branch in range(2):
                    act.wait_ge(p_turned[branch], n)
                    nc.scalar.activation(pT_hi[branch][:, :], bank[:, 5 + 2 * branch, 0:SCORES],
                                         ACT.Copy).then_inc(p_hi[branch], 1)
                    split_hi(after, j, p0 + 2 + branch)
                act.wait_ge(gates_by_token, n)
                for b in range(2):
                    last = nc.scalar.activation(gates[:, bass.ds((n - 1) * 4 + 2 * b, 2), :].rearrange(
                        "p a b -> p (a b)"), bank[:, 2 + b, :], ACT.Tanh, scale=0.5)
                last.then_inc(pair_read[1], 1)
                if phase is not LAST:
                    for p in range(12, HEAD_PIECES):
                        split_hi(phase, i, first + p)

            def output_hi(branch, heads):
                nc.scalar.activation(oT_split[branch][0][:, heads, :], oT[:, branch, heads, :],
                                     ACT.Copy).then_inc(o_split_hi, 1)

            with act.Fori(0, HEADS.trips) as i:
                for half in range(2):
                    one_head(HEADS, i, i * 2 + (half + 1), half * HEAD_PIECES)
            one_head(SEVENTH, 0, H - 1, 0)
            one_head(LAST, 0, H, 0)

            act.wait_ge(o_read[1], H)
            for group in O_GROUPS[2:]:
                output_hi(*group)

            def merged_hi(n):
                act.wait_ge(merged, n)
                panel = bass.ds((n - 1) * 4, 4)
                nc.scalar.activation(mT_hi[:, panel, :], gates[:, bass.ds((n - 1) * 4 + KD, 4), :], ACT.Copy,
                                     scale=0.5).then_inc(m_hi, 1)

            for p in range(4, 8):
                split_hi(MERGE, 0, p)
            with act.Fori(1, MERGE.trips) as i:
                for p in range(8):
                    split_hi(MERGE, i, p)
                    if p == 4:
                        merged_hi(i)

            def residual_squares(norm, pair, read, panel):
                squares = squares_h if norm is norm_h else squares_y
                act.wait_ge(pair_read[pair], read)
                for b in range(NB):
                    last = nc.scalar.activation(squares[:, pair, b, :],
                                                h[:, b, panel * 512:panel * 512 + 512], ACT.Square,
                                                accum_out=ss[:, b, panel:panel + 1])
                last.then_inc(norm.squared, 1)

            def turned_panel_hi(n):
                act.wait_ge(norm_h.turned, n + 1)
                for t in range(4):
                    k = 4 * n + t
                    last = nc.scalar.activation(xT_hi[:, k, :], panel_bank(n, t), ACT.Copy,
                                                scale=gain_T[:, KD + k:KD + k + 1])
                last.then_inc(norm_h.hi, 1)

            for i in range(OUT.trips):
                for p in range(16):
                    split_hi(OUT, i, p)
                    if i == 0 and p == 4:
                        merged_hi(MERGE.trips)
                    if i and p == 3:
                        residual_squares(norm_h, 1, READ_B[OUT] + i, 2 * i - 1)
                    if i and p == 5:
                        turned_panel_hi(1)
                    if p == 11:
                        residual_squares(norm_h, 0, READ_A[OUT] + i + 1, 2 * i)
                    if p == 13:
                        turned_panel_hi(2 * i)
            warm_up(ACT.Sqrt)
            for p in range(4):
                split_hi(FFN_IN, 0, p)
            residual_squares(norm_h, 1, READ_B[OUT] + 2, 3)
            take_root(norm_h)
            split_hi(FFN_IN, 0, 4)
            split_hi(FFN_IN, 0, 5)
            turned_panel_hi(3)
            split_hi(FFN_IN, 0, 6)
            spread_rstd(4, 2)
            split_hi(FFN_IN, 0, 7)

            def hidden_panel(i, b, n, between):
                act.wait_ge(taps_on, n)
                act.wait_ge(hidden_by_token, n)
                for part in range(2):
                    for t in range(2):
                        last = nc.scalar.activation(hidden[:, part, t, :], bank[:, 2 * b + part, t * S:t * S + S],
                                                    ACT.Identity, bias=conv_now[:, b, 3, part, t:t + 1],
                                                    scale=conv_now[:, b, 2, part, t:t + 1])
                    last.then_inc(first_tap, 1)
                between(0)
                act.wait_ge(pair_read[b], i + (READ_A, READ_B)[b][FFN_IN] + 1)
                nc.scalar.activation(th[:, :, :], hidden[:, 0, :, :], ACT.Tanh, scale=0.5).then_inc(th_ready, 1)
                between(1)
                act.wait_ge(act_ready, n)
                nc.scalar.activation(aT_hi[:, bass.ds((n - 1) * 2, 2), :], hidden[:, 0, :, :], ACT.Copy,
                                     scale=0.5).then_inc(a_hi, 1)

            def ffn_in_body(i, first):
                if not first:
                    for p in range(4):
                        split_hi(FFN_IN, i, p)
                    hidden_panel(i - 1, 1, i * 2, lambda step: split_hi(FFN_IN, i, 4 + step))
                for p in range(8 if first else 6, 12):
                    split_hi(FFN_IN, i, p)
                hidden_panel(i, 0, i * 2 + 1, lambda step: split_hi(FFN_IN, i, 12 + step))
                split_hi(FFN_IN, i, 14)
                split_hi(FFN_IN, i, 15)

            ffn_in_body(0, True)
            with act.Fori(1, FFN_IN.trips) as i:
                ffn_in_body(i, False)

            for i in range(FFN_OUT.trips):
                for p in range(4):
                    split_hi(FFN_OUT, i, p)
                if i == 0:
                    hidden_panel(FFN_IN.trips - 1, 1, 2 * FFN_IN.trips, lambda step: split_hi(FFN_OUT, 0, 4 + step))
                else:
                    residual_squares(norm_y, 1, READ_B[FFN_OUT] + i, 2 * i - 1)
                    split_hi(FFN_OUT, i, 4)
                    split_hi(FFN_OUT, i, 5)
                for p in range(6, 44):
                    split_hi(FFN_OUT, i, p)
                    if p == 25:
                        residual_squares(norm_y, 0, READ_A[FFN_OUT] + i + 1, 2 * i)
            nc.scalar.activation(spare[:, 3:4], rstd_x[:, 0:1], ACT.Sqrt)
            for b in range(NB):
                act.wait_ge(last_added, b + 1)
                nc.scalar.activation(squares_y[:, 1, b, :], h[:, b, D - 512:D], ACT.Square,
                                     accum_out=ss[:, b, 3:4]).then_inc(norm_y.squared, 1)
                take_root(norm_y, slice(b, b + 1), b + 1)
            act.wait_ge(norm_y.scaled, 1)
            nc.scalar.activation(y_out[:, 1, D // 2:D], y_out[:, 1, D // 2:D], ACT.Copy,
                                 scale=rstd[:, 1:2]).then_inc(y_ready[2], 1)

        @block.vector
        def _(dve):
            chain = Chain(dve, dve_chain)

            def split_lo(phase, i, p):
                c, n, s = p // 2, phase.widths[p // 2], phase.split_slot(p)
                dve.wait_ge(hi_done, phase.piece(i, p))
                nc.vector.tensor_tensor(w_lo[s][:, 0:n], raw[phase.slot(c)][:, p % 2 * n:p % 2 * n + n],
                                        w_hi[s][:, 0:n].bitcast(F32), ALU.subtract).then_inc(lo_done, 1)

            def reciprocal_root(norm, squares, panels, width, out=rstd, ready=None, within=None, blocks=slice(0, NB),
                                n=1):
                dve.wait_ge(norm.squared, squares)
                source, sums, mean, rooted, out = ss[:, blocks, 0], newt[:, blocks], var[:, blocks], root[:, blocks], \
                    out[:, blocks]
                if panels > 1:
                    chain.link(nc.vector.reduce_sum(sums, ss[:, blocks, 0:panels], AX.X))
                    source = sums
                if within is not None:
                    for _ in range(2):
                        chain.link(nc.vector.tensor_tensor(sums, source, within[:, blocks], ALU.mult))
                        source = sums
                nc.vector.tensor_scalar(mean, source, 1.0 / width, EPS, ALU.mult, ALU.add).then_inc(norm.varied, 1)
                dve.wait_ge(norm.rooted, n)
                chain.link(nc.vector.reciprocal(out, rooted))
                chain.link(nc.vector.scalar_tensor_tensor(out=sums, in0=out, scalar=-0.5, in1=out, op0=ALU.mult,
                                                          op1=ALU.mult))
                chain.link(nc.vector.tensor_tensor(sums, sums, mean, ALU.mult))
                last = nc.vector.scalar_tensor_tensor(out=out, in0=sums, scalar=1.5, in1=out, op0=ALU.add, op1=ALU.mult)
                if within is not None:
                    chain.link(last)
                    last = nc.vector.tensor_tensor(out, out, within[:, blocks], ALU.mult)
                if ready is None:
                    chain.link(last)
                else:
                    last.then_inc(ready, 1)
                    dve.wait_ge(ready, 1)

            def diagonal(values, out):
                for b in range(NB):
                    last = nc.vector.tensor_scalar(out[:, b, :], ident[:, :], values[:, b:b + 1], None, ALU.mult)
                last.then_inc(diag_ready, 1)

            def by_token(tiles, count, ready):
                nc.vector.tensor_tensor(tiles, tiles, rstd_wide[:, :].unsqueeze(1).to_broadcast([P, count, S]),
                                        ALU.mult).then_inc(ready, 1)

            def turned_lo(norm, source, gain, hi, lo, tiles, at_once=False):
                for k in tiles:
                    dve.wait_ge(norm.hi, KR if at_once else k + 1)
                    nc.vector.scalar_tensor_tensor(out=lo(k), in0=source(k), scalar=gain_T[:, gain + k:gain + k + 1],
                                                   in1=hi(k).bitcast(F32), op0=ALU.mult,
                                                   op1=ALU.subtract).then_inc(norm.lo, 1)

            def rotary_products(b, source, heads, scale=None):
                pairs = source.rearrange("p (t f) -> p t f", f=HALF)
                for table, product in ((cos_t, rot_a), (sin_t, rot_b)):
                    out = product[:, b, 0:heads * ROPE].rearrange("p (t f) -> p t f", f=HALF)
                    factor = table[:, b, :].unsqueeze(1).to_broadcast([P, 2 * heads, HALF])
                    if scale is None:
                        last = nc.vector.tensor_tensor(out, pairs, factor, ALU.mult)
                    else:
                        last = nc.vector.scalar_tensor_tensor(out=out, in0=pairs, scalar=scale[:, b:b + 1], in1=factor,
                                                              op0=ALU.mult, op1=ALU.mult)
                return last

            dve.wait_ge(mix_turned, 1)
            nc.vector.tensor_copy(gain_T[:, 0:KD], bank[:, 1, 0:KD]).then_inc(mix_read, 1)
            x_tiles = (norm_x, spread_bank, 0, lambda k: xT_hi[:, k, :], lambda k: xT_lo[:, k, :])
            turned_lo(*x_tiles, range(4))
            for p in range(2):
                split_lo(LATENT, 0, p)
            dve.wait_ge(pos_landed, 16 * NB)
            dve.wait_ge(tables_built, 5)
            chain.link(nc.vector.tensor_copy(pos[:, :], pos_i[:, :]))
            for b in range(NB):
                for t in range(2):
                    last = nc.vector.tensor_scalar(ang[:, t, b, :], inv_freq[:, :], pos[:, b:b + 1], None, ALU.mult)
            chain.link(last)
            for t in range(2):
                last = nc.vector.tensor_scalar(turns[:, t, :, :], ang[:, t, :, :], 1.0 / (2 * math.pi), 0.25 * t,
                                               ALU.mult, ALU.add)
            chain.link(last)
            to_whole = 1.5 * 2.0 ** 23
            for step in (to_whole, -to_whole):
                chain.link(nc.vector.tensor_scalar(turns[:, :, :, :], turns[:, :, :, :], step, None, ALU.add))
            rest, source = 2 * math.pi, ang
            for bits in (5, 13, 21, None):
                part = rest if bits is None else math.floor(rest * 2.0 ** bits) / 2.0 ** bits
                rest -= part
                chain.link(nc.vector.scalar_tensor_tensor(
                    out=redu[:, :, :, :].rearrange("p a b f -> p (a b f)"),
                    in0=turns[:, :, :, :].rearrange("p a b f -> p (a b f)"), scalar=-part,
                    in1=source[:, :, :, :].rearrange("p a b f -> p (a b f)"), op0=ALU.mult, op1=ALU.add))
                source = redu
            chain.link(nc.vector.tensor_scalar(redu[:, 1, :, :], redu[:, 1, :, :], math.pi / 2, None, ALU.add))
            limit = 3.1415925
            nc.vector.tensor_scalar(redu[:, :, :, :], redu[:, :, :, :], limit, -limit, ALU.min,
                                    ALU.max).then_inc(angles_ready, 1)
            turned_lo(*x_tiles, range(*TILES_AT[1]))
            for p in range(2, 10):
                split_lo(LATENT, 0, p)
                if p in TILES_AT:
                    turned_lo(*x_tiles, range(*TILES_AT[p]))
                if p == 7:
                    dve.wait_ge(taps_turned, 1)
                    nc.vector.tensor_copy(conv_T[:, :, :, :].rearrange("p a h t -> p (a h t)"), bank[:, 1, 0:8 * KF])
                    nc.vector.tensor_copy(gain_T[:, KD:2 * KD + 2 * KR],
                                          bank[:, 1, 8 * KF:8 * KF + KD + 2 * KR]).then_inc(taps_read, 1)
            reciprocal_root(norm_x, NB, 1, D, out=rstd_x)
            diagonal(rstd_x, x_diag)
            for p in range(10, 12):
                split_lo(LATENT, 0, p)
            reciprocal_root(norm_cq, NB, 1, RANK, within=rstd_x)
            for b in range(NB):
                last = nc.vector.tensor_scalar(cq_n[:, b, :], bank[:, 2 + b, :], rstd[:, b:b + 1], None, ALU.mult)
            last.then_inc(pair_read[1], 1)
            for p in range(12, 16):
                split_lo(LATENT, 0, p)
            turned_lo(norm_cq, latent_bank(6), 2 * KD, lambda k: cT_hi[:, 0, k, :], lambda k: cT_lo[:, 0, k, :],
                      range(KR), at_once=True)
            dve.wait_ge(misc_turned, 1)
            dve.wait_ge(bf_landed, 16)
            dve.wait_ge(tables_ready, 1)

            def misc_of(b, cols):
                return bank[:, 5, b * MISC + cols.start:b * MISC + cols.stop]

            for b in range(NB):
                last = nc.vector.scalar_tensor_tensor(out=zf[:, b, :], in0=misc_of(b, slice(ROPE, MISC)),
                                                      scalar=rstd_x[:, b:b + 1], in1=bf[:, :], op0=ALU.mult, op1=ALU.add)
            chain.link(last)
            nc.vector.scalar_tensor_tensor(out=zabs[:, :, :], in0=zf[:, :, :], scalar=-1.0, in1=zf[:, :, :],
                                           op0=ALU.mult, op1=ALU.max).then_inc(f_abs, 1)
            nc.vector.tensor_scalar(nlf[:, :, :], zf[:, :, :], -1.0, 0.0, ALU.mult, ALU.max)
            for b in range(NB):
                last = rotary_products(b, misc_of(b, slice(0, ROPE)), 1, rstd_x)
            last.then_inc(misc_read, 1)
            dve.wait_ge(misc_read, 1)
            for b in range(NB):
                for copy in range(2):
                    last = rotary_sums(nc.vector, k_rot[:, b, copy:copy + 1, :], b, 1)
            last.then_inc(krot_ready, 1)
            split_lo(LATENT, 0, 16)
            split_lo(LATENT, 0, 17)
            dve.wait_ge(f_exp, 2)
            nc.vector.tensor_tensor(nlf[:, :, :], nlf[:, :, :], zln[:, :, :], ALU.add).then_inc(nlf_ready, 1)
            for p in range(2):
                split_lo(PROJ0, 0, p)
            dve.wait_ge(kr_hi_ready, 1)
            nc.vector.tensor_tensor(kr_lo[:, :], bank[0:ROPE, 6, 0:S], kr_hi[0:ROPE, :].bitcast(F32),
                                    ALU.subtract).then_inc(kr_ready, 1)
            split_lo(PROJ0, 0, 2)
            dve.wait_ge(cumq_done, 1)
            nc.vector.tensor_scalar(cum_q[:, :, :].rearrange("p b h -> p (b h)"), bank[:, 7, 0:NB * H], -1.0, None,
                                    ALU.mult).then_inc(cumq_read, 1)

            for p in range(3, 5):
                split_lo(PROJ0, 0, p)
            for head in range(H):
                split_lo(PROJ0, 0, 5 + head)
                dve.wait_ge(decay_done, head + 1)
                nc.vector.tensor_copy(decay[:, head, :], bank[:, 6 + head % 2, 0:S]).then_inc(decay_read, 1)
                if head == 2:
                    reciprocal_root(norm_ckv, NB, 1, RANK, within=rstd_x)
                    for b in range(NB):
                        last = nc.vector.tensor_scalar(ckv_n[:, b, :], bank[:, b, :], rstd[:, b:b + 1], None,
                                                       ALU.mult)
                    last.then_inc(pair_read[0], 1)
                if head in (3, 4):
                    rotary_products(head - 3, bank[:, 2 + head - 3, :], H).then_inc(q_products, 1)
                if head == 6:
                    turned_lo(norm_ckv, latent_bank(0), 2 * KD + KR, lambda k: cT_hi[:, 1, k, :],
                              lambda k: cT_lo[:, 1, k, :], range(KR), at_once=True)
            split_lo(PROJ0, 0, 13)
            dve.wait_ge(qrope_ready, NB)
            dve.wait_ge(spread_ready, 1)

            def lo_of(hi, lo, source):
                return nc.vector.tensor_tensor(lo[:, :, :].rearrange("p a b -> p (a b)"), source,
                                               hi[:, :, :].rearrange("p a b -> p (a b)").bitcast(F32), ALU.subtract)

            def stage_fox_lo(n):
                dve.wait_ge(fox_hi, n)
                lo_of(fqk_hi, fqk_lo, bank[:, 4, :]).then_inc(fox_lo, 1)

            before_heads, HEAD_STEPS = chain.n, 8

            def shift(branch, n, scale, bias):
                dve.wait_ge(scores_done[branch], n)
                chain.link(nc.vector.scalar_tensor_tensor(
                    out=prob[branch][:, :], in0=bank[:, 4 + 2 * branch, 0:SCORES], scalar=scale, in1=bias[:, :],
                    op0=ALU.mult, op1=ALU.add))
                nc.vector.reduce_max(top[:, branch, 0:1], prob[branch][:, 0:P], AX.X)
                chain.link(nc.vector.reduce_max(top[:, branch, 1:2], prob[branch][:, P:SCORES], AX.X))
                nc.vector.tensor_scalar(top[:, branch, :], top[:, branch, :], -1.0, None,
                                        ALU.mult).then_inc(shifted[branch], 1)

            def normalise(branch, n):
                dve.wait_ge(expd[branch], n)
                chain.link(nc.vector.reciprocal(rden[:, branch, :], den[:, branch, :]))
                for b, cols in enumerate((slice(0, P), slice(P, SCORES))):
                    last = nc.vector.tensor_scalar(prob[branch][:, cols], prob[branch][:, cols],
                                                   rden[:, branch, b:b + 1], None, ALU.mult)
                last.then_inc(normed[branch], 1)

            def one_head(phase, i, n, first):
                chain.body(n - 1, HEAD_STEPS, before_heads)
                dve.wait_ge(piece_used, phase.piece(i, first - 5))
                by_token(tiles_of(4, 3), 3, fox_by_token)
                for p in range(2):
                    split_lo(phase, i, first + p)
                stage_fox_lo(n)
                for p in range(2, 4):
                    split_lo(phase, i, first + p)
                for copy in range(2):
                    last = nc.vector.tensor_copy(q_rot[:, :, copy, :], q_rot_all[:, :, bass.ds(n - 1, 1), :].rearrange(
                        "p b h n -> p b (h n)"))
                last.then_inc(qrot_ready, 1)
                chain.link(nc.vector.tensor_copy(cum_now[:, :], cum_q[:, :, bass.ds(n - 1, 1)]))
                for b, cols in enumerate((slice(0, P), slice(P, SCORES))):
                    last = nc.vector.scalar_tensor_tensor(
                        out=prob[0][:, cols], in0=decay[:, bass.ds(n - 1, 1), 0:P * (b + 1)],
                        scalar=cum_now[:, b:b + 1], in1=mask[:, cols], op0=ALU.add, op1=ALU.add)
                chain.done(last)
                dve.wait_ge(mla_hi, n)
                lo_of(mqk_hi, mqk_lo, bank[:, 6, :]).then_inc(mla_lo, 1)
                split_lo(phase, i, first + 4)
                split_lo(phase, i, first + 5)
                dve.wait_ge(bank5_hi, n)
                lower = qr_parts[ROPE:2 * ROPE, :]
                nc.vector.tensor_tensor(lower, bank[ROPE:2 * ROPE, 5, S:2 * S], lower.bitcast(F32), ALU.subtract)
                lo_of(fv_hi, fv_lo, bank[:, 5, 0:S]).then_inc(bank5_lo, 1)
                dve.wait_ge(bank7_hi, n)
                lo_of(mv_hi, mv_lo, bank[:, 7, 0:S]).then_inc(bank7_lo, 1)
                chain.wait()
                shift(0, n, FOX_SCALE, prob[0])
                split_lo(phase, i, first + 6)
                normalise(0, n)
                if phase is LAST:
                    output_lo(*O_GROUPS[0], 1)
                split_lo(phase, i, first + 7)
                shift(1, n, MLA_SCALE, mask)
                if phase is LAST:
                    output_lo(*O_GROUPS[1], 2)
                after, j, p0 = (MERGE, 0, 0) if phase is LAST else (phase, i, first + 8)
                split_lo(after, j, p0)
                normalise(1, n)
                split_lo(after, j, p0 + 1)
                for branch in range(2):
                    dve.wait_ge(p_hi[branch], n)
                    nc.vector.tensor_tensor(pT_lo[branch][:, :], bank[:, 5 + 2 * branch, 0:SCORES],
                                            pT_hi[branch][:, :].bitcast(F32), ALU.subtract).then_inc(p_lo[branch], 1)
                    split_lo(after, j, p0 + 2 + branch)
                for branch in range(2):
                    dve.wait_ge(o_done[branch], n)
                    nc.vector.tensor_copy(oT[:, branch, bass.ds(n - 1, 1), :],
                                          bank[:, 6 + branch, 0:S]).then_inc(o_read[branch], 1)
                by_token(tiles_of(2, 4), 4, gates_by_token)
                if phase is not LAST:
                    for p in range(12, HEAD_PIECES):
                        split_lo(phase, i, first + p)
                assert chain.n == HEAD_STEPS, chain.n

            def output_lo(branch, heads, done):
                dve.wait_ge(o_split_hi, done)
                nc.vector.tensor_tensor(oT_split[branch][1][:, heads, :], oT[:, branch, heads, :],
                                        oT_split[branch][0][:, heads, :].bitcast(F32), ALU.subtract).then_inc(o_split, 1)

            with dve.Fori(0, HEADS.trips) as i:
                for half in range(2):
                    one_head(HEADS, i, i * 2 + (half + 1), half * HEAD_PIECES)
            one_head(SEVENTH, 0, H - 1, 0)
            one_head(LAST, 0, H, 0)
            chain.body(0, 0, before_heads + H * HEAD_STEPS)

            for done, group in enumerate(O_GROUPS[2:]):
                output_lo(*group, done + 3)

            def panel_of(n, first):
                return (slice(None), bass.ds((n - 1) * 4 + first, 4), slice(None))

            def weigh(pair, first, n, done):
                dve.wait_ge(piece_used, done)
                for b in range(2):
                    g = gates[:, bass.ds((n - 1) * 4 + first + 2 * b, 2), :].rearrange("p a b -> p (a b)")
                    last = nc.vector.scalar_tensor_tensor(out=g, in0=g, scalar=1.0, in1=bank[:, 2 * pair + b, :],
                                                          op0=ALU.add, op1=ALU.mult)
                last.then_inc(pair_read[pair], 1)

            def merge_panel(n, done, between):
                weigh(1, KD, n, done)
                dve.wait_ge(pair_read[1], READ_B[MERGE] + n)
                nc.vector.tensor_tensor(gates[panel_of(n, KD)], gates[panel_of(n, 0)], gates[panel_of(n, KD)],
                                        ALU.add).then_inc(merged, 1)
                between()
                dve.wait_ge(m_hi, n)
                nc.vector.scalar_tensor_tensor(out=mT_lo[panel_of(n, 0)], in0=gates[panel_of(n, KD)], scalar=0.5,
                                               in1=mT_hi[panel_of(n, 0)].bitcast(F32), op0=ALU.mult,
                                               op1=ALU.subtract).then_inc(m_lo, 1)

            for p in range(4, 8):
                split_lo(MERGE, 0, p)
            weigh(0, 0, 1, MERGE.piece(0, 3))
            with dve.Fori(1, MERGE.trips) as i:
                for p in range(4):
                    split_lo(MERGE, i, p)
                merge_panel(i, MERGE.piece(i - 1, 7), lambda: split_lo(MERGE, i, 4))
                for p in range(5, 8):
                    split_lo(MERGE, i, p)
                weigh(0, 0, i + 1, MERGE.piece(i, 3))

            def add_residual(pair, done, source, panel):
                dve.wait_ge(piece_used, done)
                cols = slice(panel * 512, panel * 512 + 512)
                for b in range(NB):
                    last = nc.vector.tensor_tensor(h[:, b, cols], bank[:, 2 * pair + b, :], source[:, b, cols], ALU.add)
                last.then_inc(pair_read[pair], 1)

            def turned_panel_lo(n):
                dve.wait_ge(norm_h.hi, n + 1)
                for t in range(4):
                    k = 4 * n + t
                    last = nc.vector.scalar_tensor_tensor(
                        out=xT_lo[:, k, :], in0=panel_bank(n, t), scalar=gain_T[:, KD + k:KD + k + 1],
                        in1=xT_hi[:, k, :].bitcast(F32), op0=ALU.mult, op1=ALU.subtract)
                last.then_inc(norm_h.lo, 1)

            for i in range(OUT.trips):
                for p in range(16):
                    if i == 0 and p == 4:
                        merge_panel(MERGE.trips, MERGE.piece(MERGE.trips - 1, 7), lambda: split_lo(OUT, 0, 4))
                        dve.wait_ge(x_again_landed, 16)
                    else:
                        split_lo(OUT, i, p)
                    if i and p == 3:
                        add_residual(1, OUT.piece(i - 1, 15), x_again, 2 * i - 1)
                    if i and p == 5:
                        turned_panel_lo(1)
                    if p == 11:
                        add_residual(0, OUT.piece(i, 7), x_again, 2 * i)
                    if p == 14:
                        turned_panel_lo(2 * i)
            for p in range(4):
                split_lo(FFN_IN, 0, p)
            add_residual(1, OUT.piece(1, 15), x_again, 3)
            reciprocal_root(norm_h, 4, 4, D)
            diagonal(rstd, h_diag)
            split_lo(FFN_IN, 0, 4)
            split_lo(FFN_IN, 0, 5)
            turned_panel_lo(3)
            split_lo(FFN_IN, 0, 6)
            split_lo(FFN_IN, 0, 7)
            dve.wait_ge(spread_ready, 2)
            before_ffn, PANEL_STEPS = chain.base + chain.n, 3

            def hidden_panel(i, b, n, between):
                chain.body(n - 1, PANEL_STEPS, before_ffn)
                nc.vector.tensor_copy(conv_now[:, b, :, :, :],
                                      conv_T[:, :, :, bass.ds((n - 1) * 2, 2)]).then_inc(taps_on, 1)
                dve.wait_ge(piece_used, FFN_IN.piece(i, 8 * b + 7))
                by_token(tiles_of(2 * b, 4), 4, hidden_by_token)
                for part in range(2):
                    dve.wait_ge(first_tap, (n - 1) * 2 + (part + 1))
                    for back in (1, 2):
                        for t in range(2):
                            out = hidden[:, part, t, back:S]
                            last = nc.vector.scalar_tensor_tensor(
                                out=out, in0=bank[:, 2 * b + part, t * S:t * S + S - back],
                                scalar=conv_now[:, b, 2 - back, part, t:t + 1], in1=out, op0=ALU.mult, op1=ALU.add)
                        if back == 1:
                            chain.link(last)
                last.then_inc(pair_read[b], 1)
                between(0)
                dve.wait_ge(th_ready, n)
                chain.link(nc.vector.scalar_tensor_tensor(out=hidden[:, 0, :, :], in0=th[:, :, :], scalar=1.0,
                                                          in1=hidden[:, 0, :, :], op0=ALU.add, op1=ALU.mult))
                nc.vector.tensor_tensor(hidden[:, 0, :, :], hidden[:, 0, :, :], hidden[:, 1, :, :],
                                        ALU.mult).then_inc(act_ready, 1)
                between(1)
                dve.wait_ge(a_hi, n)
                tiles = bass.ds((n - 1) * 2, 2)
                nc.vector.scalar_tensor_tensor(out=aT_lo[:, tiles, :], in0=hidden[:, 0, :, :], scalar=0.5,
                                               in1=aT_hi[:, tiles, :].bitcast(F32), op0=ALU.mult,
                                               op1=ALU.subtract).then_inc(a_lo, 1)
                assert chain.n == PANEL_STEPS

            def ffn_in_body(i, first):
                if not first:
                    for p in range(4):
                        split_lo(FFN_IN, i, p)
                    hidden_panel(i - 1, 1, i * 2, lambda step: split_lo(FFN_IN, i, 4 + step))
                for p in range(8 if first else 6, 12):
                    split_lo(FFN_IN, i, p)
                hidden_panel(i, 0, i * 2 + 1, lambda step: split_lo(FFN_IN, i, 12 + step))
                split_lo(FFN_IN, i, 14)
                split_lo(FFN_IN, i, 15)

            ffn_in_body(0, True)
            with dve.Fori(1, FFN_IN.trips) as i:
                ffn_in_body(i, False)

            def gain_panel(panel, blocks=range(NB)):
                if len(blocks) == NB:
                    dve.wait_ge(pair_read[panel % 2], (READ_A, READ_B)[panel % 2][FFN_OUT] + panel // 2 + 1)
                else:
                    dve.wait_ge(last_added, blocks[0] + 1)
                cols = slice(panel * 512, panel * 512 + 512)
                for b in blocks:
                    last = nc.vector.tensor_tensor(y_out[:, b, cols], h[:, b, cols], gain_final[:, cols], ALU.mult)
                return last

            for i in range(FFN_OUT.trips):
                for p in range(4):
                    split_lo(FFN_OUT, i, p)
                if i == 0:
                    hidden_panel(FFN_IN.trips - 1, 1, 2 * FFN_IN.trips, lambda step: split_lo(FFN_OUT, 0, 4 + step))
                    chain.body(0, 0, before_ffn + 2 * FFN_IN.trips * PANEL_STEPS)
                else:
                    add_residual(1, FFN_OUT.piece(i - 1, 43), h, 2 * i - 1)
                    split_lo(FFN_OUT, i, 4)
                    split_lo(FFN_OUT, i, 5)
                    dve.wait_ge(gain_landed, 16)
                    gain_panel(0)
                for p in range(6, 44):
                    split_lo(FFN_OUT, i, p)
                    if i and p == 8:
                        gain_panel(1)
                    if p == 25:
                        add_residual(0, FFN_OUT.piece(i, 21), h, 2 * i)
                    if i and p == 27:
                        gain_panel(2)
            for b in range(NB):
                block = slice(b, b + 1)
                dve.wait_ge(last_product, b + 1)
                nc.vector.tensor_tensor(h[:, b, D - 512:D], bank[:, 2 + b, :], h[:, b, D - 512:D],
                                        ALU.add).then_inc(last_added, 1)
                gained = gain_panel(3, range(b, b + 1))
                chain.done(gained)
                reciprocal_root(norm_y, 4 + b, 4, D, ready=norm_y.scaled if b else None, blocks=block, n=b + 1)
                cols = slice(0, D // 2 if b else D)
                nc.vector.tensor_scalar(y_out[:, b, cols], y_out[:, b, cols], rstd[:, block], None,
                                        ALU.mult).then_inc(y_ready[b], 1)

        @block.tensor
        def _(pe):
            def mm(out, still, moving, start, stop):
                return nc.tensor.matmul(out, still, moving, start=start, stop=stop, skip_group_check=True)

            def product(out, still, moving, start, stop):
                mm(out, still[0], moving[0], start, False)
                mm(out, still[0], moving[1], False, False)
                return mm(out, still[1], moving[0], False, stop)

            def weights(phase, p, col, n):
                s = phase.split_slot(p)
                return w_hi[s][:, col:col + n], w_lo[s][:, col:col + n]

            def piece(phase, i, p, products):
                pe.wait_ge(lo_done, phase.piece(i, p))
                products().then_inc(piece_used, 1)

            def still_tiles(phase, p, k0, tiles, wide, outs, xk, k_last):
                def run():
                    for kk in range(2):
                        k = k0 + kk
                        for t in range(tiles):
                            last = product(outs(t), weights(phase, p, kk * wide + t * P, P), xk(k),
                                           k == 0 and t % 2 == 0, k == k_last)
                    return last
                return run

            def moving_tiles(phase, p, k0, wide, outs, xk, k_last):
                def run():
                    for kk in range(2):
                        k = k0 + kk
                        for b in range(NB):
                            hi, lo = xk(k)
                            last = product(outs(b), (hi[:, b * P:(b + 1) * P], lo[:, b * P:(b + 1) * P]),
                                           weights(phase, p, kk * wide, wide), k == 0, k == k_last)
                    return last
                return run

            def xk(k):
                return xT_hi[:, k, :], xT_lo[:, k, :]

            def turn(norm, source, target, tiles):
                for k in tiles:
                    if k >= 4:
                        pe.wait_ge(norm.lo, k - 3)
                    for b in range(NB):
                        last = nc.tensor.transpose(target(k)[:, b * P:(b + 1) * P], source[:, b, k * P:(k + 1) * P],
                                                   ident[:, :])
                    last.then_inc(norm.turned, 1)

            pe.wait_ge(tables_built, 1)
            pe.wait_ge(mix_landed, 16)
            nc.tensor.transpose(bank[:, 1, 0:KD], mix_rows[:, :], ident[0:KD, 0:KD]).then_inc(mix_turned, 1)

            def turn_x(tiles):
                pe.wait_ge(x_landed[tiles[0] // 4], 16)
                turn(norm_x, x_in, spread_bank, tiles)

            turn_x(range(4))
            for p in range(8):
                pe.wait_ge(norm_x.lo, 2 * p + 2)
                piece(LATENT, 0, p, moving_tiles(LATENT, p, 2 * p, RANK, lambda b: bank[:, 2 + b, :], xk, KD - 1))
                if 2 * p + 4 < KD:
                    turn_x(range(2 * p + 4, 2 * p + 6))
                if p == 4:
                    pe.wait_ge(mix_read, 1)
                    pe.wait_ge(taps_landed, 5 * 16)
                    for a in range(4):
                        nc.tensor.transpose(bank[:, 1, a * 2 * KF:(a + 1) * 2 * KF], conv_rows[:, a, :],
                                            ident[0:2 * KF, 0:2 * KF])
                    n_rows = KD + 2 * KR
                    nc.tensor.transpose(bank[:, 1, 8 * KF:8 * KF + n_rows], gain_rows[:, :],
                                        ident[0:n_rows, 0:n_rows]).then_inc(taps_turned, 1)

            def spread(diag, b, n):
                pe.wait_ge(diag_ready, n)
                for t in range(NB):
                    last = nc.tensor.matmul(bank[:, b, t * P:(t + 1) * P], ones[:, :], diag[:, t, :], start=True,
                                            stop=True)
                last.then_inc(wide_rstd, 1)

            for p in range(8, 10):
                def run():
                    for kk in range(8):
                        k = 8 * (p - 8) + kk
                        last = product(bank[0:MISC, 4, 0:S], weights(LATENT, p, kk * MISC, MISC), xk(k), k == 0,
                                       k == KD - 1)
                    return last
                piece(LATENT, 0, p, run)
            pe.wait_ge(tables_built, 5)
            spread(x_diag, 5, 1)
            pe.wait_ge(taps_read, 1)
            for p in range(10, 18):
                piece(LATENT, 0, p, moving_tiles(LATENT, p, 2 * (p - 10), RANK, lambda b: bank[:, b, :], xk, KD - 1))
                if p == 12:
                    pe.wait_ge(misc_copied, 1)
                    pe.wait_ge(spread_ready, 1)
                    for b in range(NB):
                        last = nc.tensor.transpose(bank[:, 5, b * MISC:(b + 1) * MISC], misc_T[:, b * P:(b + 1) * P],
                                                   ident[0:MISC, 0:MISC])
                    last.then_inc(misc_turned, 1)
                    pe.wait_ge(pair_read[1], 1)
                    turn(norm_cq, cq_n, latent_bank(6), range(KR))
                if p == 15:
                    pe.wait_ge(norm_cq.lo, KR)
                    pe.wait_ge(krot_ready, 1)
                    for b in range(NB):
                        last = nc.tensor.transpose(bank[:, 6, b * P:(b + 1) * P],
                                                   k_rot[:, b, :, :].rearrange("p t n -> p (t n)"), ident[:, :])
                    last.then_inc(kr_turned, 1)
                if p == 16:
                    pe.wait_ge(nlf_ready, 1)
                    nc.tensor.matmul(bank[:, 7, 0:H], upto[:, 0:P], nlf[:, 0, :], start=True, stop=True)
                    nc.tensor.matmul(bank[:, 7, H:2 * H], upto[:, P:S], nlf[:, 0, :], start=True, stop=False)
                    nc.tensor.matmul(bank[:, 7, H:2 * H], upto[:, 0:P], nlf[:, 1, :], start=False,
                                     stop=True).then_inc(cumq_done, 1)
            def project_fox(phase, i, p0, after=lambda p: None):
                for q in range(8):
                    piece(phase, i, p0 + q, still_tiles(phase, p0 + q, 2 * q, 3, 3 * HD,
                                                        lambda t: bank[:, 4 + t // 2, t % 2 * S:t % 2 * S + S], xk, KD - 1))
                    after(q)

            def latent(which):
                return lambda k: (cT_hi[:, which, k, :], cT_lo[:, which, k, :])

            def project_mla(phase, i, p0):
                for q in range(2):
                    def run():
                        for kk in range(2):
                            k = 2 * q + kk
                            product(bank[:, 6, 0:S], weights(phase, p0 + q, kk * 2 * HD, HD), latent(1)(k), k == 0,
                                    k == KR - 1)
                            last = product(bank[:, 7, 0:S], weights(phase, p0 + q, kk * 2 * HD + HD, HD), latent(1)(k),
                                           k == 0, k == KR - 1)
                        return last
                    piece(phase, i, p0 + q, run)
                for q in range(2):
                    def run():
                        for kk in range(2):
                            k = 2 * q + kk
                            last = product(bank[:, 6, S:2 * S], weights(phase, p0 + 2 + q, kk * HD, HD), latent(0)(k),
                                           False, k == KR - 1)
                        return last
                    piece(phase, i, p0 + 2 + q, run)

            def decay_of(head):
                pe.wait_ge(wide_ready, head + 1)
                if head >= 2:
                    pe.wait_ge(decay_read, head - 1)
                else:
                    pe.wait_ge((kr_ready, cumq_read)[head], 1)
                out = bank[:, 6 + head % 2, 0:S]
                wide = nlf_wide[:, head % 2]
                nc.tensor.matmul(out, wide[:, 0, :], upto[:, :], start=True, stop=False)
                nc.tensor.matmul(out[:, P:S], wide[:, 1, :], upto[:, 0:P], start=False,
                                 stop=True).then_inc(decay_done, 1)
                if head == 5:
                    pe.wait_ge(pair_read[0], 1)
                    turn(norm_ckv, ckv_n, latent_bank(0), range(KR))

            for p in range(2):
                piece(PROJ0, 0, p, moving_tiles(PROJ0, p, 2 * p, H * ROPE, lambda b: bank[:, 2 + b, :], latent(0), KR - 1))
            pe.wait_ge(misc_read, 1)
            decay_of(0)
            project_fox(PROJ0, 0, 2, lambda q: decay_of(q + 1) if q + 1 < H else None)
            pe.wait_ge(q_products, NB)
            pe.wait_ge(norm_ckv.lo, KR)
            pe.wait_ge(decay_read, H)
            project_mla(PROJ0, 0, 10)

            def scores(branch, n, qk_hi, qk_lo, rotary, q_at=0):
                for b in range(NB):
                    out = bank[:, 4 + 2 * branch, b * P:b * P + (b + 1) * P]
                    qs, ks = slice(b * P, (b + 1) * P), slice(0, (b + 1) * P)
                    last = product(out, (qk_hi[:, q_at, qs], qk_lo[:, q_at, qs]),
                                   (qk_hi[:, 1 - q_at, ks], qk_lo[:, 1 - q_at, ks]), True, not rotary)
                    if rotary:
                        mm(out, qr_parts[:, qs], kr_hi[:, ks], False, False)
                        last = mm(out, qr_parts[0:ROPE, qs], kr_lo[:, ks], False, True)
                last.then_inc(scores_done[branch], 1)

            def turn_probabilities(branch, n):
                pe.wait_ge(normed[branch], n)
                for blk in range(3):
                    last = nc.tensor.transpose(bank[:, 5 + 2 * branch, blk * P:(blk + 1) * P],
                                               prob[branch][:, blk * P:(blk + 1) * P], ident[:, :])
                last.then_inc(p_turned[branch], 1)

            def outputs(branch, n, v_hi, v_lo):
                pe.wait_ge(p_lo[branch], n)
                out = bank[:, 6 + branch, 0:S]
                product(out, (v_hi[:, 0, :], v_lo[:, 0, :]), (pT_hi[branch][:, 0:S], pT_lo[branch][:, 0:S]), True, False)
                product(out[:, P:S], (v_hi[:, 1, :], v_lo[:, 1, :]),
                        (pT_hi[branch][:, S:SCORES], pT_lo[branch][:, S:SCORES]), False, True).then_inc(o_done[branch], 1)

            def one_head(phase, i, n, first):
                pe.wait_ge(pair_read[1], n)
                for p in range(8):
                    piece(phase, i, first + p, still_tiles(phase, first + p, 2 * p, 4, 4 * P,
                                                   lambda t: bank[:, 2 + t // 2, t % 2 * S:t % 2 * S + S], xk, KD - 1))
                    if p == 1:
                        pe.wait_ge(qrot_ready, n)
                        pe.wait_ge(mla_hi, n)
                        pe.wait_ge(fox_lo, n)
                        scores(0, n, fqk_hi, fqk_lo, False)
                        for b in range(NB):
                            cols = slice(b * P, (b + 1) * P)
                            nc.tensor.transpose(bank[:, 5, cols], vT[0][:, cols], ident[:, :])
                            nc.tensor.transpose(bank[:, 7, cols], vT[1][:, cols], ident[:, :])
                            last = nc.tensor.transpose(bank[:, 5, S + b * P:S + (b + 1) * P],
                                                       q_rot[:, b, :, :].rearrange("p t n -> p (t n)"), ident[:, :])
                        last.then_inc(v_turned, 1)
                    if p == 3:
                        pe.wait_ge(mla_lo, n)
                        pe.wait_ge(bank5_lo, n)
                        scores(1, n, mqk_hi, mqk_lo, True, q_at=1)
                    if p == 5:
                        pe.wait_ge(bank7_lo, n)
                        turn_probabilities(0, n)
                    if p == 6:
                        turn_probabilities(1, n)
                outputs(0, n, fv_hi, fv_lo)
                outputs(1, n, mv_hi, mv_lo)
                if phase is not LAST:
                    project_fox(phase, i, first + 8)
                    pe.wait_ge(o_read[0], n)
                    pe.wait_ge(o_read[1], n)
                    project_mla(phase, i, first + 16)

            with pe.Fori(0, HEADS.trips) as i:
                for half in range(2):
                    one_head(HEADS, i, i * 2 + (half + 1), half * HEAD_PIECES)
            one_head(SEVENTH, 0, H - 1, 0)
            one_head(LAST, 0, H, 0)

            def bank_of(pair):
                return lambda t: bank[:, 2 * pair + t // 2, t % 2 * S:t % 2 * S + S]

            with pe.Fori(0, MERGE.trips) as i:
                for p in range(8):
                    pair, q = p // 4, p % 4
                    if q == 0:
                        pe.wait_ge(pair_read[pair], i + (READ_A, READ_B)[pair][MERGE])
                    pe.wait_ge(o_split, GROUPS_READ[p])
                    piece(MERGE, i, p, still_tiles(
                        MERGE, p, 2 * q, 4, 4 * P, bank_of(pair),
                        lambda k: tuple(part[:, k, :] for part in oT_split[1 - pair]), H - 1))

            def moving_panels(phase, i, per_panel, activation, ready, k_last, after=lambda i, p: None, pieces=None):
                for p in range(pieces or 2 * per_panel):
                    pair, q = p // per_panel, p % per_panel
                    if q == 0:
                        pe.wait_ge(pair_read[pair], i + (READ_A, READ_B)[pair][phase])
                    pe.wait_ge(*ready(q))
                    piece(phase, i, p, moving_tiles(phase, p, 2 * q, 512, lambda b: bank[:, 2 * pair + b, :],
                                                    activation, k_last))
                    after(i, p)

            def turn_residual(n):
                pe.wait_ge(pair_read[n % 2], (READ_A, READ_B)[n % 2][OUT] + n // 2 + 1)
                if n >= 2:
                    pe.wait_ge(norm_h.lo, n - 1)
                for t in range(4):
                    k = 4 * n + t
                    for b in range(NB):
                        last = nc.tensor.transpose(panel_bank(n, t)[:, b * P:(b + 1) * P], h[:, b, k * P:(k + 1) * P],
                                                   ident[:, :])
                last.then_inc(norm_h.turned, 1)

            def residual_beside(i, p):
                if i and p == 1:
                    turn_residual(1)
                if p == 10:
                    turn_residual(2 * i)

            for i in range(OUT.trips):
                moving_panels(OUT, i, 8, lambda k: (mT_hi[:, k, :], mT_lo[:, k, :]), lambda q: (m_lo, q // 2 + 1),
                              KD - 1, residual_beside)

            def ffn_in_body(i, first):
                for p in range(16):
                    pair, q = p // 8, p % 8
                    if q == 0:
                        pe.wait_ge(pair_read[pair], i + (READ_A, READ_B)[pair][FFN_IN])
                    if first:
                        pe.wait_ge(norm_h.lo, q // 2 + 1)
                    piece(FFN_IN, i, p, still_tiles(FFN_IN, p, 2 * q, 4, 4 * P, bank_of(pair), xk, KD - 1))
                    if first and p == 1:
                        turn_residual(3)
                    if first and p == 2:
                        pe.wait_ge(norm_h.lo, 3)
                        spread(h_diag, 4, 2)

            ffn_in_body(0, True)
            with pe.Fori(1, FFN_IN.trips) as i:
                ffn_in_body(i, False)

            def hidden_tile(k):
                return aT_hi[:, k, :], aT_lo[:, k, :]

            for i in range(FFN_OUT.trips):
                moving_panels(FFN_OUT, i, 22, hidden_tile, lambda q: (a_lo, q + 1), KF - 1,
                              pieces=2 * 22 - SPLIT_SLOTS * (i == FFN_OUT.trips - 1))
            for b in range(NB):
                tokens = slice(b * P, (b + 1) * P)
                for k in range(KF - 2 * SPLIT_SLOTS, KF):
                    p, kk = 22 + k // 2, k % 2
                    if b == 0 and kk == 0:
                        pe.wait_ge(lo_done, FFN_OUT.piece(FFN_OUT.trips - 1, p))
                    last = product(bank[:, 2 + b, :], [part[:, tokens] for part in hidden_tile(k)],
                                   weights(FFN_OUT, p, kk * 512, 512), False, k == KF - 1)
                last.then_inc(last_product, 1)


NAMES = ["x", "positions", "norm_mix", "w_in", "b_forget", "norm_q_a", "w_uq", "norm_kv_a", "w_ukv", "w_proj_mla",
         "w_proj_fox", "w_out", "norm_ffn", "w_ffn_in", "w_conv", "b_conv", "w_ffn_out", "norm_final"]


def kernel(**inputs):
    import concourse.bacc as bacc
    from concourse.bass_utils import run_bass_kernel_spmd

    nc = bacc.Bacc("TRN2", target_bir_lowering=False, num_devices=1)
    arrays, args = {}, []
    for name in NAMES:
        a = np.ascontiguousarray(inputs[name])
        arrays[name] = a
        args.append(nc.dram_tensor(name, a.shape, mybir.dt.from_np(a.dtype), kind="ExternalInput").ap())
    y = nc.dram_tensor("y", (1, S, D), mybir.dt.float32, kind="ExternalOutput").ap()
    hybrid_layer(nc, *args, y)
    result = run_bass_kernel_spmd(nc, [arrays], core_ids=[0])
    return result.results[0]["y"]
```
